# Optimizing a Trainium2 kernel written in Bass

```python
import math
import jax, jax.numpy as jnp
from jax import lax
import numpy as np

D_MODEL = 1024
BATCH = 1
SEQ = 512
DEPTH = 1
DEC_BATCH = 1
DEC_SEQ = 32
PAST_LEN = 1024

CHUNK = 64
Q_BLOCK = 128
ML_CHUNK = CHUNK
ML_HEADS = 4
ML_DK = 128
ML_DV = 128
SC_W = 512
CONV_W = 3
DA_HEADS = 4
DA_DQK = 64
DA_DV = 2 * DA_DQK
BR_W = 512
N_BRANCH = 3
D_FF = 2816
EPS = 1e-6
SPLIT_SIZES = (ML_HEADS * ML_DK, ML_HEADS * ML_DK, ML_HEADS * ML_DV, ML_HEADS * ML_DV, ML_HEADS, ML_HEADS,
               SC_W, SC_W, SC_W,
               DA_HEADS * 2 * DA_DQK, DA_HEADS * 2 * DA_DQK, DA_HEADS * DA_DV,
               N_BRANCH * D_MODEL)
IN_WIDTH = sum(SPLIT_SIZES)

kernel_name = "hybrid_mlstm_shortconv_diffattn_stream_step"

def rmsnorm(x, g):
    xf = x.astype(jnp.float32)
    y = xf * lax.rsqrt(jnp.mean(xf * xf, axis=-1, keepdims=True) + EPS)
    return (y * g.astype(jnp.float32)).astype(x.dtype)

def causal_dwconv(x, hist, w):
    T = x.shape[1]
    xp = jnp.concatenate([hist.astype(x.dtype), x], axis=1)
    y = sum(w[j] * xp[:, j:j + T] for j in range(CONV_W))
    return y, xp[:, -(CONV_W - 1):]

def mlstm_chunk(carry, inp):
    C, n, m = carry
    q, k, v, ig, lf = inp
    L = q.shape[1]
    b = jnp.cumsum(lf, axis=1).transpose(0, 2, 1)
    igh = ig.transpose(0, 2, 1)
    causal = jnp.tril(jnp.ones((L, L), dtype=bool))
    dlog = jnp.where(causal, b[..., :, None] - b[..., None, :] + igh[..., None, :], -jnp.inf)
    a = b + m[..., None]
    mt = jnp.maximum(a, jnp.max(dlog, axis=-1))
    w = jnp.exp(dlog - mt[..., None])
    inter = jnp.exp(a - mt)
    s = jnp.einsum('blhd,bshd->bhls', q, k) * w
    num = (jnp.einsum('bhls,bshe->blhe', s, v)
           + inter.transpose(0, 2, 1)[..., None] * jnp.einsum('blhd,bhde->blhe', q, C))
    den = jnp.sum(s, axis=-1) + inter * jnp.einsum('blhd,bhd->bhl', q, n)
    den = jnp.maximum(jnp.abs(den), jnp.exp(-mt))
    h = num / den.transpose(0, 2, 1)[..., None]
    wl = w[..., -1, :]
    il = inter[..., -1]
    C_new = il[..., None, None] * C + jnp.einsum('bhs,bshd,bshe->bhde', wl, k, v)
    n_new = il[..., None] * n + jnp.einsum('bhs,bshd->bhd', wl, k)
    return (C_new, n_new, mt[..., -1]), h

def mlstm_prompt(q, k, v, ig, lf):
    Bsz, S = q.shape[:2]
    nc = S // ML_CHUNK

    def to_chunks(t):
        return jnp.moveaxis(t.reshape((Bsz, nc, ML_CHUNK) + t.shape[2:]), 1, 0)

    init = (jnp.zeros((Bsz, ML_HEADS, ML_DK, ML_DV), jnp.float32),
            jnp.zeros((Bsz, ML_HEADS, ML_DK), jnp.float32),
            jnp.zeros((Bsz, ML_HEADS), jnp.float32))
    state, h = lax.scan(mlstm_chunk, init, (to_chunks(q), to_chunks(k), to_chunks(v), to_chunks(ig), to_chunks(lf)))
    return state, jnp.moveaxis(h, 0, 1).reshape(Bsz, S, ML_HEADS, ML_DV)

def diff_attend(q, k, v, lam, mask):
    s = jnp.einsum('bqhcd,bkhcd->bhcqk', q, k).astype(jnp.float32)
    if mask is not None:
        s = jnp.where(mask, s, -jnp.inf)
    p = jax.nn.softmax(s, axis=-1)
    wdiff = p[:, :, 0] - lam * p[:, :, 1]
    return jnp.einsum('bhqk,bkhe->bqhe', wdiff.astype(v.dtype), v)

def diff_attn_prompt(q, k, v, lam):
    Bsz, S = q.shape[:2]
    nb = S // Q_BLOCK
    qb = jnp.moveaxis(q.reshape((Bsz, nb, Q_BLOCK) + q.shape[2:]), 1, 0)
    qpos = jnp.arange(S).reshape(nb, Q_BLOCK)
    kchunk = jnp.arange(S) // CHUNK

    def one(args):
        qblk, pos = args
        mask = kchunk[None, :] <= (pos // CHUNK)[:, None]
        return diff_attend(qblk, k, v, lam, mask)

    o = lax.map(one, (qb, qpos))
    return jnp.moveaxis(o, 0, 1).reshape(Bsz, S, DA_HEADS, DA_DV)

def layer(x, l, w, past):
    (g1, w_in, b_if, ml_g, sc_w, lam_p, da_g, w_br, w_o, g2, w_up, f_w, w_dn) = w
    Bsz, T, _ = x.shape
    f32 = jnp.float32
    h = rmsnorm(x, g1)
    z = h @ w_in
    splits = tuple(int(i) for i in np.cumsum(SPLIT_SIZES)[:-1])
    (mq, mk, mv, mo, mi, mf, sb, sc, sx, dq, dk, dv, gt) = jnp.split(z, splits, axis=-1)

    q = mq.reshape(Bsz, T, ML_HEADS, ML_DK).astype(f32)
    k = mk.reshape(Bsz, T, ML_HEADS, ML_DK).astype(f32) * (ML_DK ** -0.5)
    v = mv.reshape(Bsz, T, ML_HEADS, ML_DV).astype(f32)
    ig = mi.astype(f32) + b_if[0].astype(f32)
    lf = jax.nn.log_sigmoid(mf.astype(f32) + b_if[1].astype(f32))
    if past is None:
        (C, n, m), hm = mlstm_prompt(q, k, v, ig, lf)
    else:
        carry = (past[2].astype(f32), past[3].astype(f32), past[4].astype(f32))
        (C, n, m), hm = mlstm_chunk(carry, (q, k, v, ig, lf))
    hm = rmsnorm(hm, ml_g).astype(x.dtype).reshape(Bsz, T, ML_HEADS * ML_DV)
    ya = jax.nn.sigmoid(mo) * hm

    hist = jnp.zeros((Bsz, CONV_W - 1, SC_W), x.dtype) if past is None else past[5]
    cu, conv_state = causal_dwconv(sc * sx, hist, sc_w)
    yb = sb * cu

    lam_init = 0.8 - 0.6 * math.exp(-0.3 * l)
    lp = lam_p.astype(f32)
    lam = jnp.exp(jnp.sum(lp[0] * lp[1])) - jnp.exp(jnp.sum(lp[2] * lp[3])) + lam_init
    q5 = dq.reshape(Bsz, T, DA_HEADS, 2, DA_DQK) * (DA_DQK ** -0.5)
    kk = dk.reshape(Bsz, T, DA_HEADS, 2 * DA_DQK)
    vv = dv.reshape(Bsz, T, DA_HEADS, DA_DV)
    if past is None:
        o = diff_attn_prompt(q5, kk.reshape(Bsz, T, DA_HEADS, 2, DA_DQK), vv, lam)
    else:
        keys = jnp.concatenate([past[0].astype(x.dtype), kk], axis=1)
        vals = jnp.concatenate([past[1].astype(x.dtype), vv], axis=1)
        keys = keys.reshape(Bsz, keys.shape[1], DA_HEADS, 2, DA_DQK)
        o = diff_attend(q5, keys, vals, lam, None)
    o = rmsnorm(o, da_g) * (1.0 - lam_init)
    yc = o.reshape(Bsz, T, DA_HEADS * DA_DV)

    br = jnp.stack([ya, yb, yc], axis=2)
    proj = jnp.einsum('btnc,ncd->btnd', br, w_br)
    gates = jax.nn.sigmoid(gt.reshape(Bsz, T, N_BRANCH, D_MODEL))
    x = x + jnp.einsum('btnd,btnd->btd', gates, proj) @ w_o

    h2 = rmsnorm(x, g2)
    up = h2 @ w_up
    fhist = jnp.zeros((Bsz, CONV_W - 1, 2 * D_FF), x.dtype) if past is None else past[6]
    upc, ffn_state = causal_dwconv(up, fhist, f_w)
    x = x + (jax.nn.silu(upc[..., :D_FF]) * upc[..., D_FF:]) @ w_dn
    new_state = (kk, vv, C.astype(x.dtype), n.astype(x.dtype), m.astype(x.dtype),
                 conv_state, ffn_state.astype(x.dtype))
    return x, new_state

def setup_inputs(seed: int = 0) -> dict:
    key = jax.random.key(seed)
    ks = jax.random.split(key, 24)
    nrm = jax.random.normal
    f = jnp.float32
    return {
        "x_prompt": nrm(ks[0], (BATCH, SEQ, D_MODEL), f),
        "x_sample": nrm(ks[1], (DEC_BATCH, DEC_SEQ, D_MODEL), f),
        "cache_k": nrm(ks[2], (DEPTH, DEC_BATCH, PAST_LEN, DA_HEADS, 2 * DA_DQK), f),
        "cache_v": nrm(ks[3], (DEPTH, DEC_BATCH, PAST_LEN, DA_HEADS, DA_DV), f),
        "state_C": 0.1 * nrm(ks[4], (DEPTH, DEC_BATCH, ML_HEADS, ML_DK, ML_DV), f),
        "state_n": 0.1 * nrm(ks[5], (DEPTH, DEC_BATCH, ML_HEADS, ML_DK), f),
        "state_m": 0.5 * nrm(ks[6], (DEPTH, DEC_BATCH, ML_HEADS), f),
        "state_conv": nrm(ks[7], (DEPTH, DEC_BATCH, CONV_W - 1, SC_W), f),
        "state_ffn": nrm(ks[8], (DEPTH, DEC_BATCH, CONV_W - 1, 2 * D_FF), f),
        "norm1": 1.0 + 0.02 * nrm(ks[9], (DEPTH, D_MODEL), f),
        "w_in": nrm(ks[10], (DEPTH, D_MODEL, IN_WIDTH), f) * D_MODEL ** -0.5,
        "b_if": jnp.stack([0.1 * nrm(ks[11], (DEPTH, ML_HEADS), f),
                           3.0 + 0.1 * nrm(ks[12], (DEPTH, ML_HEADS), f)], axis=1),
        "ml_norm": 1.0 + 0.02 * nrm(ks[13], (DEPTH, ML_HEADS, ML_DV), f),
        "w_sc_conv": nrm(ks[14], (DEPTH, CONV_W, SC_W), f) * CONV_W ** -0.5,
        "da_lambda": 0.1 * nrm(ks[15], (DEPTH, 4, DA_DQK), f),
        "da_norm": 1.0 + 0.02 * nrm(ks[16], (DEPTH, DA_DV), f),
        "w_branch": nrm(ks[17], (DEPTH, N_BRANCH, BR_W, D_MODEL), f) * BR_W ** -0.5,
        "w_out": nrm(ks[18], (DEPTH, D_MODEL, D_MODEL), f) * D_MODEL ** -0.5,
        "norm2": 1.0 + 0.02 * nrm(ks[19], (DEPTH, D_MODEL), f),
        "w_up": nrm(ks[20], (DEPTH, D_MODEL, 2 * D_FF), f) * D_MODEL ** -0.5,
        "w_fconv": nrm(ks[21], (DEPTH, CONV_W, 2 * D_FF), f) * CONV_W ** -0.5,
        "w_down": nrm(ks[22], (DEPTH, D_FF, D_MODEL), f) * D_FF ** -0.5,
        "norm_f": 1.0 + 0.02 * nrm(ks[23], (D_MODEL,), f),
    }

def reference(x_prompt, x_sample, cache_k, cache_v, state_C, state_n, state_m, state_conv, state_ffn,
              norm1, w_in, b_if, ml_norm, w_sc_conv, da_lambda, da_norm, w_branch, w_out,
              norm2, w_up, w_fconv, w_down, norm_f):
    xp = x_prompt
    xs = x_sample
    prompt_states = []
    sample_states = []
    for l in range(DEPTH):
        w = (norm1[l], w_in[l], b_if[l], ml_norm[l], w_sc_conv[l], da_lambda[l], da_norm[l],
             w_branch[l], w_out[l], norm2[l], w_up[l], w_fconv[l], w_down[l])
        xp, st_p = layer(xp, l, w, None)
        past = (cache_k[l], cache_v[l], state_C[l], state_n[l], state_m[l], state_conv[l], state_ffn[l])
        xs, st_s = layer(xs, l, w, past)
        prompt_states.append(st_p)
        sample_states.append(st_s)
    y_prompt = rmsnorm(xp, norm_f)
    y_sample = rmsnorm(xs, norm_f)
    p_k, p_v, p_C, p_n, p_m, p_conv, p_ffn = [jnp.stack(t) for t in zip(*prompt_states)]
    s_k, s_v, s_C, s_n, s_m, s_conv, s_ffn = [jnp.stack(t) for t in zip(*sample_states)]
    return (y_prompt, y_sample, p_k, p_v, p_C, p_n, p_m, p_conv, p_ffn,
            s_k, s_v, s_C, s_n, s_m, s_conv, s_ffn)


_drawn_inputs = setup_inputs


def setup_inputs(seed=0):
    import zlib

    import numpy as np

    out = dict(_drawn_inputs(seed))
    spreads = {}
    factors = {'state_n': 3.988,
     'state_m': 3.271,
     'ml_norm': 8.0,
     'da_norm': 7.165,
     'norm2': 2.753,
     'norm_f': 2.909}
    for name, (base, spread) in spreads.items():
        noise = np.random.default_rng([zlib.crc32(name.encode()), seed]).standard_normal(out[name].shape)
        drawn = base * np.exp(spread * noise) if base else spread * noise
        out[name] = __import__('jax').numpy.asarray(drawn.astype(out[name].dtype))
    for name, factor in factors.items():
        out[name] = (out[name] * factor).astype(out[name].dtype)
    return out
```

```python
import concourse.bass as bass
from concourse import mybir
from contextlib import ExitStack

F32 = mybir.dt.float32
ALU = mybir.AluOpType
ACT = mybir.ActivationFunctionType
AX = mybir.AxisListType

P = 128
DM = 1024
KD = DM // P
TP, TS, PAST = 512, 32, 1024
S0 = TP + 2
T = S0 + TS
HALF = T // 2
TILES = [(0, P), (P, P), (2 * P, P), (3 * P, P), (S0, TS)]
H = 4
BW = 512
DFF = 2816
JF = DFF // P
JU = 2 * JF
EPS = 1e-6
LAM_INIT = 0.2
NEG = -1e30
NSLOT = 3
SLOT = 4096
W_IN_AT = dict(mq=0, mk=512, mv=1024, mo=1536, sb=2056, sc=2568, sx=3080, dq=3592, dk=4104, dv=4616,
               gt0a=5128, gt0b=5640, gt1a=6152, gt1b=6664, gt2a=7176, gt2b=7688)
IG_AT, FG_AT = 2048, 2052


def streaming_encoder_step(nc, x_prompt, x_sample, cache_k, cache_v, state_C, state_n, state_m, state_conv,
                           state_ffn, norm1, w_in, b_if, ml_norm, w_sc_conv, da_lambda, da_norm, w_branch,
                           w_out, norm2, w_up, w_fconv, w_down, norm_f,
                           y_p, y_s, p_k, p_v, p_C, p_n, p_m, p_conv, p_ffn,
                           s_k, s_v, s_C, s_n, s_m, s_conv, s_ffn):
    ORDER, block_of = [], {}

    def add(kind, *a):
        block_of[(kind, *a)] = len(block_of)
        ORDER.append((kind, a, block_of[(kind, *a)]))

    def unit(kind, *a):
        ORDER.append((kind, a, None))

    add("small")
    for j in range(KD):
        add("xT", j)
    add("norm", 0)
    add("if")
    for name, j in [("mk", 0), ("mk", 1), ("tok", ("mk", 0)), ("mk", 2), ("tok", ("mk", 1)), ("mk", 3),
                    ("tok", ("mk", 2)), ("mq", 0), ("tok", ("mk", 3)), ("mq", 1), ("mq", 2), ("mq", 3),
                    ("mv", 0), ("mv", 1), ("tok", ("mv", 0)), ("mv", 2), ("tok", ("mv", 1)), ("mv", 3),
                    ("tok", ("mv", 2)), ("gtr", 0), ("dk", 0), ("tok", ("mv", 3))]:
        add(name, j)
    ml_fill = [[("dk", 1)], [("tok", ("dk", 0)), ("dk", 2)], [("tok", ("dk", 1)), ("dk", 3)],
               [("tok", ("dk", 2)), ("dv", 0)], [("tok", ("dk", 3)), ("dv", 1)], [("tok", ("dv", 0)), ("dv", 2)],
               [("tok", ("dv", 1)), ("dv", 3)], [("tok", ("dv", 2)), ("dq", 0)], [("tok", ("dv", 3)), ("dq", 1)],
               [("dq", 2)]]
    for c in range(5):
        for stage in range(3):
            unit("ml", stage, c)
            if stage < 2:
                for s in ml_fill.pop(0):
                    add(*s)
    add("dq", 3)
    unit("ck", 0)
    add("mo", 0)
    unit("ck", 1)
    add("mo", 1)
    unit("sample", 0)
    add("mo", 2)
    unit("sample", 1)
    add("mo", 3)
    unit("at", 1, 0)
    add("sc", 0)
    unit("at", 2, 0)
    add("sc", 1)
    unit("at", 3, 0)
    fill = [("sc", 2), ("sc", 3)] + [(s, j) for s in ("sx", "sb") for j in range(4)]
    fill += [(s, b, j) for b in (1, 0) for j in range(KD) for s in ("gt", "pr")]
    fill += [("gt", 2, j) for j in range(KD)]
    for k in range(1, 20):
        for stage in (3, 0, 1, 2):
            if 1 <= k - stage <= 16:
                unit("at", stage, k - stage)
        add(*fill.pop(0))
        if k > 10:
            add(*fill.pop(0))
    for f in fill:
        add(*f)
    for j in range(KD):
        add("pr", 2, j)
    for j in range(KD):
        add("wo", j)
    add("norm", 1)
    for j in range(JF):
        add("up", j, 0)
        add("up", j, 1)
    add("state")
    for j in range(KD):
        add("dn", j)
    add("norm", 2)
    for j in range(KD):
        add("yT", j)

    BY_DVE = {"small", "xT", "tok", "gtr", "sx", "sb", "pr", "wo", "dn", "state"}
    drained, count = {}, {"act": 0, "dve": 0}
    for kind, a, n in ORDER:
        if n is not None:
            e = "dve" if kind in BY_DVE else "act"
            count[e] += 1
            drained[n] = (e, count[e])

    ITEMS = ["x", "mk", "mq", "mv", "dk", "dv", "dq", "ck", "mo", "cv", "sc", "sx", "sb",
             "gt1a", "br1", "gt1b", "gt0a", "br0", "gt0b", "gt2a", "gt2b", "br2", "woa", "wob"]
    ITEMS += [f"up{i}" for i in range(JF // 2)] + [f"dn{j}" for j in range(KD)]

    def item_of(kind, a):
        if kind in ("mk", "mq", "mv", "dk", "dv", "dq", "mo", "sc", "sx", "sb"):
            return kind
        if kind == "xT":
            return "x"
        if kind == "gt":
            return f"gt{a[0]}" + "ab"[a[1] // 4]
        if kind == "pr":
            return f"br{a[0]}"
        if kind == "wo":
            return "wo" + "ab"[a[0] // 4]
        if kind == "up":
            return f"up{a[0] // 2}"
        if kind == "dn":
            return f"dn{a[0]}"
        return None

    last_block = {}
    for kind, a, n in ORDER:
        if n is not None and item_of(kind, a):
            last_block[item_of(kind, a)] = n

    tmp_index, tmp_users = {}, []

    def tmp_user(key, sem_name, value):
        tmp_index[key] = len(tmp_users)
        tmp_users.append((sem_name, value))

    for j in range(KD):
        tmp_user(("sq", 0, j), "sq_added", j + 1)
    for j in range(4):
        tmp_user(("mo", j), "ya_ready", j + 1)
    for j in range(KD):
        tmp_user(("gt", 1, j), "dve_drained", drained[block_of[("pr", 1, j)]][1])
    for j in range(KD):
        tmp_user(("gt", 0, j), "merged_added", j + 1)
    for j in range(KD):
        tmp_user(("sq", 1, j), "sq_added", KD + j + 1)
    for j in range(JF):
        tmp_user(("up", j), "g_ready", j + 1)
    for j in range(KD):
        tmp_user(("sq", 2, j), "sq_added", 2 * KD + j + 1)

    ctx = ExitStack()
    with ctx:
        def sb(name, shape):
            return ctx.enter_context(nc.sbuf_tensor(name, shape, F32))

        def sem(name):
            return ctx.enter_context(nc.semaphore(name))

        D = ctx.enter_context(nc.psum_tensor("D", [P, 4, 512], F32))
        X = ctx.enter_context(nc.psum_tensor("X", [P, 4, 512], F32))
        ring = sb("ring", [P, NSLOT, SLOT])
        xT = sb("xT", [P, KD, T])
        hT = sb("hT", [P, KD, T])
        tmp = sb("tmp", [P, 2, T])
        ident = sb("ident", [P, P])
        mean_w = sb("mean_w", [P, P])
        causal = sb("causal", [P, P])
        vec = sb("vec", [P, 49])
        hist = sb("hist", [P, 2, JU])
        fcw = sb("fcw", [P, 3, JU])
        ffn_last = sb("ffn_last", [P, 2, 2, JU])
        conv_last = sb("conv_last", [P, 2, 2, 4])
        wif = sb("wif", [P, KD, 36])
        half_row = sb("half_row", [1, P])
        neg_row = sb("neg_row", [1, 64])
        b_i, b_f, m_s = sb("b_i", [H, 1]), sb("b_f", [H, 1]), sb("m_s", [H, 1])
        neg_lam = sb("neg_lam", [P, 1])
        lam_e = sb("lam_e", [P, 2])
        m_half = sb("m_half", [P, 1])
        il = sb("il", [P, H])
        gT = sb("gT", [P, 5, H])
        emT = sb("emT", [P, 5, H])
        den, rden, ssq, rr = sb("den", [P, H]), sb("rden", [P, H]), sb("ssq", [P, H]), sb("rr", [P, H])
        nmax = sb("nmax", [P, 2, 2])
        psum_p = sb("psum_p", [P, 2, 2])
        rsum = sb("rsum", [P, 4, 2])
        kap = sb("kap", [P, 1])
        assq, arr = sb("assq", [P, 2]), sb("arr", [P, 2])

        ARENA = 28800
        arena = sb("arena", [P, ARENA])

        def region(at, *shape, parts=P):
            size = 1
            for s in shape:
                size *= s
            assert at + size <= ARENA
            v = arena[0:parts, at:at + size]
            if len(shape) == 2:
                v = v.rearrange("p (a b) -> p a b", a=shape[0])
            elif len(shape) == 3:
                v = v.rearrange("p (a b c) -> p a b c", a=shape[0], b=shape[1])
            return v

        M_AT = 0
        G_AT = M_AT + KD * T
        K_AT = G_AT + KD * T
        Q_AT = K_AT + 7360
        DQ_AT = Q_AT + 4 * T
        DK_AT = DQ_AT + 4 * T
        DV_AT = DK_AT + 4 * T
        WORK_AT = DV_AT + 5 * 512
        small_a = region(M_AT, P)
        small_b = region(M_AT + P, P)
        small_c = region(M_AT + 2 * P, 2, P)
        lam_t = region(M_AT + 4 * P, 2, 2, 64)
        lam_p = region(M_AT + 6 * P, 2, 64)
        x_s = region(G_AT, DM)
        ssum = region(WORK_AT, T)
        rstd = region(WORK_AT + T, T)
        f_tmp = region(M_AT, 2, T)
        k_out = region(M_AT + 2 * T, 5, 512)
        sel = region(M_AT + 2 * T + 2560, H, P)
        names = ("lf", "ig", "cum", "m", "u", "g", "inter", "em")
        row = {nm: region(G_AT + i * T, T)[0:H, :] for i, nm in enumerate(names)}
        mkT = region(K_AT, 4, T)
        mk_tok = region(K_AT + 4 * T, 5, H, P)
        mv_tok = region(K_AT + 4 * T + 2560, 5, H, P + 1)
        mqT = region(Q_AT, 4, T)
        dqT = region(DQ_AT, 4, T)
        dkT = region(DK_AT, 4, T)
        dv_tok = region(DV_AT, 5, H, P)
        w_ml = region(WORK_AT, H, P)
        p_ml = region(WORK_AT + 512, H, P)
        kw = region(WORK_AT + 1024, H, P)
        qi = region(WORK_AT + 1536, H, P)
        hn = region(WORK_AT + 2048, H, P)
        C_p = region(WORK_AT + 2560, H, P + 1)
        C_s = region(WORK_AT + 2560 + 516, H, P + 1)
        ckT = region(K_AT, H, PAST)
        prob = region(K_AT + H * PAST, 2, 1056)
        prob2 = region(K_AT + H * PAST, 2, 2, 512)
        wdT = region(K_AT + H * PAST + 2112, 9, P)
        u_c = region(G_AT, 4, T + 2)
        scb = region(WORK_AT, 4, T)
        on = region(WORK_AT + 4 * T, 2, P)
        cst = region(WORK_AT + 4 * T + 2 * P, P)[0:16, :]
        junk = region(WORK_AT + 4 * T + 3 * P, P)
        merged = region(M_AT, KD, T)
        gate2 = region(G_AT, KD, T)
        gff = region(0, JF, T)
        FF_AT = JF * T
        ups = region(FF_AT, 2, 2, T + 2)
        acc = region(FF_AT + 4 * (T + 2), 2, 2, T)
        Y_AT = FF_AT + 4 * (T + 2) + 4 * T
        fst = region(Y_AT, 2, P)
        yst = region(Y_AT + 2 * P, 4, DM)
        yst_s = region(Y_AT + 2 * P + 4 * DM, DM)
        assert Y_AT + 2 * P + 5 * DM <= WORK_AT

        sems = {}
        for nm in ("dense_done act_drained dve_drained small_in xs_in const_ready wif_zeroed wif_in h_ready sq_done "
                   "sq_added rstd_ready rows_act rows_dve ml_scores ml_w ml_qi ml_pt ml_kw ml_num ml_c ml_rd ml_ssq "
                   "ml_rr ml_hn ml_ht ml_hm ck_tr ck_dve ck_act at_s at_mx at_exp at_wd at_tr at_wt at_o at_sq at_rr "
                   "at_on at_ot at_yc ya_ready th_ready u_ready conv_kept merged_added hist_ready conv_a g_ready "
                   "lam_dve lam_act state_out y_out dve_chain act_chain pool_chain cst_ready out_k out_v out_m out_C").split():
            sems[nm] = sem(nm)
        slot_in = [sem(f"slot_in{i}") for i in range(NSLOT)]
        S = sems

        def slot_of(item):
            return ITEMS.index(item) % NSLOT

        def wait_item(eng, item):
            i = ITEMS.index(item)
            mine = ITEMS[i % NSLOT:i + 1:NSLOT]
            eng.wait_ge(slot_in[i % NSLOT], sum(32 if x[:2] == "up" else 16 for x in mine))

        def wait_drained(eng, n):
            e, v = drained[n]
            eng.wait_ge(S[e + "_drained"], v)

        def wait_tmp_free(eng, k):
            if k >= 2:
                name, v = tmp_users[k - 2]
                eng.wait_ge(S[name], v)

        def dbuf(n):
            return D[:, 2 * (n % 2):2 * (n % 2) + 2, 0:HALF]

        def two(ap):
            return ap.rearrange("p (a b) -> p a b", a=2)

        def src_tok(name, j):
            return {"mk": mkT[:, j, :], "mv": f_tmp[:, j % 2, :], "dk": dkT[:, j, :], "dv": f_tmp[:, j % 2, :]}[name]

        block = ctx.enter_context(nc.Block())

        @block.sync
        def _(sp):
            def load(item):
                i = ITEMS.index(item)
                if i >= NSLOT:
                    old = ITEMS[i - NSLOT]
                    if old == "ck":
                        sp.wait_ge(S["ck_tr"], 2)
                    elif old == "cv":
                        sp.wait_ge(S["at_o"], 1)
                    else:
                        sp.wait_ge(S["dense_done"], last_block[old] + 1)
                dst = ring[:, i % NSLOT, :]
                s = slot_in[i % NSLOT]
                if item == "x":
                    sp.dma_start(dst.rearrange("p (c f) -> p c f", c=4),
                                 x_prompt[0].rearrange("(c p) f -> p c f", p=P)).then_inc(s, 16)
                elif item in ("ck", "cv"):
                    src = (cache_k if item == "ck" else cache_v)[0, 0].rearrange("(b p) h d -> p b (h d)", p=P)
                    sp.dma_start(dst.rearrange("p (b f) -> p b f", b=8), src).then_inc(s, 16)
                elif item in W_IN_AT:
                    at = W_IN_AT[item]
                    sp.dma_start(dst.rearrange("p (k f) -> p k f", k=KD),
                                 w_in[0][:, at:at + 512].rearrange("(k p) f -> p k f", p=P)).then_inc(s, 16)
                elif item[:2] == "br":
                    sp.dma_start(dst.rearrange("p (k f) -> p k f", k=4),
                                 w_branch[0, int(item[2])].rearrange("(k p) f -> p k f", p=P)).then_inc(s, 16)
                elif item[:2] == "wo":
                    at = 512 * "ab".index(item[2])
                    sp.dma_start(dst.rearrange("p (k f) -> p k f", k=KD),
                                 w_out[0][:, at:at + 512].rearrange("(k p) f -> p k f", p=P)).then_inc(s, 16)
                elif item[:2] == "up":
                    at = 256 * int(item[2:])
                    v = w_up[0].rearrange("(k p) (g f) -> p k g f", p=P, g=2)
                    for g in range(2):
                        sp.dma_start(dst.rearrange("p (g k f) -> p g k f", k=KD, g=2)[:, g],
                                     v[:, :, g, at:at + 256]).then_inc(s, 16)
                else:
                    at = P * int(item[2:])
                    sp.dma_start(dst[:, 0:JF * P].rearrange("p (k f) -> p k f", k=JF),
                                 w_down[0][:, at:at + P].rearrange("(k p) f -> p k f", p=P)).then_inc(s, 16)

            for item in ITEMS:
                load(item)
            for q in range(4):
                e, v = drained[block_of[("yT", 2 * q + 1)]]
                sp.wait_ge(S[e + "_drained"], v)
                f = slice(256 * q, 256 * q + 256)
                sp.dma_start(y_p[0].rearrange("(c p) f -> p c f", p=P)[:, :, f], yst[:, :, f]).then_inc(S["y_out"], 16)
                sp.dma_start(y_s[0][:, f], yst_s[0:TS, f]).then_inc(S["y_out"], 16)
            sp.wait_ge(S["y_out"], 8 * 16)
            sp.wait_ge(S["out_k"], 32)
            sp.wait_ge(S["out_v"], 32)
            sp.wait_ge(S["out_m"], 32)
            sp.wait_ge(S["out_C"], 64)
            sp.wait_ge(S["state_out"], 64)

        @block.gpsimd
        def _(pool):
            g = nc.gpsimd
            chain = [0]

            def link(ins):
                chain[0] += 1
                ins.then_inc(S["pool_chain"], 1)
                pool.wait_ge(S["pool_chain"], chain[0])

            g.memset(wif[:], 0.0).then_inc(S["wif_zeroed"], 1)
            link(g.memset(ident[:], 0.0))
            g.affine_select(out=ident[:], in_=ident[:], compare_op=ALU.not_equal, fill=1.0, base=0,
                            pattern=[[-1, P]], channel_multiplier=1).then_inc(S["const_ready"], 1)
            g.memset(mean_w[:], 1.0 / DM).then_inc(S["const_ready"], 1)
            g.memset(xT[:, :, TP:S0], 0.0).then_inc(S["const_ready"], 1)
            link(g.memset(causal[:], 0.0))
            g.affine_select(out=causal[:], in_=causal[:], compare_op=ALU.is_ge, fill=NEG, base=0,
                            pattern=[[1, P]], channel_multiplier=-1).then_inc(S["const_ready"], 1)
            link(g.memset(half_row[:], 0.0))
            g.memset(half_row[0:1, 0:64], 1.0).then_inc(S["const_ready"], 1)
            g.memset(neg_row[:], NEG).then_inc(S["const_ready"], 1)
            g.memset(m_half[:], -0.5).then_inc(S["const_ready"], 1)
            g.memset(C_p[:], 0.0).then_inc(S["const_ready"], 1)
            g.memset(mv_tok[:, :, :, P:P + 1], 1.0).then_inc(S["const_ready"], 1)
            link(g.memset(sel[0:H], 0.0))
            g.affine_select(out=sel[0:H], in_=sel[0:H], compare_op=ALU.not_equal, fill=1.0, base=0,
                            pattern=[[-1, H], [0, P]], channel_multiplier=1).then_inc(S["const_ready"], 1)

            def rstd_small(x, scale, out, done):
                link(g.tensor_scalar(x, x, 1.0 / P, EPS, ALU.mult, ALU.add))
                link(g.tensor_tensor(x, x, m_half[0:x.shape[0], 0:1].to_broadcast(list(x.shape)), ALU.pow))
                g.tensor_tensor(out, x, scale, ALU.mult).then_inc(S[done], 1)

            for kind, a, n in ORDER:
                if kind in ("xT", "wo", "dn"):
                    r = {"xT": 0, "wo": 1, "dn": 2}[kind]
                    k = tmp_index[("sq", r, a[0])]
                    pool.wait_ge(S["sq_done"], KD * r + a[0] + 1)
                    if a[0] == 0:
                        g.tensor_copy(ssum[:], tmp[:, k % 2, :]).then_inc(S["sq_added"], 1)
                    else:
                        pool.wait_ge(S["sq_added"], KD * r + a[0])
                        g.tensor_tensor(ssum[:], ssum[:], tmp[:, k % 2, :], ALU.add).then_inc(S["sq_added"], 1)
                elif kind == "ml" and a[0] == 0:
                    c, (col, L) = a[1], TILES[a[1]]
                    pool.wait_ge(S["ml_w"], c + 1)
                    if c >= 1:
                        pool.wait_ge(S["ml_num"], c)
                    wait_drained(pool, block_of[("tok", ("mk", 3))])
                    g.tensor_tensor(kw[0:L], mk_tok[0:L, c], w_ml[0:L, :, L - 1:L].to_broadcast([L, H, P]),
                                    ALU.mult).then_inc(S["ml_kw"], 1)
                elif kind == "ml" and a[0] == 1:
                    c, (col, L) = a[1], TILES[a[1]]
                    pool.wait_ge(S["ml_ssq"], c + 1)
                    rstd_small(ssq[0:L, :], rden[0:L, :], rr[0:L, :], "ml_rr")
                    if c >= 3:
                        pool.wait_ge(S["ml_c"], c + 1)
                        Cn, oC, on_ = (C_p, p_C, p_n) if c == 3 else (C_s, s_C, s_n)
                        pool.dma_start(oC[0, 0].rearrange("h d e -> d h e"), Cn[:, :, 0:P]).then_inc(S["out_C"], 16)
                        pool.dma_start(on_[0, 0].rearrange("h d -> d h").unsqueeze(2), Cn[:, :, P:P + 1],
                                       allow_slow_non_contiguous=True)\
                            .then_inc(S["out_C"], 16)
                elif kind == "tok" and a[0] in (("dk", 3), ("dv", 3)):
                    wait_drained(pool, n)
                    tok, op, os, so = (k_out, p_k, s_k, "out_k") if a[0][0] == "dk" else \
                        (dv_tok.rearrange("p c h d -> p c (h d)"), p_v, s_v, "out_v")
                    pool.dma_start(op[0, 0].rearrange("(c p) h d -> p c (h d)", p=P), tok[:, 0:4, :])\
                        .then_inc(S[so], 16)
                    pool.dma_start(os[0, 0].rearrange("t h d -> t (h d)"), tok[0:TS, 4, :]).then_inc(S[so], 16)
                elif kind == "gtr":
                    pool.wait_ge(S["rows_dve"], 6)
                    pool.dma_start(p_m[0, 0].unsqueeze(1), row["m"][:, TP - 1:TP],
                                   allow_slow_non_contiguous=True).then_inc(S["out_m"], 16)
                    pool.dma_start(s_m[0, 0].unsqueeze(1), row["m"][:, T - 1:T],
                                   allow_slow_non_contiguous=True).then_inc(S["out_m"], 16)
                elif kind == "sx":
                    j = a[0]
                    pool.wait_ge(S["u_ready"], j + 1)
                    g.tensor_copy(conv_last[:, 0, :, j], u_c[:, j, TP:TP + 2])
                    g.tensor_copy(conv_last[:, 1, :, j], u_c[:, j, T:T + 2]).then_inc(S["conv_kept"], 1)
                elif kind == "at" and a[0] == 2:
                    u = a[1]
                    pool.wait_ge(S["at_sq"], u + 1)
                    rstd_small(assq[:, u % 2:u % 2 + 1], rsum[:, u % 4, 0:1], arr[:, u % 2:u % 2 + 1], "at_rr")
                elif kind == "norm" and a[0] == 1:
                    pool.wait_ge(S["rstd_ready"], 2)
                    for part in range(2):
                        for b in range(2):
                            last = g.memset(ups[:, part, b, 0:2], 0.0)
                    last.then_inc(S["conv_kept"], 1)
                elif kind == "up":
                    j, part = a
                    jj = j + JF * part
                    buf = ups[:, part, j % 2, :]
                    wait_drained(pool, n)
                    g.tensor_copy(buf[:, S0:S0 + 2], hist[:, :, jj])
                    g.tensor_copy(ffn_last[:, 0, :, jj], buf[:, TP:TP + 2])
                    g.tensor_copy(ffn_last[:, 1, :, jj], buf[:, T:T + 2]).then_inc(S["hist_ready"], 1)
                elif kind == "state":
                    pool.wait_ge(S["cst_ready"], 2)
                    pool.dma_start(p_ffn[0, 0].rearrange("r (j f) -> (r j) f", f=P), fst[0:2 * JU, 0, :])\
                        .then_inc(S["state_out"], 16)
                    pool.dma_start(s_ffn[0, 0].rearrange("r (j f) -> (r j) f", f=P), fst[0:2 * JU, 1, :])\
                        .then_inc(S["state_out"], 16)
                    pool.dma_start(p_conv[0, 0].rearrange("r (j f) -> (r j) f", f=P), cst[0:8, :])\
                        .then_inc(S["state_out"], 16)
                    pool.dma_start(s_conv[0, 0].rearrange("r (j f) -> (r j) f", f=P), cst[8:16, :])\
                        .then_inc(S["state_out"], 16)

        @block.scalar
        def _(act):
            sc = nc.scalar
            chain = [0]

            def link(ins):
                chain[0] += 1
                ins.then_inc(S["act_chain"], 1)
                act.wait_ge(S["act_chain"], chain[0])

            def small(dst, src):
                act.dma_start(dst, src, allow_slow_non_contiguous=True).then_inc(S["small_in"], 16)

            act.dma_start(x_s[0:TS, :], x_sample[0]).then_inc(S["xs_in"], 16)
            rows = lambda ap: ap.rearrange("(j f) -> j f", f=P)
            small(small_a[0:8, :], rows(norm1[0]))
            small(small_a[8:16, :], rows(norm2[0]))
            small(small_a[16:24, :], rows(norm_f))
            small(small_a[24:36, :], w_sc_conv[0].rearrange("t (j f) -> (t j) f", f=P))
            small(small_a[36:44, :], state_conv[0, 0].rearrange("t (j f) -> (t j) f", f=P))
            small(small_a[44:48, :], ml_norm[0])
            small(small_a[48:49, :], da_norm)
            small(small_b[0:2 * JU, :], state_ffn[0, 0].rearrange("t (j f) -> (t j) f", f=P))
            fc = w_fconv[0].rearrange("t (j f) -> (t j) f", f=P)
            small(small_c[0:66, 0, :], fc[0:66, :])
            small(small_c[0:66, 1, :], fc[66:132, :])
            small(b_i[:], b_if[0, 0].unsqueeze(1))
            small(b_f[:], b_if[0, 1].unsqueeze(1))
            small(m_s[:], state_m[0, 0].unsqueeze(1))
            small(lam_t[:], da_lambda[0].rearrange("(a b) f -> a b f", a=2).unsqueeze(0).to_broadcast([P, 2, 2, 64]))
            small(C_s[:, :, 0:P], state_C[0, 0].rearrange("h d e -> d h e"))
            small(C_s[:, :, P:P + 1], state_n[0, 0].rearrange("h d -> d h").unsqueeze(2))
            act.wait_ge(S["wif_zeroed"], 1)
            act.dma_start(wif[:, :, 0:H], w_in[0][:, IG_AT:IG_AT + H].rearrange("(k p) f -> p k f", p=P))\
                .then_inc(S["wif_in"], 16)
            act.dma_start(wif[:, :, 32:32 + H], w_in[0][:, FG_AT:FG_AT + H].rearrange("(k p) f -> p k f", p=P))\
                .then_inc(S["wif_in"], 16)
            act.wait_ge(S["lam_dve"], 2)
            sc.activation(lam_e[:], lam_e[:], ACT.Exp).then_inc(S["lam_act"], 1)

            def square_block(r, j, n):
                k = tmp_index[("sq", r, j)]
                wait_drained(act, n)
                wait_tmp_free(act, k)
                sc.activation(tmp[:, k % 2, :], xT[:, j, :], ACT.Square).then_inc(S["sq_done"], 1)

            sq_wait = None
            th = [0]
            for kind, a, n in ORDER:
                if kind in ("xT", "wo", "dn"):
                    if kind == "xT" and a[0] == 0:
                        act.wait_ge(S["const_ready"], 10)
                    square_block({"xT": 0, "wo": 1, "dn": 2}[kind], a[0], n)
                elif kind == "norm":
                    act.wait_ge(S["dense_done"], n + 1)
                    sc.activation(two(rstd), dbuf(n), ACT.Ln, bias=EPS).then_inc(S["act_drained"], 1)
                    act.wait_ge(S["act_drained"], drained[n][1])
                    sc.activation(rstd, rstd, ACT.Exp, scale=-0.5).then_inc(S["rstd_ready"], 1)
                elif kind == "if":
                    act.wait_ge(S["dense_done"], n + 1)
                    act.wait_ge(S["small_in"], 16 * 16)
                    sc.activation(two(row["ig"]), dbuf(n)[0:H], ACT.Identity, bias=b_i[:])
                    sc.activation(two(row["lf"]), dbuf(n)[32:32 + H], ACT.Copy).then_inc(S["act_drained"], 1)
                    act.wait_ge(S["rows_dve"], 1)
                    link(sc.activation(row["g"], row["lf"], ACT.Abs))
                    link(sc.activation(row["g"], row["g"], ACT.Exp, scale=-1.0))
                    sc.activation(row["g"], row["g"], ACT.Ln, bias=1.0).then_inc(S["rows_act"], 1)
                    act.wait_ge(S["rows_dve"], 7)
                    sc.activation(row["em"], row["m"], ACT.Exp, scale=-1.0)
                    sc.activation(row["inter"][:, 0:P], row["u"][:, 0:P], ACT.Exp)
                    for col, L in TILES[1:4]:
                        sc.activation(row["inter"][:, col:col + L], row["u"][:, col:col + L], ACT.Exp,
                                      bias=row["m"][:, col - 1:col])
                    sc.activation(row["inter"][:, S0:T], row["u"][:, S0:T], ACT.Exp, bias=m_s[:])\
                        .then_inc(S["rows_act"], 1)
                elif kind in ("mk", "mq", "mv", "dk", "dv", "dq", "sc"):
                    j = a[0]
                    act.wait_ge(S["dense_done"], n + 1)
                    if kind in ("mv", "dv"):
                        if (kind, j) == ("mv", 0):
                            wait_drained(act, block_of[("small",)])
                            act.wait_ge(S["lam_dve"], 3)
                        elif j >= 2:
                            act.wait_ge(S["dense_done"], block_of[("tok", (kind, j - 2))] + 1)
                    if kind == "sc" and j == 0:
                        act.wait_ge(S["out_C"], 64)
                    dst = {"mk": mkT, "mq": mqT, "dk": dkT, "dq": dqT, "sc": scb}.get(kind)
                    dst = f_tmp[:, j % 2, :] if dst is None else dst[:, j, :]
                    scale = {"mk": P ** -0.5, "dq": 64 ** -0.5}.get(kind, 1.0)
                    sc.activation(two(dst), dbuf(n), ACT.Copy, scale=scale).then_inc(S["act_drained"], 1)
                elif kind == "ml":
                    stage, c = a
                    col, L = TILES[c]
                    if stage == 0:
                        act.wait_ge(S["ml_scores"], c + 1)
                        wait_drained(act, block_of[("gtr", 0)])
                        if c >= 1:
                            act.wait_ge(S["ml_pt"], c)
                            act.wait_ge(S["ml_kw"], c)
                        for h in range(H):
                            last = sc.activation(w_ml[0:L, h, 0:L], X[0:L, 0, P * h:P * h + L], ACT.Exp,
                                                 bias=gT[0:L, c, h:h + 1])
                        last.then_inc(S["ml_w"], 1)
                    elif stage == 1:
                        act.wait_ge(S["ml_rd"], c + 1)
                        for h in range(H):
                            last = sc.activation(tmp[0:L, 0, P * h:P * h + P],
                                                 X[0:L, h // 2, 129 * (h % 2):129 * (h % 2) + P], ACT.Square,
                                                 scale=rden[0:L, h:h + 1], accum_out=ssq[0:L, h:h + 1])
                        last.then_inc(S["ml_ssq"], 1)
                    else:
                        act.wait_ge(S["ml_ht"], c + 1)
                        for h in range(H):
                            last = sc.activation(mqT[:, h, col:col + L], X[:, 0, P * h:P * h + L], ACT.Copy,
                                                 scale=vec[:, 44 + h:45 + h])
                        last.then_inc(S["ml_hm"], 1)
                elif kind == "ck":
                    act.wait_ge(S["ck_tr"], a[0] + 1)
                    sc.activation(ckT[:, 2 * a[0] + 1, :].rearrange("p (a b) -> p a b", a=2), X[:, 2:4, :],
                                  ACT.Copy).then_inc(S["ck_act"], 1)
                elif kind == "sample":
                    c = a[0]
                    act.wait_ge(S["at_mx"], c + 1)
                    sc.activation(prob[:, c, :], X[:].rearrange("p a b -> p (a b)")[:, 0:1056], ACT.Exp,
                                  bias=nmax[:, 0, c:c + 1], accum_out=psum_p[:, 0, c:c + 1]).then_inc(S["at_exp"], 1)
                elif kind == "at":
                    stage, u = a
                    h, i = (u - 1) // 4, (u - 1) % 4
                    nk = P * (i + 1)
                    if stage == 0:
                        act.wait_ge(S["at_mx"], u + 2)
                        if u >= 2:
                            act.wait_ge(S["at_tr"], u - 1)
                        for c in range(2):
                            last = sc.activation(prob2[:, u % 2, c, 0:nk], X[:, c, 0:nk], ACT.Exp,
                                                 bias=nmax[:, u % 2, c:c + 1], accum_out=psum_p[:, u % 2, c:c + 1])
                        last.then_inc(S["at_exp"], 1)
                    elif stage == 1:
                        act.wait_ge(S["at_tr"], u + 1)
                        if u == 0:
                            sc.activation(wdT[:, 0:8, :].rearrange("p a b -> p (a b)"),
                                          X[:].rearrange("p a b -> p (a b)")[:, 0:1024], ACT.Copy)
                            sc.activation(wdT[0:TS, 8, :], X[0:TS, 2, 0:P], ACT.Copy).then_inc(S["at_wt"], 1)
                        else:
                            act.wait_ge(S["at_o"], max(u - 1, 1))
                            sc.activation(wdT[:, 4 * (u % 2):4 * (u % 2) + i + 1, :].rearrange("p a b -> p (a b)"),
                                          X[:, 2, 0:nk], ACT.Copy).then_inc(S["at_wt"], 1)
                    elif stage == 2:
                        act.wait_ge(S["at_o"], u + 1)
                        sc.activation(junk, X[:, 3, 0:P], ACT.Square, scale=rsum[:, u % 4, 0:1],
                                      accum_out=assq[:, u % 2:u % 2 + 1]).then_inc(S["at_sq"], 1)
                    else:
                        act.wait_ge(S["at_ot"], u + 1)
                        if u == 0:
                            sc.activation(dqT[:, :, S0:T], X[:, 2, 0:P].rearrange("p (h t) -> p h t", h=H),
                                          ACT.Copy, scale=vec[:, 48:49]).then_inc(S["at_yc"], 1)
                        else:
                            sc.activation(dqT[:, h, P * i:P * i + P], X[:, 2, 0:P], ACT.Copy,
                                          scale=vec[:, 48:49]).then_inc(S["at_yc"], 1)
                elif kind in ("mo", "gt"):
                    act.wait_ge(S["dense_done"], n + 1)
                    if kind == "gt" and a[0] == 2:
                        if a[1] == 0:
                            wait_drained(act, block_of[("sb", 3)])
                        sc.activation(two(gate2[:, a[1], :]), dbuf(n), ACT.Tanh, scale=0.5)\
                            .then_inc(S["act_drained"], 1)
                    else:
                        k = tmp_index[(kind, *a)]
                        wait_tmp_free(act, k)
                        sc.activation(two(tmp[:, k % 2, :]), dbuf(n), ACT.Tanh, scale=0.5)\
                            .then_inc(S["act_drained"], 1)
                elif kind == "up":
                    j, part = a
                    jj = j + JF * part
                    act.wait_ge(S["dense_done"], n + 1)
                    if j < 2:
                        act.wait_ge(S["conv_kept"], 5)
                    else:
                        act.wait_ge(S["g_ready"], j - 1)
                    sc.activation(two(ups[:, part, j % 2, 2:T + 2]), dbuf(n), ACT.Copy)
                    sc.activation(two(acc[:, part, j % 2, :]), dbuf(n), ACT.Copy, scale=fcw[:, 2, jj:jj + 1])\
                        .then_inc(S["act_drained"], 1)
                    if part == 1:
                        k = tmp_index[("up", j)]
                        act.wait_ge(S["conv_a"], j + 1)
                        wait_tmp_free(act, k)
                        sc.activation(tmp[:, k % 2, :], acc[:, 0, j % 2, :], ACT.Tanh, scale=0.5)\
                            .then_inc(S["th_ready"], 1)
                elif kind == "yT":
                    j = a[0]
                    act.wait_ge(S["dense_done"], n + 1)
                    b = 2 * (n % 2)
                    sc.activation(yst[:, :, P * j:P * j + P], D[:, b, :].rearrange("p (c f) -> p c f", c=4), ACT.Copy)
                    sc.activation(yst_s[0:TS, P * j:P * j + P], D[0:TS, b + 1, 0:P], ACT.Copy)\
                        .then_inc(S["act_drained"], 1)

        @block.vector
        def _(dve):
            v = nc.vector
            chain = [0]

            def link(ins):
                chain[0] += 1
                ins.then_inc(S["dve_chain"], 1)
                dve.wait_ge(S["dve_chain"], chain[0])

            def combine(u, p0, p1):
                s = psum_p[:, u % 2, :]
                dve.wait_ge(S["at_exp"], u + 2)
                if u == 0:
                    dve.wait_ge(S["lam_dve"], 3)
                link(v.reciprocal(rsum[:, u % 4, :], s))
                link(v.scalar_tensor_tensor(out=kap[:], in0=s[:, 0:1], scalar=rsum[:, u % 4, 1:2], in1=neg_lam[:],
                                            op0=ALU.mult, op1=ALU.mult))
                v.scalar_tensor_tensor(out=p0, in0=p1, scalar=kap[:], in1=p0, op0=ALU.mult, op1=ALU.add)\
                    .then_inc(S["at_wd"], 1)

            for kind, a, n in ORDER:
                b = None if n is None else 2 * (n % 2)
                if kind == "small":
                    dve.wait_ge(S["small_in"], 16 * 16)
                    link(v.tensor_tensor(lam_p[:], lam_t[:, :, 0, :], lam_t[:, :, 1, :], ALU.mult))
                    v.reduce_sum(lam_e[:], lam_p[:], axis=AX.X).then_inc(S["lam_dve"], 2)
                    dve.wait_ge(S["lam_act"], 1)
                    link(v.tensor_scalar(neg_lam[:], lam_e[:, 1:2], -LAM_INIT, None, ALU.add))
                    v.tensor_tensor(neg_lam[:], neg_lam[:], lam_e[:, 0:1], ALU.subtract).then_inc(S["lam_dve"], 1)
                    dve.wait_ge(S["dense_done"], n + 1)
                    link(v.tensor_copy(vec[:], D[:, b, 0:49]))
                    link(v.tensor_scalar(vec[:, 44:48], vec[:, 44:48], 0.5, None, ALU.mult))
                    link(v.tensor_scalar(vec[:, 48:49], vec[:, 48:49], 1.0 - LAM_INIT, None, ALU.mult))
                    v.tensor_copy(hist[:].rearrange("p a b -> p (a b)"), D[:, b, 49:49 + 2 * JU])
                    v.tensor_copy(fcw[:].rearrange("p a b -> p (a b)"), D[:, b + 1, 0:3 * JU])\
                        .then_inc(S["dve_drained"], 1)
                elif kind == "xT":
                    dve.wait_ge(S["dense_done"], n + 1)
                    v.tensor_copy(xT[:, a[0], 0:TP], D[:, b, :])
                    v.tensor_copy(xT[:, a[0], S0:T], D[:, b + 1, 0:TS]).then_inc(S["dve_drained"], 1)
                elif kind == "norm":
                    r = a[0]
                    dve.wait_ge(S["rstd_ready"], r + 1)
                    dst = hT if r < 2 else xT
                    for j in range(KD):
                        v.scalar_tensor_tensor(out=dst[:, j, :], in0=xT[:, j, :], scalar=vec[:, KD * r + j:KD * r + j + 1],
                                               in1=rstd, op0=ALU.mult, op1=ALU.mult).then_inc(S["h_ready"], 1)
                elif kind == "if":
                    wait_drained(dve, n)
                    v.tensor_scalar(row["lf"], row["lf"], b_f[:], None, ALU.add).then_inc(S["rows_dve"], 1)
                    link(v.memset(row["em"], 1.0))
                    for col, _ in TILES:
                        last = v.memset(row["em"][:, col:col + 1], 0.0)
                    last.then_inc(S["rows_dve"], 1)
                    dve.wait_ge(S["rows_act"], 1)
                    dve.wait_ge(S["rows_dve"], 2)
                    v.scalar_tensor_tensor(out=row["lf"], in0=row["lf"], scalar=0.0, in1=row["g"], op0=ALU.min,
                                           op1=ALU.subtract).then_inc(S["rows_dve"], 1)
                    dve.wait_ge(S["rows_dve"], 3)
                    v.tensor_tensor_scan(row["cum"], row["em"], row["lf"], 0.0, ALU.mult, ALU.add)
                    v.memset(row["m"][:, TP:S0], 0.0)
                    v.tensor_tensor_scan(row["m"][:, 0:TP], row["lf"][:, 0:TP], row["ig"][:, 0:TP], 0.0,
                                         ALU.add, ALU.max).then_inc(S["rows_dve"], 2)
                    v.tensor_tensor_scan(row["m"][:, S0:T], row["lf"][:, S0:T], row["ig"][:, S0:T], m_s[:],
                                         ALU.add, ALU.max).then_inc(S["rows_dve"], 1)
                    dve.wait_ge(S["rows_dve"], 6)
                    v.tensor_tensor(row["g"], row["ig"], row["cum"], ALU.subtract)
                    v.tensor_tensor(row["u"], row["cum"], row["m"], ALU.subtract).then_inc(S["rows_dve"], 1)
                elif kind == "tok":
                    name, j = a[0]
                    dve.wait_ge(S["dense_done"], n + 1)
                    if name == "dv" or name == "mv":
                        dst = (mv_tok if name == "mv" else dv_tok)[:, :, j, 0:P]
                    elif name == "mk":
                        dst = mk_tok[:, :, j, :]
                    else:
                        dst = k_out[:, :, P * j:P * j + P]
                    v.tensor_copy(dst[:, 0:4, :], D[:, b, :].rearrange("p (c f) -> p c f", c=4))
                    v.tensor_copy(dst[0:TS, 4, :], D[0:TS, b + 1, 0:P]).then_inc(S["dve_drained"], 1)
                elif kind == "gtr":
                    dve.wait_ge(S["dense_done"], n + 1)
                    for t, s in ((gT, 0), (emT, 1)):
                        v.tensor_copy(t[:, 0:4, :], D[:, b + s, 0:16].rearrange("p (c h) -> p c h", c=4))
                        last = v.tensor_copy(t[0:TS, 4, :], D[0:TS, b + s, 16:20])
                    last.then_inc(S["dve_drained"], 1)
                elif kind == "ml":
                    stage, c = a
                    col, L = TILES[c]
                    C = C_p if c < 4 else C_s
                    if stage == 0:
                        dve.wait_ge(S["ml_scores"], c + 1)
                        if c >= 1:
                            dve.wait_ge(S["ml_num"], c)
                        inter = X[:, 2, :].rearrange("p (h t) -> p h t", h=H)
                        v.tensor_tensor(qi[:, :, 0:L], mqT[:, :, col:col + L], inter[:, :, 0:L], ALU.mult)
                        v.tensor_copy(il[:], inter[:, :, L - 1]).then_inc(S["ml_qi"], 1)
                        dve.wait_ge(S["ml_w"], c + 1)
                        scores = X[:, 1, :].rearrange("p (h t) -> p h t", h=H)
                        v.tensor_tensor(p_ml[0:L, :, 0:L], w_ml[0:L, :, 0:L], scores[0:L, :, 0:L], ALU.mult)\
                            .then_inc(S["ml_pt"], 1)
                    elif stage == 1:
                        dve.wait_ge(S["ml_num"], c + 1)
                        num = X[0:L, 0:2, 0:2 * (P + 1)].rearrange("p a (b e) -> p a b e", b=2)
                        den2 = den[0:L, :].rearrange("p (a b) -> p a b", a=2)
                        em2 = emT[0:L, c, :].rearrange("p (a b) -> p a b", a=2)
                        link(v.scalar_tensor_tensor(out=den2, in0=num[:, :, :, P], scalar=-1.0, in1=em2,
                                                    op0=ALU.mult, op1=ALU.max))
                        link(v.scalar_tensor_tensor(out=den2, in0=num[:, :, :, P], scalar=1.0, in1=den2,
                                                    op0=ALU.mult, op1=ALU.max))
                        v.reciprocal(rden[0:L, :], den[0:L, :]).then_inc(S["ml_rd"], 1)
                        dve.wait_ge(S["ml_qi"], c + 1)
                        for h in range(H):
                            last = v.scalar_tensor_tensor(out=C[:, h, :], in0=C[:, h, :], scalar=il[:, h:h + 1],
                                                          in1=X[:, 2 + h // 2, 129 * (h % 2):129 * (h % 2) + 129],
                                                          op0=ALU.mult, op1=ALU.add)
                        last.then_inc(S["ml_c"], 1)
                        dve.wait_ge(S["ml_rr"], c + 1)
                        if c >= 1:
                            dve.wait_ge(S["ml_ht"], c)
                        rr2 = rr[0:L, :].rearrange("p (a b) -> p a b", a=2).unsqueeze(3).to_broadcast([L, 2, 2, P])
                        v.tensor_tensor(hn[0:L].rearrange("p (a b) e -> p a b e", a=2), num[:, :, :, 0:P], rr2,
                                        ALU.mult).then_inc(S["ml_hn"], 1)
                elif kind == "ck":
                    dve.wait_ge(S["ck_tr"], a[0] + 1)
                    v.tensor_copy(ckT[:, 2 * a[0], :].rearrange("p (a b) -> p a b", a=2), X[:, 0:2, :])\
                        .then_inc(S["ck_dve"], 1)
                elif kind == "sample":
                    c = a[0]
                    dve.wait_ge(S["at_s"], c + 1)
                    v.tensor_reduce(nmax[:, 0, c:c + 1], X[:].rearrange("p a b -> p (a b)")[:, 0:1056], AX.X, ALU.max,
                                    negate=True).then_inc(S["at_mx"], 1)
                    if c == 1:
                        combine(0, prob[:, 0, :], prob[:, 1, :])
                elif kind == "at":
                    stage, u = a
                    if stage == 0:
                        nk = P * ((u - 1) % 4 + 1)
                        dve.wait_ge(S["at_s"], u + 2)
                        v.tensor_reduce(nmax[:, u % 2, :], X[:, 0:2, 0:nk], AX.X, ALU.max, negate=True)\
                            .then_inc(S["at_mx"], 1)
                        combine(u, prob2[:, u % 2, 0, 0:nk], prob2[:, u % 2, 1, 0:nk])
                    elif stage == 2:
                        dve.wait_ge(S["at_rr"], u + 1)
                        if u >= 2:
                            dve.wait_ge(S["at_ot"], u - 1)
                        v.tensor_scalar(on[:, u % 2, :], X[:, 3, 0:P], arr[:, u % 2:u % 2 + 1], None, ALU.mult)\
                            .then_inc(S["at_on"], 1)
                elif kind == "mo":
                    k = tmp_index[("mo", a[0])]
                    wait_drained(dve, n)
                    dve.wait_ge(S["ml_hm"], 5)
                    v.scalar_tensor_tensor(out=mqT[:, a[0], :], in0=tmp[:, k % 2, :], scalar=1.0, in1=mqT[:, a[0], :],
                                           op0=ALU.add, op1=ALU.mult).then_inc(S["ya_ready"], 1)
                elif kind == "sx":
                    j = a[0]
                    dve.wait_ge(S["dense_done"], n + 1)
                    wait_drained(dve, block_of[("sc", j)])
                    v.memset(u_c[:, j, 0:2], 0.0)
                    v.tensor_tensor(two(u_c[:, j, 2:T + 2]), dbuf(n), two(scb[:, j, :]), ALU.mult)\
                        .then_inc(S["dve_drained"], 1)
                    wait_drained(dve, n)
                    link(v.tensor_copy(u_c[:, j, S0:S0 + 2],
                                       vec[:, 36:44].rearrange("p (r j) -> p r j", r=2)[:, :, j]))
                    w = lambda t: vec[:, 24 + 4 * t + j:25 + 4 * t + j]
                    v.tensor_scalar(scb[:, j, :], u_c[:, j, 0:T], w(0), None, ALU.mult).then_inc(S["u_ready"], 1)
                    dve.wait_ge(S["u_ready"], j + 1)
                    link(v.scalar_tensor_tensor(out=scb[:, j, :], in0=u_c[:, j, 1:T + 1], scalar=w(1), in1=scb[:, j, :],
                                                op0=ALU.mult, op1=ALU.add))
                    link(v.scalar_tensor_tensor(out=scb[:, j, :], in0=u_c[:, j, 2:T + 2], scalar=w(2), in1=scb[:, j, :],
                                                op0=ALU.mult, op1=ALU.add))
                elif kind == "sb":
                    dve.wait_ge(S["dense_done"], n + 1)
                    v.tensor_tensor(two(scb[:, a[0], :]), dbuf(n), two(scb[:, a[0], :]), ALU.mult)\
                        .then_inc(S["dve_drained"], 1)
                elif kind == "pr":
                    br, j = a
                    dve.wait_ge(S["dense_done"], n + 1)
                    if br == 2:
                        g = gate2[:, j, :]
                    else:
                        g = tmp[:, tmp_index[("gt", br, j)] % 2, :]
                    wait_drained(dve, block_of[("gt", br, j)])
                    if br == 1 and j == 0:
                        dve.wait_ge(S["out_k"], 32)
                    out = merged[:, j, :] if br == 1 else g
                    v.scalar_tensor_tensor(out=two(out), in0=two(g), scalar=1.0, in1=dbuf(n), op0=ALU.add,
                                           op1=ALU.mult).then_inc(S["dve_drained"], 1)
                    if br != 1:
                        wait_drained(dve, n)
                        v.tensor_tensor(merged[:, j, :], merged[:, j, :], g, ALU.add).then_inc(S["merged_added"], 1)
                elif kind in ("wo", "dn"):
                    dve.wait_ge(S["dense_done"], n + 1)
                    v.scalar_tensor_tensor(out=two(xT[:, a[0], :]), in0=dbuf(n), scalar=0.5, in1=two(xT[:, a[0], :]),
                                           op0=ALU.mult, op1=ALU.add).then_inc(S["dve_drained"], 1)
                elif kind == "up":
                    j, part = a
                    jj = j + JF * part
                    u, ac = ups[:, part, j % 2, :], acc[:, part, j % 2, :]
                    dve.wait_ge(S["hist_ready"], 2 * j + part + 1)
                    link(v.scalar_tensor_tensor(out=ac, in0=u[:, 1:T + 1], scalar=fcw[:, 1, jj:jj + 1], in1=ac,
                                                op0=ALU.mult, op1=ALU.add))
                    last = v.scalar_tensor_tensor(out=ac, in0=u[:, 0:T], scalar=fcw[:, 0, jj:jj + 1], in1=ac,
                                                  op0=ALU.mult, op1=ALU.add)
                    if part == 0:
                        last.then_inc(S["conv_a"], 1)
                    else:
                        link(last)
                        k = tmp_index[("up", j)]
                        dve.wait_ge(S["th_ready"], j + 1)
                        dve.wait_ge(S["conv_a"], j + 1)
                        link(v.scalar_tensor_tensor(out=acc[:, 0, j % 2, :], in0=tmp[:, k % 2, :], scalar=1.0,
                                                    in1=acc[:, 0, j % 2, :], op0=ALU.add, op1=ALU.mult))
                        v.tensor_tensor(gff[:, j, :], acc[:, 0, j % 2, :], ac, ALU.mult).then_inc(S["g_ready"], 1)
                elif kind == "state":
                    dve.wait_ge(S["dense_done"], n + 1)
                    v.tensor_copy(fst[0:2 * JU], D[0:2 * JU, b, 0:2 * P].rearrange("p (g f) -> p g f", g=2))\
                        .then_inc(S["cst_ready"], 1)
                    v.tensor_copy(cst, D[0:16, b + 1, 0:P]).then_inc(S["cst_ready"], 1)
                    v.memset(kap[:], 0.0).then_inc(S["dve_drained"], 1)

        @block.tensor
        def _(pe):
            t = nc.tensor

            def product(n, kc, lhsT, rhs, first_wait=None):
                for half in range(2):
                    for k in range(kc):
                        if half == 0 and first_wait:
                            first_wait(k)
                        last = t.matmul(D[0:lhsT(k).shape[1], 2 * (n % 2) + half, 0:HALF], lhsT(k),
                                        rhs(k)[:, HALF * half:HALF * half + HALF], start=k == 0, stop=k == kc - 1)
                last.then_inc(S["dense_done"], 1)

            seen = set()

            def arrived(item):
                if item not in seen:
                    seen.add(item)
                    wait_item(pe, item)

            def slot(item, k):
                return ring[:, slot_of(item), :].rearrange("p (k f) -> p k f", k=k)

            first_h = {}
            for kind, a, n in ORDER:
                if n is not None and n >= 2:
                    wait_drained(pe, n - 2)
                b = None if n is None else 2 * (n % 2)
                item = item_of(kind, a)
                if item:
                    arrived(item)
                if kind == "small":
                    pe.wait_ge(S["const_ready"], 10)
                    pe.wait_ge(S["small_in"], 16 * 16)
                    t.transpose(D[:, b, 0:49], small_a[0:49, :], ident[0:49, 0:49])
                    t.transpose(D[:, b, 49:49 + 2 * JU], small_b[0:2 * JU, :], ident[0:2 * JU, 0:2 * JU])
                    t.transpose(D[:, b + 1, 0:66], small_c[0:66, 0, :], ident[0:66, 0:66])
                    t.transpose(D[:, b + 1, 66:132], small_c[0:66, 1, :], ident[0:66, 0:66])\
                        .then_inc(S["dense_done"], 1)
                elif kind == "xT":
                    j = a[0]
                    if j == 0:
                        pe.wait_ge(S["xs_in"], 16)
                    xs = slot("x", 4)
                    for c in range(4):
                        t.transpose(D[:, b, P * c:P * c + P], xs[:, c, P * j:P * j + P], ident[:])
                    t.transpose(D[:, b + 1, 0:TS], x_s[0:TS, P * j:P * j + P], ident[0:TS, 0:TS])\
                        .then_inc(S["dense_done"], 1)
                elif kind == "norm":
                    pe.wait_ge(S["sq_added"], KD * (a[0] + 1))
                    product(n, 1, lambda k: mean_w[:], lambda k: ssum)
                elif kind == "if":
                    pe.wait_ge(S["wif_in"], 32)
                    product(n, KD, lambda k: wif[:, k, :], lambda k: hT[:, k, :],
                            lambda k: pe.wait_ge(S["h_ready"], k + 1))
                elif kind in ("mk", "mq", "mv", "dk", "dv", "dq", "mo", "sc", "sx", "sb"):
                    w = slot(item, KD)
                    product(n, KD, lambda k: w[:, k, P * a[0]:P * a[0] + P], lambda k: hT[:, k, :])
                elif kind == "gt":
                    w, j = slot(item, KD), a[1] % 4
                    product(n, KD, lambda k: w[:, k, P * j:P * j + P], lambda k: hT[:, k, :])
                elif kind == "pr":
                    br, j = a
                    w, y = slot(item, 4), (mqT, scb, dqT)[br]
                    if j == 0:
                        if br == 0:
                            pe.wait_ge(S["ya_ready"], 4)
                        elif br == 1:
                            wait_drained(pe, block_of[("sb", 3)])
                        else:
                            pe.wait_ge(S["at_yc"], 17)
                    product(n, 4, lambda k: w[:, k, P * j:P * j + P], lambda k: y[:, k, :])
                elif kind == "wo":
                    w, j = slot(item, KD), a[0] % 4
                    product(n, KD, lambda k: w[:, k, P * j:P * j + P], lambda k: merged[:, k, :],
                            (lambda k: pe.wait_ge(S["merged_added"], KD + k + 1)) if a[0] == 0 else None)
                elif kind == "up":
                    w, j, part = slot(item, 2 * KD), a[0], a[1]
                    product(n, KD, lambda k: w[:, KD * part + k, P * (j % 2):P * (j % 2) + P], lambda k: hT[:, k, :],
                            (lambda k: pe.wait_ge(S["h_ready"], KD + k + 1)) if (j, part) == (0, 0) else None)
                elif kind == "dn":
                    w = ring[:, slot_of(item), 0:JF * P].rearrange("p (k f) -> p k f", k=JF)
                    product(n, JF, lambda k: w[:, k, :], lambda k: gff[:, k, :],
                            (lambda k: pe.wait_ge(S["g_ready"], k + 1)) if a[0] == 0 else None)
                elif kind == "tok":
                    name, j = a[0]
                    src = src_tok(name, j)
                    wait_drained(pe, block_of[(name, j)])
                    for c in range(4):
                        t.transpose(D[:, b, P * c:P * c + P], src[:, P * c:P * c + P], ident[:])
                    t.transpose(D[0:TS, b + 1, 0:P], src[:, S0:T], ident[:]).then_inc(S["dense_done"], 1)
                elif kind == "gtr":
                    pe.wait_ge(S["rows_act"], 2)
                    for s, nm in enumerate(("g", "em")):
                        for c, (col, L) in enumerate(TILES):
                            last = t.transpose(D[0:L, b + s, H * c:H * c + H], row[nm][:, col:col + L], ident[0:H, 0:H])
                    last.then_inc(S["dense_done"], 1)
                elif kind == "ml":
                    stage, c = a
                    col, L = TILES[c]
                    C = C_p if c < 4 else C_s
                    hs = range(H)
                    if stage == 0:
                        if c == 0:
                            wait_drained(pe, block_of[("mq", 3)])
                        else:
                            pe.wait_ge(S["ml_hm"], c)
                            pe.wait_ge(S["ml_c"], c)
                        lw = X[0:L, 0, :].rearrange("p (h t) -> p h t", h=H)[:, :, 0:L]
                        t.matmul(lw, ident[0:L, 0:L], causal[0:L, 0:L].unsqueeze(1).to_broadcast([L, H, L]),
                                 start=True, stop=False, skip_group_check=True)
                        for h in hs:
                            t.matmul(X[0:L, 0, P * h:P * h + L], sel[0:H, h, 0:L], row["u"][:, col:col + L],
                                     start=False, stop=h == H - 1, skip_group_check=True)
                        for h in hs:
                            t.matmul(X[0:L, 1, P * h:P * h + L], mkT[:, h, col:col + L], mqT[:, h, col:col + L],
                                     start=True, stop=True)
                        for h in hs:
                            last = t.matmul(X[:, 2, P * h:P * h + L], sel[0:H, h, :], row["inter"][:, col:col + L],
                                            start=True, stop=True)
                        last.then_inc(S["ml_scores"], 1)
                    elif stage == 1:
                        pe.wait_ge(S["ml_pt"], c + 1)
                        pe.wait_ge(S["ml_qi"], c + 1)
                        pe.wait_ge(S["ml_kw"], c + 1)
                        if c == 0:
                            wait_drained(pe, block_of[("tok", ("mv", 3))])
                        for h in hs:
                            o = X[0:L, h // 2, 129 * (h % 2):129 * (h % 2) + 129]
                            t.matmul(o, qi[:, h, 0:L], C[:, h, :], start=True, stop=False)
                            t.matmul(o, p_ml[0:L, h, 0:L], mv_tok[0:L, c, h, :], start=False, stop=True)
                        for h in hs:
                            last = t.matmul(X[:, 2 + h // 2, 129 * (h % 2):129 * (h % 2) + 129], kw[0:L, h, :],
                                            mv_tok[0:L, c, h, :], start=True, stop=True)
                        last.then_inc(S["ml_num"], 1)
                    else:
                        pe.wait_ge(S["ml_hn"], c + 1)
                        for h in hs:
                            last = t.transpose(X[:, 0, P * h:P * h + L], hn[0:L, h, :], ident[0:L, 0:L])
                        last.then_inc(S["ml_ht"], 1)
                elif kind == "ck":
                    arrived("ck")
                    if a[0] == 0:
                        pe.wait_ge(S["ml_hm"], 5)
                        pe.wait_ge(S["ml_c"], 5)
                    else:
                        pe.wait_ge(S["ck_dve"], 1)
                        pe.wait_ge(S["ck_act"], 1)
                    ck = slot("ck", 8)
                    for hh in range(2):
                        for kb in range(8):
                            h = 2 * a[0] + hh
                            last = t.transpose(X[:, 2 * hh + kb // 4, P * (kb % 4):P * (kb % 4) + P],
                                               ck[:, kb, P * h:P * h + P], ident[:])
                    last.then_inc(S["ck_tr"], 1)
                elif kind == "sample":
                    c = a[0]
                    if c == 0:
                        pe.wait_ge(S["ck_dve"], 2)
                        pe.wait_ge(S["ck_act"], 2)
                        wait_drained(pe, block_of[("dq", 3)])
                    else:
                        pe.wait_ge(S["at_exp"], 1)
                    d = slice(64 * c, 64 * c + 64)
                    for h in range(H):
                        q = dqT[d, h, S0:T]
                        for kb in range(2):
                            t.matmul(X[TS * h:TS * h + TS, kb, :], q, ckT[d, h, 512 * kb:512 * kb + 512],
                                     start=True, stop=True)
                        last = t.matmul(X[TS * h:TS * h + TS, 2, 0:TS], q, dkT[d, h, S0:T], start=True, stop=True)
                    last.then_inc(S["at_s"], 1)
                elif kind == "at":
                    stage, u = a
                    h, i = (u - 1) // 4, (u - 1) % 4
                    nk = P * (i + 1)
                    if stage == 0:
                        pe.wait_ge(S["at_exp"], u + 1)
                        if u == 1:
                            pe.wait_ge(S["at_wt"], 1)
                        for c in range(2):
                            d = slice(64 * c, 64 * c + 64)
                            t.matmul(X[:, c, 0:nk], dqT[d, h, P * i:P * i + P], dkT[d, h, 0:nk],
                                     start=True, stop=False, skip_group_check=True)
                            last = t.matmul(X[:, c, nk - 64:nk], half_row[:], neg_row[:], start=False, stop=True,
                                            skip_group_check=True)
                        last.then_inc(S["at_s"], 1)
                    elif stage == 1:
                        pe.wait_ge(S["at_wd"], u + 1)
                        if u == 0:
                            for kb in range(8):
                                t.transpose(X[:, kb // 4, P * (kb % 4):P * (kb % 4) + P], prob[:, 0, P * kb:P * kb + P],
                                            ident[:])
                            last = t.transpose(X[0:TS, 2, 0:P], prob[:, 0, PAST:PAST + TS], ident[:])
                        else:
                            pe.wait_ge(S["at_wt"], u)
                            pe.wait_ge(S["at_yc"], max(u - 1, 1))
                            for kb in range(i + 1):
                                last = t.transpose(X[:, 2, P * kb:P * kb + P], prob2[:, u % 2, 0, P * kb:P * kb + P],
                                                   ident[:])
                        last.then_inc(S["at_tr"], 1)
                    elif stage == 2:
                        pe.wait_ge(S["at_wt"], u + 1)
                        if u == 0:
                            arrived("cv")
                            wait_drained(pe, block_of[("tok", ("dv", 3))])
                            cv = slot("cv", 8)
                            for hh in range(H):
                                o = X[TS * hh:TS * hh + TS, 3, 0:P]
                                for kb in range(8):
                                    t.matmul(o, wdT[:, kb, TS * hh:TS * hh + TS], cv[:, kb, P * hh:P * hh + P],
                                             start=kb == 0, stop=False)
                                last = t.matmul(o, wdT[0:TS, 8, TS * hh:TS * hh + TS], dv_tok[0:TS, 4, hh, :],
                                                start=False, stop=True)
                        else:
                            pe.wait_ge(S["at_on"], u)
                            for kb in range(i + 1):
                                last = t.matmul(X[:, 3, 0:P], wdT[:, 4 * (u % 2) + kb, :], dv_tok[:, kb, h, :],
                                                start=kb == 0, stop=kb == i)
                        last.then_inc(S["at_o"], 1)
                    else:
                        pe.wait_ge(S["at_on"], u + 1)
                        pe.wait_ge(S["at_wt"], min(u + 2, 17) if u else 1)
                        t.transpose(X[:, 2, 0:P], on[:, u % 2, :], ident[:]).then_inc(S["at_ot"], 1)
                elif kind == "state":
                    pe.wait_ge(S["hist_ready"], JU)
                    for s in range(2):
                        t.transpose(D[0:2 * JU, b, P * s:P * s + P], ffn_last[:, s].rearrange("p r j -> p (r j)"),
                                    ident[:])
                    t.transpose(D[0:16, b + 1, 0:P], conv_last[:].rearrange("p s r j -> p (s r j)"), ident[:])\
                        .then_inc(S["dense_done"], 1)
                elif kind == "yT":
                    j = a[0]
                    pe.wait_ge(S["h_ready"], 2 * KD + j + 1)
                    for c in range(4):
                        t.transpose(D[:, b, P * c:P * c + P], xT[:, j, P * c:P * c + P], ident[:])
                    t.transpose(D[0:TS, b + 1, 0:P], xT[:, j, S0:T], ident[:]).then_inc(S["dense_done"], 1)


_INS = ["x_prompt", "x_sample", "cache_k", "cache_v", "state_C", "state_n", "state_m", "state_conv", "state_ffn",
        "norm1", "w_in", "b_if", "ml_norm", "w_sc_conv", "da_lambda", "da_norm", "w_branch", "w_out", "norm2",
        "w_up", "w_fconv", "w_down", "norm_f"]
_OUTS = [(1, TP, DM), (1, TS, DM),
         (1, 1, TP, 4, 128), (1, 1, TP, 4, 128), (1, 1, 4, 128, 128), (1, 1, 4, 128), (1, 1, 4), (1, 1, 2, 512),
         (1, 1, 2, 2 * DFF),
         (1, 1, TS, 4, 128), (1, 1, TS, 4, 128), (1, 1, 4, 128, 128), (1, 1, 4, 128), (1, 1, 4), (1, 1, 2, 512),
         (1, 1, 2, 2 * DFF)]


def kernel(**inputs):
    import numpy as _np
    import concourse.bacc as _bacc
    from concourse.bass_utils import run_bass_kernel_spmd as _run

    nc = _bacc.Bacc("TRN2", target_bir_lowering=False, num_devices=1)
    arrays, args = {}, []
    for name in _INS:
        a = _np.ascontiguousarray(inputs[name])
        arrays[f"in_{name}"] = a
        args.append(nc.dram_tensor(f"in_{name}", a.shape, mybir.dt.from_np(a.dtype), kind="ExternalInput").ap())
    for i, shape in enumerate(_OUTS):
        args.append(nc.dram_tensor(f"out_{i}", shape, F32, kind="ExternalOutput").ap())
    streaming_encoder_step(nc, *args)
    r = _run(nc, [arrays], core_ids=[0])
    return tuple(r.results[0][f"out_{i}"] for i in range(len(_OUTS)))
```

```python
import concourse.bass as bass
from concourse import mybir
from contextlib import ExitStack

F32 = mybir.dt.float32
F32R = mybir.dt.float32r
ALU = mybir.AluOpType
ACT = mybir.ActivationFunctionType
AX = mybir.AxisListType

P = 128
DM = 1024
KD = DM // P
TP, TS, PAST = 512, 32, 1024
S0 = TP + 4
T = S0 + TS
HALF = T // 2
TILES = [(0, P), (P, P), (2 * P, P), (3 * P, P), (S0, TS)]
H = 4
BW = 512
DFF = 2816
JF = DFF // P
JU = 2 * JF
EPS = 1e-6
LAM_INIT = 0.2
NEG = -1e30
NRAW, NSPLIT = 2, 3
GROUP = KD * P
W_IN_AT = dict(mq=0, mk=512, mv=1024, mo=1536, sb=2056, sc=2568, sx=3080, dq=3592, dk=4104, dv=4616)
GATES_AT, BRANCH_AT = 2048, 5128
ML_ORDER = (4, 0, 1, 2, 3)

def streaming_encoder_step(nc, x_prompt, x_sample, cache_k, cache_v, state_C, state_n, state_m, state_conv,
                           state_ffn, norm1, w_in, b_if, ml_norm, w_sc_conv, da_lambda, da_norm, w_branch,
                           w_out, norm2, w_up, w_fconv, w_down, norm_f,
                           y_p, y_s, p_k, p_v, p_C, p_n, p_m, p_conv, p_ffn,
                           s_k, s_v, s_C, s_n, s_m, s_conv, s_ffn):
    ORDER, block_of = [], {}

    def add(kind, *a):
        block_of[(kind, *a)] = len(block_of)
        ORDER.append((kind, a, block_of[(kind, *a)]))

    def unit(kind, *a):
        ORDER.append((kind, a, None))

    add("small")
    for j in range(KD):
        add("xT", j)
    add("norm", 0)
    add("if")
    for name, j in [("mk", 0), ("mk", 1), ("tok", ("mk", 0)), ("mk", 2), ("tok", ("mk", 1)), ("mk", 3),
                    ("tok", ("mk", 2)), ("mq", 0), ("tok", ("mk", 3)), ("mq", 1), ("mq", 2), ("mq", 3),
                    ("mv", 0), ("mv", 1), ("tok", ("mv", 0)), ("mv", 2), ("tok", ("mv", 1)), ("mv", 3),
                    ("tok", ("mv", 2)), ("gtr", 0), ("dk", 0), ("tok", ("mv", 3))]:
        add(name, j)
    ml_fill = [[("dk", 1)], [("tok", ("dk", 0)), ("dk", 2)], [("tok", ("dk", 1)), ("dk", 3)],
               [("tok", ("dk", 2)), ("dv", 0)], [("tok", ("dk", 3)), ("dv", 1)], [("tok", ("dv", 0)), ("dv", 2)],
               [("tok", ("dv", 1)), ("dv", 3)], [("tok", ("dv", 2)), ("dq", 0)], [("tok", ("dv", 3)), ("dq", 1)],
               [("dq", 2)]]
    for u in range(5):
        for stage in range(3):
            unit("ml", stage, u)
            if stage < 2:
                for s in ml_fill.pop(0):
                    add(*s)
    add("dq", 3)
    add("sc", 0)
    unit("ck", 0)
    add("sc", 1)
    unit("ck", 1)
    add("sc", 2)
    unit("sample", 0)
    add("sc", 3)
    unit("sample", 1)
    add("mo", 0)
    unit("at", 1, 0)
    add("mo", 1)
    unit("at", 2, 0)
    add("mo", 2)
    unit("at", 3, 0)
    fill = [("mo", 3)] + [(s, 0, j) for j in range(KD) for s in ("gt", "pr")]
    fill += [(s, j) for s in ("sx", "sb") for j in range(4)]
    fill += [(s, 1, j) for j in range(KD) for s in ("gt", "pr")]
    fill += [("gt", 2, j) for j in range(KD)]
    for k in range(1, 20):
        for stage in (3, 0, 1, 2):
            if 1 <= k - stage <= 16:
                unit("at", stage, k - stage)
        add(*fill.pop(0))
        if k > 10:
            add(*fill.pop(0))
    for f in fill:
        add(*f)
    for j in range(KD):
        add("pr", 2, j)
    for j in range(KD):
        add("wo", j)
    add("norm", 1)
    for j in range(0, JF, 2):
        for part in range(2):
            add("up", j, part)
            add("up", j + 1, part)
    add("state")
    for j in range(KD):
        add("dn", j)
    add("norm", 2)
    for j in range(KD):
        add("yT", j)

    up_index = {a: m for m, a in enumerate(a for kind, a, _ in ORDER if kind == "up")}
    j_of, part_of = [a[0] for a in up_index], [a[1] for a in up_index]

    BY_DVE = {"small", "xT", "tok", "gtr", "sx", "sb", "pr", "wo", "dn", "state"}
    drained, count = {}, {"act": 0, "dve": 0}
    for kind, a, n in ORDER:
        if n is not None:
            e = "dve" if kind in BY_DVE else "act"
            count[e] += 1
            drained[n] = (e, count[e])

    def groups_of(kind, a):
        if kind == "if":
            return [(("if",), 0, KD, 0)]
        if kind in W_IN_AT or kind == "wo":
            return [((kind, a[0] // 2), 0, KD, P * (a[0] % 2))]
        if kind == "gt":
            return [(("gt", a[0], a[1] // 2), 0, KD, P * (a[1] % 2))]
        if kind == "pr":
            return [(("pr", a[0], a[1] // 4), 0, 4, P * (a[1] % 4))]
        if kind == "up":
            return [(("up", a[1], a[0] // 2), 0, KD, P * (a[0] % 2))]
        if kind == "dn":
            return [(("dn", a[0], half), k, m, 0) for half in range(2) for k, m in ((0, 6), (6, 5))]
        return []

    GROUPS, ITEMS, first_group, group_used, n_used = [], [], {}, [], 0
    for kind, a, n in ORDER:
        gs = groups_of(kind, a) if n is not None else []
        first_group[n] = len(GROUPS)
        for g in gs:
            if g[0] not in ITEMS:
                ITEMS.append(g[0])
            GROUPS.append(g)
            if g is gs[-1]:
                group_used.append(("dense_done", n + 1))
            else:
                n_used += 1
                group_used.append(("part_used", n_used))
    last_group = {g[0]: i for i, g in enumerate(GROUPS)}
    AHEAD = NSPLIT - 1

    tmp_index, tmp_users = {}, []

    def tmp_user(key, sem_name, value):
        tmp_index[key] = len(tmp_users)
        tmp_users.append((sem_name, value))

    n_yl = 0
    for kind, a, n in ORDER:
        if kind in ("xT", "wo", "dn"):
            r = {"xT": 0, "wo": 1, "dn": 2}[kind]
            tmp_user(("sq", r, a[0]), "sq_added", KD * r + a[0] + 1)
        elif kind == "norm" and a[0] < 2:
            for j in range(KD):
                tmp_user(("norm", a[0], j), ("hl_dve", "hl_pool")[j % 2], KD // 2 * a[0] + j // 2 + 1)
        elif kind in ("mo", "sb"):
            n_yl += 1
            tmp_user((kind, a[0]), "y_split", n_yl)
        elif kind == "gt" and a[0] == 0:
            tmp_user(("gt", 0, a[1]), "dve_drained", drained[block_of[("pr", 0, a[1])]][1])
        elif kind == "gt" and a[0] == 1:
            tmp_user(("gt", 1, a[1]), "merged_added", a[1] + 1)
        elif kind == "pr" and a[0] == 2:
            tmp_user(("pr", 2, a[1]), "merged_split", a[1] + 1)
        elif kind == "up" and a[1] == 1:
            tmp_user(("up", a[0]), "silu_done", a[0] + 1)

    ctx = ExitStack()
    with ctx:
        def sem(name):
            return ctx.enter_context(nc.semaphore(name))

        def up32(n):
            return (n + 31) // 32 * 32

        top = [up32(nc.sbuf_base)]

        def place(name, shape, at=None, dt=F32):
            size = 4
            for n in shape[1:]:
                size *= n
            here = top[0] if at is None else at
            if at is None:
                top[0] += up32(size)
                assert top[0] <= nc.sbuf_top, top[0] - nc.sbuf_top
            return nc.alloc_sbuf_tensor_at(name, shape, dt, offset=here)

        def span(floats):
            at = top[0]
            top[0] += up32(4 * floats)
            return at

        D = ctx.enter_context(nc.psum_tensor("D", [P, 4, 512], F32))
        X = ctx.enter_context(nc.psum_tensor("X", [P, 4, 512], F32))
        raw = place("raw", [P, NRAW, 2 * GROUP])
        w_h = place("w_h", [P, NSPLIT, GROUP], dt=F32R)
        w_l = place("w_l", [P, NSPLIT, GROUP], dt=F32R)
        xT = place("xT", [P, KD, T])
        H_AT = span(2 * KD * T)
        h_h = place("h_h", [P, KD, T], H_AT, F32R)
        h_l = place("h_l", [P, KD, T], H_AT + 4 * KD * T, F32R)
        tmp = place("tmp", [P, 2, T])
        ident = place("ident", [P, P])
        mean_w = place("mean_w", [P, P])
        causal = place("causal", [P, P])
        vec = place("vec", [P, 49])
        hist = place("hist", [P, 2, JU])
        fcw = place("fcw", [P, 3, JU])
        conv_last = place("conv_last", [P, 2, 2, 4])
        b_i, b_f, m_s = place("b_i", [H, 1]), place("b_f", [H, 1]), place("m_s", [H, 1])
        neg_lam = place("neg_lam", [P, 1])
        lam_e = place("lam_e", [P, 2])
        m_half = place("m_half", [P, 1])
        eps = place("eps", [P, 1])
        il = place("il", [P, H])
        gT = place("gT", [P, 5, H])
        emT = place("emT", [P, 5, H])
        den, rden, ssq, rr = (place(x, [P, H]) for x in ("den", "rden", "ssq", "rr"))
        nmax = place("nmax", [P, 2, 2])
        psum_p = place("psum_p", [P, 2, 2])
        rsum = place("rsum", [P, 4, 2])
        kap = place("kap", [P, 1])
        assq, arr = place("assq", [P, 2]), place("arr", [P, 2])

        M_AT, G_AT, K_AT = span(KD * T), span(KD * T), span(7360)
        Q_AT, DQ_AT, DK_AT, DV_AT, WORK_AT = span(4 * T), span(4 * T), span(4 * T), span(2560), span(2564)
        assert top[0] <= nc.sbuf_top, top[0] - nc.sbuf_top
        END_AT = top[0]
        small_a = place("small_a", [49, P], M_AT)
        small_b = place("small_b", [2 * JU, P], M_AT + 512)
        small_c = place("small_c", [66, 2, P], M_AT + 1024)
        lam_t = place("lam_t", [P, 2, 2, 64], M_AT + 2048)
        lam_p = place("lam_p", [P, 2, 64], M_AT + 3072)
        x_t = place("x_t", [P, 4, DM], K_AT)
        x_s = place("x_s", [TS, DM], G_AT)
        ssum_at = {0: DK_AT, 1: DK_AT, 2: H_AT}
        ssum = [place(f"ssum{r}", [P, T], ssum_at[r]) for r in range(3)]
        rstd = [place(f"rstd{r}", [P, T], ssum_at[r] + up32(4 * T)) for r in range(3)]
        f_tmp = place("f_tmp", [P, 2, T], M_AT)
        k_out = place("k_out", [P, 5, 512], M_AT + 8 * T)
        sel = place("sel", [H, H, P], M_AT + 8 * T + 4 * 2560)
        rows_t = place("rows", [H, 8, T], G_AT)
        row = {nm: rows_t[:, i, :] for i, nm in enumerate(("lf", "ig", "cum", "m", "u", "g", "inter", "em"))}
        mkT = place("mkT", [P, 4, T], K_AT)
        mk_tok = place("mk_tok", [P, 5, H, P], K_AT + 16 * T)
        mv_tok = place("mv_tok", [P, 5, H, P + 1], K_AT + 16 * T + 4 * 2560)
        mqT = place("mqT", [P, 4, T], Q_AT)
        dqT = place("dqT", [P, 4, T], DQ_AT)
        dkT = place("dkT", [P, 4, T], DK_AT)
        dv_tok = place("dv_tok", [P, 5, H, P], DV_AT)
        w_ml = place("w_ml", [P, H, P], WORK_AT)
        p_ml = place("p_ml", [P, H, P], WORK_AT + 2048)
        kw = place("kw", [P, H, P], WORK_AT + 4096)
        qi = place("qi", [P, H, P], WORK_AT + 6144)
        hn = qi
        C_p = place("C_p", [P, H, P + 1], WORK_AT + 8192)
        C_s = place("C_s", [P, H, P + 1], DQ_AT)
        ck = place("ck", [P, 8, 512], G_AT)
        cv = place("cv", [P, 8, 512], M_AT)
        ckT = place("ckT", [P, H, PAST], K_AT)
        prob = place("prob", [P, 2, 1056], K_AT + 16384)
        prob2 = place("prob2", [P, 2, 2, 512], K_AT + 16384)
        wdT = place("wdT", [P, 9, P], K_AT + 16384 + 8448)
        u_c = place("u_c", [P, 2, T + 2], K_AT)
        yc_l = place("yc_l", [P, 4, T], K_AT + up32(8 * (T + 2)), F32R)
        A_AT = K_AT + up32(8 * (T + 2)) + 16 * T
        on = place("on", [P, 2, P], A_AT)
        y_tmp = place("y_tmp", [P, 2, P], A_AT + 1024)
        junk = place("junk", [P, P], A_AT + 2048)
        assert A_AT + 2560 <= K_AT + 16384
        scb = place("scb", [P, 4, T], WORK_AT)
        ya_h, ya_l = place("ya_h", [P, 4, T], Q_AT, F32R), place("ya_l", [P, 4, T], G_AT, F32R)
        yb_h, yb_l = place("yb_h", [P, 4, T], WORK_AT, F32R), place("yb_l", [P, 4, T], G_AT + 16 * T, F32R)
        yc_h = place("yc_h", [P, 4, T], DQ_AT, F32R)
        merged = place("merged", [P, KD, T], M_AT)
        gate2 = place("gate2", [P, KD, T], G_AT)
        mg_h, mg_l = place("mg_h", [P, KD, T], M_AT, F32R), place("mg_l", [P, KD, T], G_AT, F32R)
        g_h = place("g_h", [P, JF, T], M_AT, F32R)
        g_l = place("g_l", [P, JF, T], M_AT + 4 * JF * T, F32R)
        FF_AT = M_AT + 8 * JF * T
        ups = place("ups", [P, 2, T + 2], FF_AT)
        acc = place("acc", [P, 2, 2, T], FF_AT + up32(8 * (T + 2)))
        ffn_last = place("ffn_last", [P, 2, 2, JU], FF_AT + up32(8 * (T + 2)) + 16 * T)
        assert FF_AT + up32(8 * (T + 2)) + 16 * T + 16 * JU <= END_AT
        Y_AT = H_AT + 2 * up32(4 * T)
        fst = place("fst", [P, 2, P], Y_AT)
        cst = place("cst", [16, P], Y_AT + 1024)
        yst = place("yst", [P, 4, DM], Y_AT + 1536)
        yst_s = place("yst_s", [TS, DM], Y_AT + 1536 + 16 * DM)
        assert Y_AT + 1536 + 20 * DM <= H_AT + 8 * KD * T

        sems = {}
        for nm in ("dense_done act_drained dve_drained small_in xs_in const_ready wif_zeroed wif_in h_ready sq_done "
                   "sq_added rstd_ready rows_act rows_dve ml_scores ml_w ml_qi ml_pt ml_kw ml_num ml_c ml_rd ml_ssq "
                   "ml_rr ml_hn ml_ht ml_hm hl_dve hl_pool hn_dve hh_act wh_ready wl_ready part_used x_in ck_in cv_in y_v y_h y_split yc_split "
                   "merged_v merged_h merged_split silu_done gh_ready gl_ready conv_done ck_tr ck_dve ck_act at_s at_mx at_exp at_wd at_tr at_wt at_o at_sq at_rr "
                   "at_on at_ot at_yc th_ready u_ready conv_kept merged_added hist_ready g_ready "
                   "lam_dve lam_act state_out y_out y_ready dve_chain act_chain pool_chain cst_ready yc_spare out_k out_v out_m out_C").split():
            sems[nm] = sem(nm)
        raw_in = [sem(f"raw_in{i}") for i in range(NRAW)]
        S = sems

        def wait_drained(eng, n):
            e, v = drained[n]
            eng.wait_ge(S[e + "_drained"], v)

        def wait_tmp_free(eng, k):
            if k >= 2:
                name, v = tmp_users[k - 2]
                eng.wait_ge(S[name], v)

        def dbuf(n):
            return D[:, 2 * (n % 2):2 * (n % 2) + 2, 0:HALF]

        def two(ap):
            return ap.rearrange("p (a b) -> p a b", a=2)

        def src_tok(name, j):
            return {"mk": mkT[:, j, :], "mv": f_tmp[:, j % 2, :], "dk": dkT[:, j, :], "dv": f_tmp[:, j % 2, :]}[name]

        def raw_view(g):
            item, k0, m, c0 = GROUPS[g]
            slot = raw[:, ITEMS.index(item) % NRAW, :]
            if item[0] == "if":
                return slot[:, 0:KD * 2 * H].rearrange("p (k f) -> p k f", k=KD)
            width = {"pr": 512, "dn": P}.get(item[0], 256)
            kc = {"pr": 4, "dn": 11}.get(item[0], KD)
            return slot[:, 0:kc * width].rearrange("p (k f) -> p k f", k=kc)[:, k0:k0 + m, c0:c0 + P]

        def split_view(w, g):
            m, f = GROUPS[g][2], 36 if GROUPS[g][0][0] == "if" else P
            return w[:, g % NSPLIT, 0:m * f].rearrange("p (k f) -> p k f", k=m)

        def wait_raw(eng, g):
            i = ITEMS.index(GROUPS[g][0])
            eng.wait_ge(raw_in[i % NRAW], 16 * (i // NRAW + 1))

        def wait_split_slot(eng, g):
            if g >= NSPLIT:
                name, v = group_used[g - NSPLIT]
                eng.wait_ge(S[name], v)

        def splits(n):
            return range(first_group[n] + AHEAD, first_group.get(n + 1, len(GROUPS)) + AHEAD)

        block = ctx.enter_context(nc.Block())

        @block.sync
        def _(sp):
            for q in range(2):
                sp.dma_start(x_t[:, 2 * q:2 * q + 2, :],
                             x_prompt[0].rearrange("(c p) f -> p c f", p=P)[:, 2 * q:2 * q + 2, :])\
                    .then_inc(S["x_in"], 16)
            for i, item in enumerate(ITEMS):
                if i >= NRAW:
                    v = last_group[ITEMS[i - NRAW]] + 1
                    sp.wait_ge(S["wh_ready"], v)
                    sp.wait_ge(S["wl_ready"], v)
                kind = item[0]
                rows, width = slice(0, DM), 256
                if kind == "if":
                    src, at, width = w_in[0], GATES_AT, 2 * H
                elif kind in W_IN_AT:
                    src, at = w_in[0], W_IN_AT[kind] + 256 * item[1]
                elif kind == "gt":
                    src, at = w_in[0], BRANCH_AT + DM * item[1] + 256 * item[2]
                elif kind == "pr":
                    src, at, width, rows = w_branch[0, item[1]], 512 * item[2], 512, slice(0, BW)
                elif kind == "wo":
                    src, at = w_out[0], 256 * item[1]
                elif kind == "up":
                    src, at = w_up[0], DFF * item[1] + 256 * item[2]
                else:
                    src, at, width, rows = w_down[0], P * item[1], P, slice(11 * P * item[2], 11 * P * (item[2] + 1))
                k = (rows.stop - rows.start) // P
                sp.dma_start(raw[:, i % NRAW, 0:k * width].rearrange("p (k f) -> p k f", k=k),
                             src[rows, at:at + width].rearrange("(k p) f -> p k f", p=P))\
                    .then_inc(raw_in[i % NRAW], 16)
            for q in range(4):
                e, v = drained[block_of[("yT", 2 * q + 1)]]
                sp.wait_ge(S[e + "_drained"], v)
                f = slice(256 * q, 256 * q + 256)
                sp.dma_start(y_p[0].rearrange("(c p) f -> p c f", p=P)[:, :, f], yst[:, :, f]).then_inc(S["y_out"], 16)
                sp.dma_start(y_s[0][:, f], yst_s[0:TS, f]).then_inc(S["y_out"], 16)
            sp.wait_ge(S["y_out"], 8 * 16)
            sp.wait_ge(S["out_k"], 32)
            sp.wait_ge(S["out_v"], 32)
            sp.wait_ge(S["out_m"], 32)
            sp.wait_ge(S["out_C"], 64)
            sp.wait_ge(S["state_out"], 64)

        @block.gpsimd
        def _(pool):
            g = nc.gpsimd
            chain = [0]

            def link(ins):
                chain[0] += 1
                ins.then_inc(S["pool_chain"], 1)
                pool.wait_ge(S["pool_chain"], chain[0])

            link(g.memset(ident[:], 0.0))
            g.affine_select(out=ident[:], in_=ident[:], compare_op=ALU.not_equal, fill=1.0, base=0,
                            pattern=[[-1, P]], channel_multiplier=1).then_inc(S["const_ready"], 1)
            g.memset(mean_w[:], 1.0 / DM).then_inc(S["const_ready"], 1)
            g.memset(xT[:, :, TP:S0], 0.0).then_inc(S["const_ready"], 1)
            link(g.memset(causal[:], 0.0))
            g.affine_select(out=causal[:], in_=causal[:], compare_op=ALU.is_ge, fill=NEG, base=0,
                            pattern=[[1, P]], channel_multiplier=-1).then_inc(S["const_ready"], 1)
            g.memset(eps[:], EPS).then_inc(S["const_ready"], 1)
            g.memset(m_half[:], -0.5).then_inc(S["const_ready"], 1)
            g.memset(C_p[:], 0.0).then_inc(S["const_ready"], 1)
            link(g.memset(sel[0:H], 0.0))
            g.affine_select(out=sel[0:H], in_=sel[0:H], compare_op=ALU.not_equal, fill=1.0, base=0,
                            pattern=[[-1, H], [0, P]], channel_multiplier=1).then_inc(S["const_ready"], 1)

            def rstd_small(x, scale, out, done):
                link(g.tensor_scalar(x, x, 1.0 / P, EPS, ALU.mult, ALU.add))
                link(g.tensor_tensor(x, x, m_half[0:x.shape[0], 0:1].to_broadcast(list(x.shape)), ALU.pow))
                g.tensor_tensor(out, x, scale, ALU.mult).then_inc(S[done], 1)

            def low_g(j):
                pool.wait_ge(S["gh_ready"], j + 1)
                g.tensor_tensor(g_l[:, j, :], acc[:, 0, j % 2, :], g_h[:, j, :].bitcast(F32), ALU.subtract)\
                    .then_inc(S["gl_ready"], 1)

            for kind, a, n in ORDER:
                if kind in ("xT", "wo", "dn"):
                    r = {"xT": 0, "wo": 1, "dn": 2}[kind]
                    k = tmp_index[("sq", r, a[0])]
                    pool.wait_ge(S["sq_done"], KD * r + a[0] + 1)
                    if a[0] == 0:
                        g.tensor_copy(ssum[r][:], tmp[:, k % 2, :]).then_inc(S["sq_added"], 1)
                    else:
                        pool.wait_ge(S["sq_added"], KD * r + a[0])
                        g.tensor_tensor(ssum[r][:], ssum[r][:], tmp[:, k % 2, :], ALU.add).then_inc(S["sq_added"], 1)
                    if kind == "xT" and a[0] == KD - 1:
                        g.memset(mv_tok[:, :, :, P:P + 1], 1.0).then_inc(S["const_ready"], 1)
                elif kind == "ml" and a[0] == 0:
                    u, c = a[1], ML_ORDER[a[1]]
                    L = TILES[c][1]
                    pool.wait_ge(S["ml_w"], u + 1)
                    if u >= 1:
                        pool.wait_ge(S["ml_num"], u)
                    wait_drained(pool, block_of[("tok", ("mk", 3))])
                    g.tensor_tensor(kw[0:L], mk_tok[0:L, c], w_ml[0:L, :, L - 1:L].to_broadcast([L, H, P]),
                                    ALU.mult).then_inc(S["ml_kw"], 1)
                elif kind == "ml" and a[0] == 1:
                    u, c = a[1], ML_ORDER[a[1]]
                    L = TILES[c][1]
                    pool.wait_ge(S["ml_ssq"], u + 1)
                    rstd_small(ssq[0:L, :], rden[0:L, :], rr[0:L, :], "ml_rr")
                    if c >= 3:
                        pool.wait_ge(S["ml_c"], u + 1)
                        Cn, oC, on_ = (C_p, p_C, p_n) if c == 3 else (C_s, s_C, s_n)
                        pool.dma_start(oC[0, 0].rearrange("h d e -> d h e"), Cn[:, :, 0:P]).then_inc(S["out_C"], 16)
                        pool.dma_start(on_[0, 0].rearrange("h d -> d h").unsqueeze(2), Cn[:, :, P:P + 1],
                                       allow_slow_non_contiguous=True)\
                            .then_inc(S["out_C"], 16)
                elif kind == "tok" and a[0] in (("dk", 3), ("dv", 3)):
                    wait_drained(pool, n)
                    tok, op, os, so = (k_out, p_k, s_k, "out_k") if a[0][0] == "dk" else \
                        (dv_tok[:].rearrange("p c h d -> p c (h d)"), p_v, s_v, "out_v")
                    pool.dma_start(op[0, 0].rearrange("(c p) h d -> p c (h d)", p=P), tok[:, 0:4, :])\
                        .then_inc(S[so], 16)
                    pool.dma_start(os[0, 0].rearrange("t h d -> t (h d)"), tok[0:TS, 4, :]).then_inc(S[so], 16)
                elif kind == "gtr":
                    pool.wait_ge(S["rows_dve"], 6)
                    pool.dma_start(p_m[0, 0].unsqueeze(1), row["m"][:, TP - 1:TP],
                                   allow_slow_non_contiguous=True).then_inc(S["out_m"], 16)
                    pool.dma_start(s_m[0, 0].unsqueeze(1), row["m"][:, T - 1:T],
                                   allow_slow_non_contiguous=True).then_inc(S["out_m"], 16)
                elif kind == "sx":
                    j = a[0]
                    pool.wait_ge(S["u_ready"], j + 1)
                    g.tensor_copy(conv_last[:, 0, :, j], u_c[:, j % 2, TP:TP + 2])
                    g.tensor_copy(conv_last[:, 1, :, j], u_c[:, j % 2, T:T + 2]).then_inc(S["conv_kept"], 1)
                elif kind in ("mo", "sb"):
                    k, j = tmp_index[(kind, a[0])], a[0]
                    yh, yl = (ya_h, ya_l) if kind == "mo" else (yb_h, yb_l)
                    pool.wait_ge(S["y_h"], tmp_users[k][1])
                    g.tensor_tensor(yl[:, j, :], tmp[:, k % 2, :], yh[:, j, :].bitcast(F32), ALU.subtract)\
                        .then_inc(S["y_split"], 1)
                elif kind == "pr" and a[0] == 2:
                    k, j = tmp_index[("pr", 2, a[1])], a[1]
                    pool.wait_ge(S["merged_h"], j + 1)
                    g.tensor_tensor(mg_l[:, j, :], tmp[:, k % 2, :], mg_h[:, j, :].bitcast(F32), ALU.subtract)\
                        .then_inc(S["merged_split"], 1)
                elif kind == "at" and a[0] == 2:
                    u = a[1]
                    pool.wait_ge(S["at_sq"], u + 1)
                    rstd_small(assq[:, u % 2:u % 2 + 1], rsum[:, u % 4, 0:1], arr[:, u % 2:u % 2 + 1], "at_rr")
                elif kind == "at" and a[0] == 3:
                    u = a[1]
                    h, i = (u - 1) // 4, (u - 1) % 4
                    pool.wait_ge(S["at_yc"], u + 1)
                    if u == 0:
                        src = y_tmp[:, 0, :].rearrange("p (h t) -> p h t", h=H)
                        yh, yl = yc_h[:, :, S0:T], yc_l[:, :, S0:T]
                    else:
                        src = y_tmp[:, u % 2, :]
                        yh, yl = (y[:, h, P * i:P * i + P] for y in (yc_h, yc_l))
                    link(g.tensor_copy(yh, src))
                    g.tensor_tensor(yl, src, yh.bitcast(F32), ALU.subtract).then_inc(S["yc_split"], 1)
                elif kind == "at" and a[0] == 0 and a[1] == 1:
                    for y in (yc_h, yc_l):
                        last = g.memset(y[:, :, TP:S0].bitcast(F32), 0.0)
                    last.then_inc(S["yc_spare"], 1)
                elif kind == "norm" and a[0] < 2:
                    r = a[0]
                    if r == 1:
                        pool.wait_ge(S["rstd_ready"], 2)
                        g.memset(ups[:, :, 0:2], 0.0).then_inc(S["conv_kept"], 1)
                    for j in range(1, KD, 2):
                        k = tmp_index[("norm", r, j)]
                        pool.wait_ge(S["hh_act"], KD * r + j + 1)
                        g.tensor_tensor(h_l[:, j, :], tmp[:, k % 2, :], h_h[:, j, :].bitcast(F32), ALU.subtract)\
                            .then_inc(S["hl_pool"], 1)
                elif kind == "up":
                    j, part = a
                    jj = j + JF * part
                    m = up_index[a]
                    buf = ups[:, m % 2, :]
                    wait_drained(pool, n)
                    if m >= 1 and part_of[m - 1] == 1:
                        low_g(j_of[m - 1])
                    g.tensor_copy(buf[:, S0:S0 + 2], hist[:, :, jj])
                    g.tensor_copy(ffn_last[:, 0, :, jj], buf[:, TP:TP + 2])
                    g.tensor_copy(ffn_last[:, 1, :, jj], buf[:, T:T + 2]).then_inc(S["hist_ready"], 1)
                elif kind == "state":
                    low_g(JF - 1)
                    pool.wait_ge(S["cst_ready"], 2)
                    pool.dma_start(p_ffn[0, 0].rearrange("r (j f) -> (r j) f", f=P), fst[0:2 * JU, 0, :])\
                        .then_inc(S["state_out"], 16)
                    pool.dma_start(s_ffn[0, 0].rearrange("r (j f) -> (r j) f", f=P), fst[0:2 * JU, 1, :])\
                        .then_inc(S["state_out"], 16)
                    pool.dma_start(p_conv[0, 0].rearrange("r (j f) -> (r j) f", f=P), cst[0:8, :])\
                        .then_inc(S["state_out"], 16)
                    pool.dma_start(s_conv[0, 0].rearrange("r (j f) -> (r j) f", f=P), cst[8:16, :])\
                        .then_inc(S["state_out"], 16)

        @block.scalar
        def _(act):
            sc = nc.scalar
            chain = [0]

            def link(ins):
                chain[0] += 1
                ins.then_inc(S["act_chain"], 1)
                act.wait_ge(S["act_chain"], chain[0])

            def small(dst, src):
                act.dma_start(dst, src, allow_slow_non_contiguous=True).then_inc(S["small_in"], 16)

            act.dma_start(x_s[0:TS, :], x_sample[0]).then_inc(S["xs_in"], 16)
            rows = lambda ap: ap.rearrange("(j f) -> j f", f=P)
            small(small_a[0:8, :], rows(norm1[0]))
            small(small_a[8:16, :], rows(norm2[0]))
            small(small_a[16:24, :], rows(norm_f))
            small(small_a[24:36, :], w_sc_conv[0].rearrange("t (j f) -> (t j) f", f=P))
            small(small_a[36:44, :], state_conv[0, 0].rearrange("t (j f) -> (t j) f", f=P))
            small(small_a[44:48, :], ml_norm[0])
            small(small_a[48:49, :], da_norm)
            small(small_b[0:2 * JU, :], state_ffn[0, 0].rearrange("t (j f) -> (t j) f", f=P))
            fc = w_fconv[0].rearrange("t (j f) -> (t j) f", f=P)
            small(small_c[0:66, 0, :], fc[0:66, :])
            small(small_c[0:66, 1, :], fc[66:132, :])
            small(b_i[:], b_if[0, 0].unsqueeze(1))
            small(b_f[:], b_if[0, 1].unsqueeze(1))
            small(m_s[:], state_m[0, 0].unsqueeze(1))
            small(lam_t[:], da_lambda[0].rearrange("(a b) f -> a b f", a=2).unsqueeze(0).to_broadcast([P, 2, 2, 64]))
            small(C_s[:, :, 0:P], state_C[0, 0].rearrange("h d e -> d h e"))
            small(C_s[:, :, P:P + 1], state_n[0, 0].rearrange("h d -> d h").unsqueeze(2))

            def split(g):
                wait_raw(act, g)
                wait_split_slot(act, g)
                src, dst = raw_view(g), split_view(w_h, g)
                if GROUPS[g][0][0] == "if":
                    sc.activation(dst[:, :, 0:H], src[:, :, 0:H], ACT.Copy)
                    sc.activation(dst[:, :, 32:36], src[:, :, H:2 * H], ACT.Copy).then_inc(S["wh_ready"], 1)
                else:
                    sc.activation(dst, src, ACT.Copy).then_inc(S["wh_ready"], 1)

            def high_g(j):
                act.wait_ge(S["g_ready"], j + 1)
                sc.activation(g_h[:, j, :], acc[:, 0, j % 2, :], ACT.Copy).then_inc(S["gh_ready"], 1)

            for g in range(AHEAD):
                split(g)
            act.wait_ge(S["lam_dve"], 2)
            sc.activation(lam_e[:], lam_e[:], ACT.Exp).then_inc(S["lam_act"], 1)

            def square_block(r, j, n):
                k = tmp_index[("sq", r, j)]
                wait_drained(act, n)
                wait_tmp_free(act, k)
                sc.activation(tmp[:, k % 2, :], xT[:, j, :], ACT.Square).then_inc(S["sq_done"], 1)

            for kind, a, n in ORDER:
                if n is not None:
                    for g in splits(n):
                        if g < len(GROUPS):
                            split(g)
                if kind in ("xT", "wo", "dn"):
                    if kind == "xT" and a[0] == 0:
                        act.wait_ge(S["const_ready"], 8)
                    square_block({"xT": 0, "wo": 1, "dn": 2}[kind], a[0], n)
                elif kind == "norm":
                    r = a[0]
                    act.wait_ge(S["dense_done"], n + 1)
                    sc.activation(two(rstd[r][:]), dbuf(n), ACT.Ln, bias=eps[:]).then_inc(S["act_drained"], 1)
                    act.wait_ge(S["act_drained"], drained[n][1])
                    sc.activation(rstd[r][:], rstd[r][:], ACT.Exp, scale=-0.5).then_inc(S["rstd_ready"], 1)
                    for j in range(KD if r < 2 else 0):
                        k = tmp_index[("norm", r, j)]
                        act.wait_ge(S["hn_dve"], KD * r + j + 1)
                        sc.activation(h_h[:, j, :], tmp[:, k % 2, :], ACT.Copy).then_inc(S["hh_act"], 1)
                elif kind == "if":
                    act.wait_ge(S["dense_done"], n + 1)
                    act.wait_ge(S["small_in"], 16 * 16)
                    sc.activation(two(row["ig"]), dbuf(n)[0:H], ACT.Identity, bias=b_i[:])
                    sc.activation(two(row["lf"]), dbuf(n)[32:32 + H], ACT.Copy).then_inc(S["act_drained"], 1)
                    act.wait_ge(S["rows_dve"], 1)
                    link(sc.activation(row["g"], row["lf"], ACT.Abs))
                    link(sc.activation(row["g"], row["g"], ACT.Exp, scale=-1.0))
                    sc.activation(row["g"], row["g"], ACT.Ln, bias=1.0).then_inc(S["rows_act"], 1)
                    act.wait_ge(S["rows_dve"], 7)
                    sc.activation(row["em"], row["m"], ACT.Exp, scale=-1.0)
                    sc.activation(row["inter"][:, 0:P], row["u"][:, 0:P], ACT.Exp)
                    for col, L in TILES[1:4]:
                        sc.activation(row["inter"][:, col:col + L], row["u"][:, col:col + L], ACT.Exp,
                                      bias=row["m"][:, col - 1:col])
                    sc.activation(row["inter"][:, S0:T], row["u"][:, S0:T], ACT.Exp, bias=m_s[:])\
                        .then_inc(S["rows_act"], 1)
                elif kind in ("mk", "mq", "mv", "dk", "dv", "dq", "sc"):
                    j = a[0]
                    act.wait_ge(S["dense_done"], n + 1)
                    if kind in ("mv", "dv"):
                        if (kind, j) == ("mv", 0):
                            wait_drained(act, block_of[("small",)])
                            act.wait_ge(S["lam_dve"], 3)
                        elif j >= 2:
                            act.wait_ge(S["dense_done"], block_of[("tok", (kind, j - 2))] + 1)
                    if (kind, j) in (("dq", 0), ("sc", 0)):
                        act.wait_ge(S["out_C"], 32 if kind == "dq" else 64)
                    dst = {"mk": mkT, "mq": mqT, "dk": dkT, "dq": dqT, "sc": scb}.get(kind)
                    dst = f_tmp[:, j % 2, :] if dst is None else dst[:, j, :]
                    scale = {"mk": P ** -0.5, "dq": 64 ** -0.5}.get(kind, 1.0)
                    sc.activation(two(dst), dbuf(n), ACT.Copy, scale=scale).then_inc(S["act_drained"], 1)
                elif kind == "ml":
                    stage, u = a
                    c = ML_ORDER[u]
                    col, L = TILES[c]
                    if stage == 0:
                        act.wait_ge(S["ml_scores"], u + 1)
                        wait_drained(act, block_of[("gtr", 0)])
                        if u >= 1:
                            act.wait_ge(S["ml_pt"], u)
                            act.wait_ge(S["ml_kw"], u)
                        for h in range(H):
                            last = sc.activation(w_ml[0:L, h, 0:L], X[0:L, 0, P * h:P * h + L], ACT.Exp,
                                                 bias=gT[0:L, c, h:h + 1])
                        last.then_inc(S["ml_w"], 1)
                    elif stage == 1:
                        act.wait_ge(S["ml_rd"], u + 1)
                        for h in range(H):
                            last = sc.activation(tmp[0:L, 0, P * h:P * h + P],
                                                 X[0:L, h // 2, 129 * (h % 2):129 * (h % 2) + P], ACT.Square,
                                                 scale=rden[0:L, h:h + 1], accum_out=ssq[0:L, h:h + 1])
                        last.then_inc(S["ml_ssq"], 1)
                    else:
                        act.wait_ge(S["ml_ht"], u + 1)
                        for h in range(H):
                            last = sc.activation(mqT[:, h, col:col + L], X[:, 0, P * h:P * h + L], ACT.Copy,
                                                 scale=vec[:, 44 + h:45 + h])
                        last.then_inc(S["ml_hm"], 1)
                        if u == 4:
                            act.wait_ge(S["ml_hm"], 5)
                            act.wait_ge(S["out_m"], 32)
                            act.dma_start(ck[:], cache_k[0, 0].rearrange("(b p) h d -> p b (h d)", p=P))\
                                .then_inc(S["ck_in"], 16)
                            act.wait_ge(S["out_k"], 32)
                            act.wait_ge(S["dense_done"], block_of[("tok", ("dv", 3))] + 1)
                            act.dma_start(cv[:], cache_v[0, 0].rearrange("(b p) h d -> p b (h d)", p=P))\
                                .then_inc(S["cv_in"], 16)
                elif kind == "ck":
                    act.wait_ge(S["ck_tr"], a[0] + 1)
                    sc.activation(ckT[:, 2 * a[0] + 1, :].rearrange("p (a b) -> p a b", a=2), X[:, 2:4, :],
                                  ACT.Copy).then_inc(S["ck_act"], 1)
                elif kind == "sample":
                    c = a[0]
                    act.wait_ge(S["at_mx"], c + 1)
                    sc.activation(prob[:, c, :], X[:].rearrange("p a b -> p (a b)")[:, 0:1056], ACT.Exp,
                                  bias=nmax[:, 0, c:c + 1], accum_out=psum_p[:, 0, c:c + 1]).then_inc(S["at_exp"], 1)
                elif kind == "at":
                    stage, u = a
                    h, i = (u - 1) // 4, (u - 1) % 4
                    nk = P * (i + 1)
                    if stage == 0:
                        act.wait_ge(S["at_mx"], u + 2)
                        if u >= 2:
                            act.wait_ge(S["at_tr"], u - 1)
                        for c in range(2):
                            last = sc.activation(prob2[:, u % 2, c, 0:nk], X[:, c, 0:nk], ACT.Exp,
                                                 bias=nmax[:, u % 2, c:c + 1], accum_out=psum_p[:, u % 2, c:c + 1])
                        last.then_inc(S["at_exp"], 1)
                    elif stage == 1:
                        act.wait_ge(S["at_tr"], u + 1)
                        if u == 0:
                            sc.activation(wdT[:, 0:8, :].rearrange("p a b -> p (a b)"),
                                          X[:].rearrange("p a b -> p (a b)")[:, 0:1024], ACT.Copy)
                            sc.activation(wdT[0:TS, 8, :], X[0:TS, 2, 0:P], ACT.Copy).then_inc(S["at_wt"], 1)
                        else:
                            act.wait_ge(S["at_o"], max(u - 1, 1))
                            sc.activation(wdT[:, 4 * (u % 2):4 * (u % 2) + i + 1, :].rearrange("p a b -> p (a b)"),
                                          X[:, 2, 0:nk], ACT.Copy).then_inc(S["at_wt"], 1)
                    elif stage == 2:
                        act.wait_ge(S["at_o"], u + 1)
                        sc.activation(junk[:], X[:, 3, 0:P], ACT.Square, scale=rsum[:, u % 4, 0:1],
                                      accum_out=assq[:, u % 2:u % 2 + 1]).then_inc(S["at_sq"], 1)
                    else:
                        act.wait_ge(S["at_ot"], u + 1)
                        if u >= 2:
                            act.wait_ge(S["yc_split"], u - 1)
                        sc.activation(y_tmp[:, u % 2, :], X[:, 2, 0:P], ACT.Copy, scale=vec[:, 48:49])\
                            .then_inc(S["at_yc"], 1)
                elif kind == "sb" or (kind == "pr" and a[0] == 2):
                    k = tmp_index[(kind, *a)]
                    if kind == "sb":
                        wait_drained(act, n)
                        sc.activation(yb_h[:, a[0], :], tmp[:, k % 2, :], ACT.Copy).then_inc(S["y_h"], 1)
                    else:
                        act.wait_ge(S["merged_v"], a[1] + 1)
                        sc.activation(mg_h[:, a[1], :], tmp[:, k % 2, :], ACT.Copy).then_inc(S["merged_h"], 1)
                elif kind in ("mo", "gt"):
                    act.wait_ge(S["dense_done"], n + 1)
                    if kind == "gt" and a[0] == 2:
                        if a[1] == 0:
                            act.wait_ge(S["dense_done"], block_of[("pr", 1, KD - 1)] + 1)
                        sc.activation(two(gate2[:, a[1], :]), dbuf(n), ACT.Tanh, scale=0.5)\
                            .then_inc(S["act_drained"], 1)
                    else:
                        k = tmp_index[(kind, *a)]
                        wait_tmp_free(act, k)
                        sc.activation(two(tmp[:, k % 2, :]), dbuf(n), ACT.Tanh, scale=0.5)\
                            .then_inc(S["act_drained"], 1)
                        if kind == "mo":
                            act.wait_ge(S["y_v"], a[0] + 1)
                            if a[0] == 0:
                                act.wait_ge(S["ck_tr"], 2)
                            sc.activation(ya_h[:, a[0], :], tmp[:, k % 2, :], ACT.Copy).then_inc(S["y_h"], 1)
                elif kind == "up":
                    j, part = a
                    jj = j + JF * part
                    m = up_index[a]
                    act.wait_ge(S["dense_done"], n + 1)
                    if m >= 2:
                        act.wait_ge(S["conv_done"], m - 1)
                    else:
                        act.wait_ge(S["conv_kept"], 5)
                    if j >= 2:
                        act.wait_ge(S["gl_ready"], j - 1)
                    if m == 0:
                        act.wait_ge(S["dense_done"], block_of[("wo", KD - 1)] + 1)
                    sc.activation(two(ups[:, m % 2, 2:T + 2]), dbuf(n), ACT.Copy)
                    sc.activation(two(acc[:, part, j % 2, :]), dbuf(n), ACT.Copy, scale=fcw[:, 2, jj:jj + 1])\
                        .then_inc(S["act_drained"], 1)
                    if part == 1:
                        k = tmp_index[("up", j)]
                        act.wait_ge(S["conv_done"], up_index[(j, 0)] + 1)
                        wait_tmp_free(act, k)
                        sc.activation(tmp[:, k % 2, :], acc[:, 0, j % 2, :], ACT.Tanh, scale=0.5)\
                            .then_inc(S["th_ready"], 1)
                    if m >= 1 and part_of[m - 1] == 1:
                        high_g(j_of[m - 1])
                elif kind == "state":
                    high_g(JF - 1)
                elif kind == "yT":
                    j = a[0]
                    act.wait_ge(S["dense_done"], n + 1)
                    b = 2 * (n % 2)
                    sc.activation(yst[:, :, P * j:P * j + P], D[:, b, :].rearrange("p (c f) -> p c f", c=4), ACT.Copy)
                    sc.activation(yst_s[0:TS, P * j:P * j + P], D[0:TS, b + 1, 0:P], ACT.Copy)\
                        .then_inc(S["act_drained"], 1)

        @block.vector
        def _(dve):
            v = nc.vector
            chain = [0]

            def link(ins):
                chain[0] += 1
                ins.then_inc(S["dve_chain"], 1)
                dve.wait_ge(S["dve_chain"], chain[0])

            def split(g):
                wait_raw(dve, g)
                wait_split_slot(dve, g)
                src, hi, lo = raw_view(g), split_view(w_h, g), split_view(w_l, g)
                if GROUPS[g][0][0] == "if":
                    v.memset(hi[:, :, H:32].bitcast(F32), 0.0)
                    v.memset(lo[:, :, H:32].bitcast(F32), 0.0)
                    dve.wait_ge(S["wh_ready"], g + 1)
                    v.tensor_tensor(lo[:, :, 0:H], src[:, :, 0:H], hi[:, :, 0:H].bitcast(F32), ALU.subtract)
                    v.tensor_tensor(lo[:, :, 32:36], src[:, :, H:2 * H], hi[:, :, 32:36].bitcast(F32),
                                    ALU.subtract).then_inc(S["wl_ready"], 1)
                else:
                    dve.wait_ge(S["wh_ready"], g + 1)
                    v.tensor_tensor(lo, src, hi.bitcast(F32), ALU.subtract).then_inc(S["wl_ready"], 1)

            def combine(u, p0, p1):
                s = psum_p[:, u % 2, :]
                dve.wait_ge(S["at_exp"], u + 2)
                if u == 0:
                    dve.wait_ge(S["lam_dve"], 3)
                link(v.reciprocal(rsum[:, u % 4, :], s))
                link(v.scalar_tensor_tensor(out=kap[:], in0=s[:, 0:1], scalar=rsum[:, u % 4, 1:2], in1=neg_lam[:],
                                            op0=ALU.mult, op1=ALU.mult))
                v.scalar_tensor_tensor(out=p0, in0=p1, scalar=kap[:], in1=p0, op0=ALU.mult, op1=ALU.add)\
                    .then_inc(S["at_wd"], 1)

            for g in range(AHEAD):
                split(g)
            for kind, a, n in ORDER:
                b = None if n is None else 2 * (n % 2)
                if n is not None:
                    for g in splits(n):
                        if g < len(GROUPS):
                            split(g)
                if kind == "small":
                    dve.wait_ge(S["small_in"], 16 * 16)
                    link(v.tensor_tensor(lam_p[:], lam_t[:, :, 0, :], lam_t[:, :, 1, :], ALU.mult))
                    v.reduce_sum(lam_e[:], lam_p[:], axis=AX.X).then_inc(S["lam_dve"], 2)
                    dve.wait_ge(S["lam_act"], 1)
                    link(v.tensor_scalar(neg_lam[:], lam_e[:, 1:2], -LAM_INIT, None, ALU.add))
                    v.tensor_tensor(neg_lam[:], neg_lam[:], lam_e[:, 0:1], ALU.subtract).then_inc(S["lam_dve"], 1)
                    dve.wait_ge(S["dense_done"], n + 1)
                    link(v.tensor_copy(vec[:], D[:, b, 0:49]))
                    link(v.tensor_scalar(vec[:, 44:48], vec[:, 44:48], 0.5, None, ALU.mult))
                    link(v.tensor_scalar(vec[:, 48:49], vec[:, 48:49], 1.0 - LAM_INIT, None, ALU.mult))
                    v.tensor_copy(hist[:].rearrange("p a b -> p (a b)"), D[:, b, 49:49 + 2 * JU])
                    v.tensor_copy(fcw[:].rearrange("p a b -> p (a b)"), D[:, b + 1, 0:3 * JU])\
                        .then_inc(S["dve_drained"], 1)
                elif kind == "xT":
                    dve.wait_ge(S["dense_done"], n + 1)
                    v.tensor_copy(xT[:, a[0], 0:TP], D[:, b, :])
                    v.tensor_copy(xT[:, a[0], S0:T], D[:, b + 1, 0:TS]).then_inc(S["dve_drained"], 1)
                elif kind == "norm":
                    r = a[0]
                    dve.wait_ge(S["rstd_ready"], r + 1)

                    def scaled(j, out, done):
                        v.scalar_tensor_tensor(out=out, in0=xT[:, j, :], scalar=vec[:, KD * r + j:KD * r + j + 1],
                                               in1=rstd[r][:], op0=ALU.mult, op1=ALU.mult).then_inc(S[done], 1)

                    if r == 2:
                        for j in range(KD):
                            scaled(j, xT[:, j, :], "y_ready")
                    else:
                        for j in range(KD):
                            k = tmp_index[("norm", r, j)]
                            wait_tmp_free(dve, k)
                            scaled(j, tmp[:, k % 2, :], "hn_dve")
                            if j % 2 == 1:
                                k -= 1
                                dve.wait_ge(S["hh_act"], KD * r + j)
                                v.tensor_tensor(h_l[:, j - 1, :], tmp[:, k % 2, :], h_h[:, j - 1, :].bitcast(F32),
                                                ALU.subtract).then_inc(S["hl_dve"], 1)
                elif kind == "if":
                    wait_drained(dve, n)
                    v.tensor_scalar(row["lf"], row["lf"], b_f[:], None, ALU.add).then_inc(S["rows_dve"], 1)
                    link(v.memset(row["em"], 1.0))
                    for col, _ in TILES:
                        last = v.memset(row["em"][:, col:col + 1], 0.0)
                    last.then_inc(S["rows_dve"], 1)
                    dve.wait_ge(S["rows_act"], 1)
                    dve.wait_ge(S["rows_dve"], 2)
                    v.scalar_tensor_tensor(out=row["lf"], in0=row["lf"], scalar=0.0, in1=row["g"], op0=ALU.min,
                                           op1=ALU.subtract).then_inc(S["rows_dve"], 1)
                    dve.wait_ge(S["rows_dve"], 3)
                    v.tensor_tensor_scan(row["cum"], row["em"], row["lf"], 0.0, ALU.mult, ALU.add)
                    v.memset(row["m"][:, TP:S0], 0.0)
                    v.tensor_tensor_scan(row["m"][:, 0:TP], row["lf"][:, 0:TP], row["ig"][:, 0:TP], 0.0,
                                         ALU.add, ALU.max).then_inc(S["rows_dve"], 2)
                    v.tensor_tensor_scan(row["m"][:, S0:T], row["lf"][:, S0:T], row["ig"][:, S0:T], m_s[:],
                                         ALU.add, ALU.max).then_inc(S["rows_dve"], 1)
                    dve.wait_ge(S["rows_dve"], 6)
                    v.tensor_tensor(row["g"], row["ig"], row["cum"], ALU.subtract)
                    v.tensor_tensor(row["u"], row["cum"], row["m"], ALU.subtract).then_inc(S["rows_dve"], 1)
                elif kind == "tok":
                    name, j = a[0]
                    dve.wait_ge(S["dense_done"], n + 1)
                    if name == "dv" or name == "mv":
                        dst = (mv_tok if name == "mv" else dv_tok)[:, :, j, 0:P]
                    elif name == "mk":
                        dst = mk_tok[:, :, j, :]
                    else:
                        dst = k_out[:, :, P * j:P * j + P]
                    v.tensor_copy(dst[:, 0:4, :], D[:, b, :].rearrange("p (c f) -> p c f", c=4))
                    v.tensor_copy(dst[0:TS, 4, :], D[0:TS, b + 1, 0:P]).then_inc(S["dve_drained"], 1)
                elif kind == "gtr":
                    dve.wait_ge(S["dense_done"], n + 1)
                    for t, s in ((gT, 0), (emT, 1)):
                        v.tensor_copy(t[:, 0:4, :], D[:, b + s, 0:16].rearrange("p (c h) -> p c h", c=4))
                        last = v.tensor_copy(t[0:TS, 4, :], D[0:TS, b + s, 16:20])
                    last.then_inc(S["dve_drained"], 1)
                elif kind == "ml":
                    stage, u = a
                    c = ML_ORDER[u]
                    col, L = TILES[c]
                    C = C_p if c < 4 else C_s
                    if stage == 0:
                        dve.wait_ge(S["ml_scores"], u + 1)
                        if u >= 1:
                            dve.wait_ge(S["ml_ht"], u)
                        inter = X[:, 2, :].rearrange("p (h t) -> p h t", h=H)
                        v.tensor_tensor(qi[:, :, 0:L], mqT[:, :, col:col + L], inter[:, :, 0:L], ALU.mult)
                        v.tensor_copy(il[:], inter[:, :, L - 1]).then_inc(S["ml_qi"], 1)
                        dve.wait_ge(S["ml_w"], u + 1)
                        scores = X[:, 1, :].rearrange("p (h t) -> p h t", h=H)
                        v.tensor_tensor(p_ml[0:L, :, 0:L], w_ml[0:L, :, 0:L], scores[0:L, :, 0:L], ALU.mult)\
                            .then_inc(S["ml_pt"], 1)
                    elif stage == 1:
                        dve.wait_ge(S["ml_num"], u + 1)
                        num = X[0:L, 0:2, 0:2 * (P + 1)].rearrange("p a (b e) -> p a b e", b=2)
                        den2 = den[0:L, :].rearrange("p (a b) -> p a b", a=2)
                        em2 = emT[0:L, c, :].rearrange("p (a b) -> p a b", a=2)
                        link(v.scalar_tensor_tensor(out=den2, in0=num[:, :, :, P], scalar=-1.0, in1=em2,
                                                    op0=ALU.mult, op1=ALU.max))
                        link(v.scalar_tensor_tensor(out=den2, in0=num[:, :, :, P], scalar=1.0, in1=den2,
                                                    op0=ALU.mult, op1=ALU.max))
                        v.reciprocal(rden[0:L, :], den[0:L, :]).then_inc(S["ml_rd"], 1)
                        dve.wait_ge(S["ml_qi"], u + 1)
                        for h in range(H):
                            last = v.scalar_tensor_tensor(out=C[:, h, :], in0=C[:, h, :], scalar=il[:, h:h + 1],
                                                          in1=X[:, 2 + h // 2, 129 * (h % 2):129 * (h % 2) + 129],
                                                          op0=ALU.mult, op1=ALU.add)
                        last.then_inc(S["ml_c"], 1)
                        dve.wait_ge(S["ml_rr"], u + 1)
                        rr2 = rr[0:L, :].rearrange("p (a b) -> p a b", a=2).unsqueeze(3).to_broadcast([L, 2, 2, P])
                        v.tensor_tensor(hn[0:L].rearrange("p (a b) e -> p a b e", a=2), num[:, :, :, 0:P], rr2,
                                        ALU.mult).then_inc(S["ml_hn"], 1)
                elif kind == "ck":
                    dve.wait_ge(S["ck_tr"], a[0] + 1)
                    v.tensor_copy(ckT[:, 2 * a[0], :].rearrange("p (a b) -> p a b", a=2), X[:, 0:2, :])\
                        .then_inc(S["ck_dve"], 1)
                elif kind == "sample":
                    c = a[0]
                    dve.wait_ge(S["at_s"], c + 1)
                    v.tensor_reduce(nmax[:, 0, c:c + 1], X[:].rearrange("p a b -> p (a b)")[:, 0:1056], AX.X, ALU.max,
                                    negate=True).then_inc(S["at_mx"], 1)
                    if c == 1:
                        combine(0, prob[:, 0, :], prob[:, 1, :])
                elif kind == "at":
                    stage, u = a
                    if stage == 0:
                        nk = P * ((u - 1) % 4 + 1)
                        dve.wait_ge(S["at_s"], u + 2)
                        v.tensor_reduce(nmax[:, u % 2, :], X[:, 0:2, 0:nk], AX.X, ALU.max, negate=True)\
                            .then_inc(S["at_mx"], 1)
                        combine(u, prob2[:, u % 2, 0, 0:nk], prob2[:, u % 2, 1, 0:nk])
                    elif stage == 2:
                        dve.wait_ge(S["at_rr"], u + 1)
                        if u >= 2:
                            dve.wait_ge(S["at_ot"], u - 1)
                        v.tensor_scalar(on[:, u % 2, :], X[:, 3, 0:P], arr[:, u % 2:u % 2 + 1], None, ALU.mult)\
                            .then_inc(S["at_on"], 1)
                elif kind == "mo":
                    k = tmp_index[("mo", a[0])]
                    wait_drained(dve, n)
                    dve.wait_ge(S["ml_hm"], 5)
                    v.scalar_tensor_tensor(out=tmp[:, k % 2, :], in0=tmp[:, k % 2, :], scalar=1.0, in1=mqT[:, a[0], :],
                                           op0=ALU.add, op1=ALU.mult).then_inc(S["y_v"], 1)
                elif kind == "sx":
                    j = a[0]
                    dve.wait_ge(S["dense_done"], n + 1)
                    wait_drained(dve, block_of[("sc", j)])
                    u = u_c[:, j % 2, :]
                    if j >= 2:
                        dve.wait_ge(S["conv_kept"], j - 1)
                    v.memset(u[:, 0:2], 0.0)
                    v.tensor_tensor(two(u[:, 2:T + 2]), dbuf(n), two(scb[:, j, :]), ALU.mult)\
                        .then_inc(S["dve_drained"], 1)
                    wait_drained(dve, n)
                    link(v.tensor_copy(u[:, S0:S0 + 2], vec[:, 36:44].rearrange("p (r j) -> p r j", r=2)[:, :, j]))
                    w = lambda t: vec[:, 24 + 4 * t + j:25 + 4 * t + j]
                    v.tensor_scalar(scb[:, j, :], u[:, 0:T], w(0), None, ALU.mult).then_inc(S["u_ready"], 1)
                    dve.wait_ge(S["u_ready"], j + 1)
                    link(v.scalar_tensor_tensor(out=scb[:, j, :], in0=u[:, 1:T + 1], scalar=w(1), in1=scb[:, j, :],
                                                op0=ALU.mult, op1=ALU.add))
                    link(v.scalar_tensor_tensor(out=scb[:, j, :], in0=u[:, 2:T + 2], scalar=w(2), in1=scb[:, j, :],
                                                op0=ALU.mult, op1=ALU.add))
                elif kind == "sb":
                    k = tmp_index[("sb", a[0])]
                    dve.wait_ge(S["dense_done"], n + 1)
                    wait_tmp_free(dve, k)
                    v.tensor_tensor(two(tmp[:, k % 2, :]), dbuf(n), two(scb[:, a[0], :]), ALU.mult)\
                        .then_inc(S["dve_drained"], 1)
                elif kind == "pr":
                    br, j = a
                    dve.wait_ge(S["dense_done"], n + 1)
                    if br == 2:
                        g = gate2[:, j, :]
                    else:
                        g = tmp[:, tmp_index[("gt", br, j)] % 2, :]
                    wait_drained(dve, block_of[("gt", br, j)])
                    if br == 0 and j == 0:
                        dve.wait_ge(S["at_o"], 1)
                    out = merged[:, j, :] if br == 0 else g
                    v.scalar_tensor_tensor(out=two(out), in0=two(g), scalar=1.0, in1=dbuf(n), op0=ALU.add,
                                           op1=ALU.mult).then_inc(S["dve_drained"], 1)
                    if br == 1:
                        wait_drained(dve, n)
                        v.tensor_tensor(merged[:, j, :], merged[:, j, :], g, ALU.add).then_inc(S["merged_added"], 1)
                    elif br == 2:
                        k = tmp_index[("pr", 2, j)]
                        wait_drained(dve, n)
                        wait_tmp_free(dve, k)
                        v.tensor_tensor(tmp[:, k % 2, :], merged[:, j, :], g, ALU.add).then_inc(S["merged_v"], 1)
                elif kind in ("wo", "dn"):
                    dve.wait_ge(S["dense_done"], n + 1)
                    v.scalar_tensor_tensor(out=two(xT[:, a[0], :]), in0=dbuf(n), scalar=0.5, in1=two(xT[:, a[0], :]),
                                           op0=ALU.mult, op1=ALU.add).then_inc(S["dve_drained"], 1)
                elif kind == "up":
                    j, part = a
                    jj = j + JF * part
                    m = up_index[a]
                    u, ac = ups[:, m % 2, :], acc[:, part, j % 2, :]
                    dve.wait_ge(S["hist_ready"], m + 1)
                    link(v.scalar_tensor_tensor(out=ac, in0=u[:, 1:T + 1], scalar=fcw[:, 1, jj:jj + 1], in1=ac,
                                                op0=ALU.mult, op1=ALU.add))
                    v.scalar_tensor_tensor(out=ac, in0=u[:, 0:T], scalar=fcw[:, 0, jj:jj + 1], in1=ac,
                                           op0=ALU.mult, op1=ALU.add).then_inc(S["conv_done"], 1)
                    if part == 1:
                        k = tmp_index[("up", j)]
                        dve.wait_ge(S["th_ready"], j + 1)
                        v.scalar_tensor_tensor(out=acc[:, 0, j % 2, :], in0=tmp[:, k % 2, :], scalar=1.0,
                                               in1=acc[:, 0, j % 2, :], op0=ALU.add, op1=ALU.mult)\
                            .then_inc(S["silu_done"], 1)
                        dve.wait_ge(S["silu_done"], j + 1)
                        dve.wait_ge(S["conv_done"], m + 1)
                        v.tensor_tensor(acc[:, 0, j % 2, :], acc[:, 0, j % 2, :], ac, ALU.mult)\
                            .then_inc(S["g_ready"], 1)
                elif kind == "state":
                    dve.wait_ge(S["dense_done"], n + 1)
                    v.tensor_copy(fst[0:2 * JU], D[0:2 * JU, b, 0:2 * P].rearrange("p (g f) -> p g f", g=2))\
                        .then_inc(S["cst_ready"], 1)
                    v.tensor_copy(cst[:], D[0:16, b + 1, 0:P]).then_inc(S["cst_ready"], 1)
                    v.memset(kap[:], 0.0).then_inc(S["dve_drained"], 1)

        @block.tensor
        def _(pe):
            t = nc.tensor

            def product(n, x_h, x_l, wait_k=None):
                gs, kx = range(first_group[n], first_group[n + 1]), 0
                kall = sum(GROUPS[g][2] for g in gs)
                for g in gs:
                    pe.wait_ge(S["wh_ready"], g + 1)
                    pe.wait_ge(S["wl_ready"], g + 1)
                    wh, wl = split_view(w_h, g), split_view(w_l, g)
                    for k in range(GROUPS[g][2]):
                        if wait_k:
                            wait_k(kx)
                        for i, (w, x) in enumerate(((wh, x_h), (wh, x_l), (wl, x_h))):
                            for half in range(2):
                                last = t.matmul(D[0:w.shape[2], 2 * (n % 2) + half, 0:HALF], w[:, k, :],
                                                x[:, kx, HALF * half:HALF * half + HALF],
                                                start=kx == 0 and i == 0, stop=kx == kall - 1 and i == 2)
                        kx += 1
                    last.then_inc(S["dense_done" if g == gs[-1] else "part_used"], 1)

            def wait_h(r):
                return lambda k: pe.wait_ge(S[("hl_dve", "hl_pool")[k % 2]], KD // 2 * r + k // 2 + 1)

            for kind, a, n in ORDER:
                if n is not None and n >= 2:
                    wait_drained(pe, n - 2)
                b = None if n is None else 2 * (n % 2)
                if kind == "small":
                    pe.wait_ge(S["const_ready"], 8)
                    pe.wait_ge(S["small_in"], 16 * 16)
                    t.transpose(D[:, b, 0:49], small_a[0:49, :], ident[0:49, 0:49])
                    t.transpose(D[:, b, 49:49 + 2 * JU], small_b[0:2 * JU, :], ident[0:2 * JU, 0:2 * JU])
                    t.transpose(D[:, b + 1, 0:66], small_c[0:66, 0, :], ident[0:66, 0:66])
                    t.transpose(D[:, b + 1, 66:132], small_c[0:66, 1, :], ident[0:66, 0:66])\
                        .then_inc(S["dense_done"], 1)
                elif kind == "xT":
                    j = a[0]
                    if j == 0:
                        pe.wait_ge(S["xs_in"], 16)
                        pe.wait_ge(S["x_in"], 32)
                    for c in range(4):
                        t.transpose(D[:, b, P * c:P * c + P], x_t[:, c, P * j:P * j + P], ident[:])
                    t.transpose(D[:, b + 1, 0:TS], x_s[0:TS, P * j:P * j + P], ident[0:TS, 0:TS])\
                        .then_inc(S["dense_done"], 1)
                elif kind == "norm":
                    pe.wait_ge(S["sq_added"], KD * (a[0] + 1))
                    for half in range(2):
                        last = t.matmul(D[:, b + half, 0:HALF], mean_w[:],
                                        ssum[a[0]][:, HALF * half:HALF * half + HALF], start=True, stop=True)
                    last.then_inc(S["dense_done"], 1)
                elif kind == "if":
                    product(n, h_h, h_l, wait_h(0))
                elif kind in W_IN_AT or kind == "gt":
                    product(n, h_h, h_l)
                elif kind == "pr":
                    br, j = a
                    if j == 0:
                        if br < 2:
                            pe.wait_ge(S["y_split"], 4 * (br + 1))
                        else:
                            pe.wait_ge(S["yc_split"], 17)
                            pe.wait_ge(S["yc_spare"], 1)
                    product(n, (ya_h, yb_h, yc_h)[br], (ya_l, yb_l, yc_l)[br])
                elif kind == "wo":
                    product(n, mg_h, mg_l, (lambda k: pe.wait_ge(S["merged_split"], k + 1)) if a[0] == 0 else None)
                elif kind == "up":
                    product(n, h_h, h_l, wait_h(1) if a == (0, 0) else None)
                elif kind == "dn":
                    product(n, g_h, g_l, (lambda k: pe.wait_ge(S["gl_ready"], k + 1)) if a[0] == 0 else None)
                elif kind == "tok":
                    name, j = a[0]
                    src = src_tok(name, j)
                    wait_drained(pe, block_of[(name, j)])
                    for c in range(4):
                        t.transpose(D[:, b, P * c:P * c + P], src[:, P * c:P * c + P], ident[:])
                    t.transpose(D[0:TS, b + 1, 0:P], src[:, S0:T], ident[:]).then_inc(S["dense_done"], 1)
                elif kind == "gtr":
                    pe.wait_ge(S["rows_act"], 2)
                    for s, nm in enumerate(("g", "em")):
                        for c, (col, L) in enumerate(TILES):
                            last = t.transpose(D[0:L, b + s, H * c:H * c + H], row[nm][:, col:col + L], ident[0:H, 0:H])
                    last.then_inc(S["dense_done"], 1)
                elif kind == "ml":
                    stage, u = a
                    c = ML_ORDER[u]
                    col, L = TILES[c]
                    C = C_p if c < 4 else C_s
                    hs = range(H)
                    if stage == 0:
                        if u == 0:
                            wait_drained(pe, block_of[("mq", 3)])
                        else:
                            pe.wait_ge(S["ml_hm"], u)
                            pe.wait_ge(S["ml_c"], u)
                        lw = X[0:L, 0, :].rearrange("p (h t) -> p h t", h=H)[:, :, 0:L]
                        t.matmul(lw, ident[0:L, 0:L], causal[0:L, 0:L].unsqueeze(1).to_broadcast([L, H, L]),
                                 start=True, stop=False, skip_group_check=True)
                        for h in hs:
                            t.matmul(X[0:L, 0, P * h:P * h + L], sel[0:H, h, 0:L], row["u"][:, col:col + L],
                                     start=False, stop=h == H - 1, skip_group_check=True)
                        for h in hs:
                            t.matmul(X[0:L, 1, P * h:P * h + L], mkT[:, h, col:col + L], mqT[:, h, col:col + L],
                                     start=True, stop=True)
                        for h in hs:
                            last = t.matmul(X[:, 2, P * h:P * h + L], sel[0:H, h, :], row["inter"][:, col:col + L],
                                            start=True, stop=True)
                        last.then_inc(S["ml_scores"], 1)
                    elif stage == 1:
                        pe.wait_ge(S["ml_pt"], u + 1)
                        pe.wait_ge(S["ml_qi"], u + 1)
                        pe.wait_ge(S["ml_kw"], u + 1)
                        if u == 0:
                            wait_drained(pe, block_of[("tok", ("mv", 3))])
                            pe.wait_ge(S["const_ready"], 9)
                        for h in hs:
                            o = X[0:L, h // 2, 129 * (h % 2):129 * (h % 2) + 129]
                            t.matmul(o, qi[:, h, 0:L], C[:, h, :], start=True, stop=False)
                            t.matmul(o, p_ml[0:L, h, 0:L], mv_tok[0:L, c, h, :], start=False, stop=True)
                        for h in hs:
                            last = t.matmul(X[:, 2 + h // 2, 129 * (h % 2):129 * (h % 2) + 129], kw[0:L, h, :],
                                            mv_tok[0:L, c, h, :], start=True, stop=True)
                        last.then_inc(S["ml_num"], 1)
                    else:
                        pe.wait_ge(S["ml_hn"], u + 1)
                        for h in hs:
                            last = t.transpose(X[:, 0, P * h:P * h + L], hn[0:L, h, :], ident[0:L, 0:L])
                        last.then_inc(S["ml_ht"], 1)
                elif kind == "ck":
                    if a[0] == 0:
                        pe.wait_ge(S["ck_in"], 16)
                        pe.wait_ge(S["ml_hm"], 5)
                        pe.wait_ge(S["ml_c"], 5)
                    else:
                        pe.wait_ge(S["ck_dve"], 1)
                        pe.wait_ge(S["ck_act"], 1)
                    for hh in range(2):
                        for kb in range(8):
                            h = 2 * a[0] + hh
                            last = t.transpose(X[:, 2 * hh + kb // 4, P * (kb % 4):P * (kb % 4) + P],
                                               ck[:, kb, P * h:P * h + P], ident[:])
                    last.then_inc(S["ck_tr"], 1)
                elif kind == "sample":
                    c = a[0]
                    if c == 0:
                        pe.wait_ge(S["ck_dve"], 2)
                        pe.wait_ge(S["ck_act"], 2)
                        wait_drained(pe, block_of[("dq", 3)])
                    else:
                        pe.wait_ge(S["at_exp"], 1)
                    d = slice(64 * c, 64 * c + 64)
                    for h in range(H):
                        q = dqT[d, h, S0:T]
                        for kb in range(2):
                            t.matmul(X[TS * h:TS * h + TS, kb, :], q, ckT[d, h, 512 * kb:512 * kb + 512],
                                     start=True, stop=True)
                        last = t.matmul(X[TS * h:TS * h + TS, 2, 0:TS], q, dkT[d, h, S0:T], start=True, stop=True)
                    last.then_inc(S["at_s"], 1)
                elif kind == "at":
                    stage, u = a
                    h, i = (u - 1) // 4, (u - 1) % 4
                    nk = P * (i + 1)
                    if stage == 0:
                        pe.wait_ge(S["at_exp"], u + 1)
                        if u == 1:
                            pe.wait_ge(S["at_wt"], 1)
                        for c in range(2):
                            d = slice(64 * c, 64 * c + 64)
                            t.matmul(X[:, c, 0:nk], dqT[d, h, P * i:P * i + P], dkT[d, h, 0:nk],
                                     start=True, stop=False, skip_group_check=True)
                            last = t.matmul(X[:, c, nk - 64:nk], causal[64:65, :], mean_w[64:65, 0:64], start=False,
                                            stop=True, skip_group_check=True)
                        last.then_inc(S["at_s"], 1)
                    elif stage == 1:
                        pe.wait_ge(S["at_wd"], u + 1)
                        if u == 0:
                            for kb in range(8):
                                t.transpose(X[:, kb // 4, P * (kb % 4):P * (kb % 4) + P], prob[:, 0, P * kb:P * kb + P],
                                            ident[:])
                            last = t.transpose(X[0:TS, 2, 0:P], prob[:, 0, PAST:PAST + TS], ident[:])
                        else:
                            pe.wait_ge(S["at_wt"], u)
                            pe.wait_ge(S["at_yc"], max(u - 1, 1))
                            for kb in range(i + 1):
                                last = t.transpose(X[:, 2, P * kb:P * kb + P], prob2[:, u % 2, 0, P * kb:P * kb + P],
                                                   ident[:])
                        last.then_inc(S["at_tr"], 1)
                    elif stage == 2:
                        pe.wait_ge(S["at_wt"], u + 1)
                        if u == 0:
                            pe.wait_ge(S["cv_in"], 16)
                            wait_drained(pe, block_of[("tok", ("dv", 3))])
                            for hh in range(H):
                                o = X[TS * hh:TS * hh + TS, 3, 0:P]
                                for kb in range(8):
                                    t.matmul(o, wdT[:, kb, TS * hh:TS * hh + TS], cv[:, kb, P * hh:P * hh + P],
                                             start=kb == 0, stop=False)
                                last = t.matmul(o, wdT[0:TS, 8, TS * hh:TS * hh + TS], dv_tok[0:TS, 4, hh, :],
                                                start=False, stop=True)
                        else:
                            pe.wait_ge(S["at_on"], u)
                            for kb in range(i + 1):
                                last = t.matmul(X[:, 3, 0:P], wdT[:, 4 * (u % 2) + kb, :], dv_tok[:, kb, h, :],
                                                start=kb == 0, stop=kb == i)
                        last.then_inc(S["at_o"], 1)
                    else:
                        pe.wait_ge(S["at_on"], u + 1)
                        pe.wait_ge(S["at_wt"], min(u + 2, 17) if u else 1)
                        t.transpose(X[:, 2, 0:P], on[:, u % 2, :], ident[:]).then_inc(S["at_ot"], 1)
                elif kind == "state":
                    pe.wait_ge(S["hist_ready"], JU)
                    for s in range(2):
                        t.transpose(D[0:2 * JU, b, P * s:P * s + P], ffn_last[:, s].rearrange("p r j -> p (r j)"),
                                    ident[:])
                    t.transpose(D[0:16, b + 1, 0:P], conv_last[:].rearrange("p s r j -> p (s r j)"), ident[:])\
                        .then_inc(S["dense_done"], 1)
                elif kind == "yT":
                    j = a[0]
                    pe.wait_ge(S["y_ready"], j + 1)
                    for c in range(4):
                        t.transpose(D[:, b, P * c:P * c + P], xT[:, j, P * c:P * c + P], ident[:])
                    t.transpose(D[0:TS, b + 1, 0:P], xT[:, j, S0:T], ident[:]).then_inc(S["dense_done"], 1)


_INS = ["x_prompt", "x_sample", "cache_k", "cache_v", "state_C", "state_n", "state_m", "state_conv", "state_ffn",
        "norm1", "w_in", "b_if", "ml_norm", "w_sc_conv", "da_lambda", "da_norm", "w_branch", "w_out", "norm2",
        "w_up", "w_fconv", "w_down", "norm_f"]
_OUTS = [(1, TP, DM), (1, TS, DM),
         (1, 1, TP, 4, 128), (1, 1, TP, 4, 128), (1, 1, 4, 128, 128), (1, 1, 4, 128), (1, 1, 4), (1, 1, 2, 512),
         (1, 1, 2, 2 * DFF),
         (1, 1, TS, 4, 128), (1, 1, TS, 4, 128), (1, 1, 4, 128, 128), (1, 1, 4, 128), (1, 1, 4), (1, 1, 2, 512),
         (1, 1, 2, 2 * DFF)]


def kernel(**inputs):
    import numpy as _np
    import concourse.bacc as _bacc
    from concourse.bass_utils import run_bass_kernel_spmd as _run

    nc = _bacc.Bacc("TRN2", target_bir_lowering=False, num_devices=1)
    arrays, args = {}, []
    for name in _INS:
        a = _np.ascontiguousarray(inputs[name])
        arrays[f"in_{name}"] = a
        args.append(nc.dram_tensor(f"in_{name}", a.shape, mybir.dt.from_np(a.dtype), kind="ExternalInput").ap())
    for i, shape in enumerate(_OUTS):
        args.append(nc.dram_tensor(f"out_{i}", shape, F32, kind="ExternalOutput").ap())
    streaming_encoder_step(nc, *args)
    r = _run(nc, [arrays], core_ids=[0])
    return tuple(r.results[0][f"out_{i}"] for i in range(len(_OUTS)))
```

```python
import concourse.bass as bass
from concourse import mybir
from contextlib import ExitStack

F32 = mybir.dt.float32
F32R = mybir.dt.float32r
ALU = mybir.AluOpType
ACT = mybir.ActivationFunctionType
AX = mybir.AxisListType

P = 128
DM = 1024
KD = DM // P
TP, TS, PAST = 512, 32, 1024
S0 = TP + 4
T = S0 + TS
HALF = T // 2
TILES = [(0, P), (P, P), (2 * P, P), (3 * P, P), (S0, TS)]
H = 4
BW = 512
DFF = 2816
JF = DFF // P
JU = 2 * JF
EPS = 1e-6
LAM_INIT = 0.2
NEG = -1e30
NRAW, NSPLIT = 2, 3
GROUP = KD * P
W_IN_AT = dict(mq=0, mk=512, mv=1024, mo=1536, sb=2056, sc=2568, sx=3080, dq=3592, dk=4104, dv=4616)
GATES_AT, BRANCH_AT = 2048, 5128
ML_ORDER = (4, 0, 1, 2, 3)

def streaming_encoder_step(nc, x_prompt, x_sample, cache_k, cache_v, state_C, state_n, state_m, state_conv,
                           state_ffn, norm1, w_in, b_if, ml_norm, w_sc_conv, da_lambda, da_norm, w_branch,
                           w_out, norm2, w_up, w_fconv, w_down, norm_f,
                           y_p, y_s, p_k, p_v, p_C, p_n, p_m, p_conv, p_ffn,
                           s_k, s_v, s_C, s_n, s_m, s_conv, s_ffn):
    ORDER, block_of = [], {}

    def add(kind, *a):
        block_of[(kind, *a)] = len(block_of)
        ORDER.append((kind, a, block_of[(kind, *a)]))

    def unit(kind, *a):
        ORDER.append((kind, a, None))

    for c in range(5):
        add("xT", c)
    add("small")
    add("rstd")
    unit("norm", 0)
    add("if")
    add("mk", 0)
    unit("lam")
    for name, j in [("mk", 1), ("tok", ("mk", 0)), ("mk", 2), ("tok", ("mk", 1)), ("mk", 3),
                    ("tok", ("mk", 2)), ("mq", 0), ("tok", ("mk", 3)), ("rows", 0), ("mq", 1), ("rows", 1), ("mq", 2),
                    ("mq", 3), ("rows", 2), ("mv", 0), ("mv", 1), ("tok", ("mv", 0)), ("mv", 2),
                    ("tok", ("mv", 1)), ("mv", 3), ("tok", ("mv", 2)), ("gtr", 0), ("dk", 0), ("tok", ("mv", 3))]:
        (unit if name == "rows" else add)(name, j)
    ml_fill = [[("dk", 1)], [("tok", ("dk", 0)), ("dk", 2)], [("tok", ("dk", 1)), ("dk", 3)],
               [("tok", ("dk", 2)), ("dv", 0)], [("tok", ("dk", 3)), ("dv", 1)], [("tok", ("dv", 0)), ("dv", 2)],
               [("tok", ("dv", 1)), ("dv", 3)], [("tok", ("dv", 2)), ("dq", 0)], [("tok", ("dv", 3)), ("dq", 1)],
               [("dq", 2)]]
    for u in range(5):
        for stage in range(3):
            unit("ml", stage, u)
            if stage < 2:
                for s in ml_fill.pop(0):
                    add(*s)
    add("dq", 3)
    add("sc", 0)
    unit("ck", 0)
    add("sc", 1)
    unit("ck", 1)
    add("sc", 2)
    unit("sample", 0)
    add("sc", 3)
    unit("sample", 1)
    add("mo", 0)
    unit("at", 1, 0)
    add("mo", 1)
    unit("at", 2, 0)
    add("mo", 2)
    unit("at", 3, 0)
    fill = [("mo", 3)] + [(s, 0, j) for j in range(KD) for s in ("gt", "pr")]
    fill += [(s, j) for s in ("sx", "sb") for j in range(4)]
    fill += [(s, 1, j) for j in range(KD) for s in ("gt", "pr")]
    fill += [("gt", 2, j) for j in range(KD // 2)]
    for k in range(1, 20):
        for stage in (3, 0, 2, 1):
            if 1 <= k - stage <= 16:
                unit("at", stage, k - stage)
        add(*fill.pop(0))
        if k > 10:
            add(*fill.pop(0))
    for f in fill:
        add(*f)
    for s, j in [("pr", 0), ("gt", 4), ("pr", 1), ("pr", 2), ("pr", 3), ("gt", 5), ("pr", 4), ("pr", 5), ("gt", 6),
                 ("pr", 6), ("gt", 7), ("pr", 7)]:
        add(s, 2, j)
    for j in range(KD):
        add("wo", j)
    unit("norm", 1)
    for j in range(0, JF, 2):
        for part in range(2):
            add("up", j, part)
            add("up", j + 1, part)
    unit("last_g")
    for j in range(KD):
        add("dn", j)
        if j == 1:
            add("state")
        if j >= 1:
            unit("yT", j - 1)
    unit("norm", 2)
    unit("yT", KD - 1)
    unit("scale")

    up_index = {a: m for m, a in enumerate(a for kind, a, _ in ORDER if kind == "up")}
    j_of, part_of = [a[0] for a in up_index], [a[1] for a in up_index]

    BY_DVE = {"small", "xT", "tok", "gtr", "sx", "sb", "pr", "wo", "up", "dn", "state"}
    drained, count = {}, {"act": 0, "dve": 0}
    for kind, a, n in ORDER:
        if n is not None:
            e = "dve" if kind in BY_DVE else "act"
            count[e] += 1
            drained[n] = (e, count[e])

    buffer, used_before, last_user = {}, {}, {}
    turns = {"D": 0, "X": 2}
    for kind, a, n in ORDER:
        if n is not None:
            where = "X" if kind == "tok" and n < block_of[("tok", ("mv", 2))] else "D"
            buffer[n] = turns[where]
            turns[where] ^= 1
            used_before[n], last_user[buffer[n]] = last_user.get(buffer[n]), n

    def groups_of(kind, a):
        if kind == "if":
            return [(("if",), 0, KD, 0)]
        if kind in W_IN_AT or kind == "wo":
            return [((kind, a[0] // 2), 0, KD, P * (a[0] % 2))]
        if kind == "gt":
            return [(("gt", a[0], a[1] // 2), 0, KD, P * (a[1] % 2))]
        if kind == "pr":
            return [(("pr", a[0], a[1] // 4), 0, 4, P * (a[1] % 4))]
        if kind == "up":
            return [(("up", a[1], a[0] // 2), 0, KD, P * (a[0] % 2))]
        if kind == "dn":
            return [(("dn", a[0], half), k, m, 0) for half in range(2) for k, m in ((0, 6), (6, 5))]
        return []

    GROUPS, ITEMS, first_group, group_used, n_used = [], [], {}, [], 0
    for kind, a, n in ORDER:
        gs = groups_of(kind, a) if n is not None else []
        first_group[n] = len(GROUPS)
        for g in gs:
            if g[0] not in ITEMS:
                ITEMS.append(g[0])
            GROUPS.append(g)
            if g is gs[-1]:
                group_used.append(("dense_done", n + 1))
            else:
                n_used += 1
                group_used.append(("part_used", n_used))
    last_group = {g[0]: i for i, g in enumerate(GROUPS)}
    AHEAD = NSPLIT - 1

    tmp_slot, tmp_before, tmp_done, holder = {}, {}, {}, [None, None]

    def tmp_user(key, sem_name, value, slot=None):
        slot = (len(tmp_slot)) % 2 if slot is None else slot
        tmp_slot[key], tmp_before[key], tmp_done[key] = slot, holder[slot], (sem_name, value)
        holder[slot] = (sem_name, value)

    n_yl = 0
    for kind, a, n in ORDER:
        if kind in ("wo", "dn"):
            r = {"wo": 1, "dn": 2}[kind]
            if a[0] < KD - 1:
                tmp_user(("sq", r, a[0]), "sq_added", (KD - 1) * (r - 1) + a[0] + 1, slot=a[0] % 2)
            else:
                tmp_user(("sq", r, a[0]), "norm_mm", 2 * r, slot=a[0] % 2)
        elif kind == "norm" and a[0] == 1:
            tmp_user(("rstd", 1), "dve_drained", drained[block_of[("up", JF - 1, 1)]][1], slot=1)
        elif kind in ("mo", "sb"):
            n_yl += 1
            tmp_user((kind, a[0]), "y_split", n_yl)
        elif kind == "gt" and a[0] == 0:
            tmp_user(("gt", 0, a[1]), "dve_drained", drained[block_of[("pr", 0, a[1])]][1])
        elif kind == "gt" and a[0] == 1:
            tmp_user(("gt", 1, a[1]), "merged_added", a[1] + 1)
        elif kind == "pr" and a[0] == 2:
            tmp_user(("pr", 2, a[1]), "merged_split", a[1] + 1)
        elif kind == "up" and a[1] == 1:
            tmp_user(("up", a[0]), "silu_done", a[0] + 1, slot=0)

    ctx = ExitStack()
    with ctx:
        def sem(name):
            return ctx.enter_context(nc.semaphore(name))

        def up32(n):
            return (n + 31) // 32 * 32

        top = [up32(nc.sbuf_base)]

        def place(name, shape, at=None, dt=F32):
            size = 4
            for n in shape[1:]:
                size *= n
            here = top[0] if at is None else at
            if at is None:
                top[0] += up32(size)
                assert top[0] <= nc.sbuf_top, top[0] - nc.sbuf_top
            return nc.alloc_sbuf_tensor_at(name, shape, dt, offset=here)

        def span(floats):
            at = top[0]
            top[0] += up32(4 * floats)
            return at

        D = ctx.enter_context(nc.psum_tensor("D", [P, 4, 512], F32))
        X = ctx.enter_context(nc.psum_tensor("X", [P, 4, 512], F32))
        raw = place("raw", [P, NRAW, 2 * GROUP])
        w_h = place("w_h", [P, NSPLIT, GROUP], dt=F32R)
        w_l = place("w_l", [P, NSPLIT, GROUP], dt=F32R)
        xT = place("xT", [P, KD, T])
        H_AT = span(2 * KD * T)
        h_h = place("h_h", [P, KD, T], H_AT, F32R)
        h_l = place("h_l", [P, KD, T], H_AT + 4 * KD * T, F32R)
        TMP_AT = top[0]
        tmp = place("tmp", [P, 2, T])
        ident_r = place("ident", [P, P], dt=F32R)
        mean_r = place("mean_w", [P, P], dt=F32R)
        causal = place("causal", [P, P], dt=F32R)
        ident, mean_w = ident_r[:].bitcast(F32), mean_r[:].bitcast(F32)
        sel = place("sel", [36, H])
        vec = place("vec", [P, 41])
        hist = place("hist", [P, 2, JU])
        fcw = place("fcw", [P, 3, JU])
        conv_last = place("conv_last", [P, 2, 2, 4])
        b_i, b_f, m_s = place("b_i", [H, 1]), place("b_f", [H, 1]), place("m_s", [H, 1])
        neg_lam = place("neg_lam", [P, 1])
        lam_e = place("lam_e", [P, 2])
        m_half = place("m_half", [P, 1])
        il = place("il", [P, H])
        gT = place("gT", [P, 5, H])
        emT = place("emT", [P, 5, H])
        den, rden, ssq, rr = (place(x, [P, H]) for x in ("den", "rden", "ssq", "rr"))
        nmax = place("nmax", [P, 2, 2])
        psum_p = place("psum_p", [P, 2, 2])
        rsum = place("rsum", [P, 4, 2])
        kap = place("kap", [P, 1])
        assq, arr = place("assq", [P, 2]), place("arr", [P, 2])
        ssx = place("ssx", [P, 5])

        M_AT, G_AT, K_AT = span(KD * T), span(KD * T), span(7360)
        Q_AT, DQ_AT, DK_AT, DV_AT, WORK_AT = span(4 * T), span(4 * T), span(4 * T), span(2560), span(2564)
        assert top[0] <= nc.sbuf_top, top[0] - nc.sbuf_top
        END_AT = top[0]
        small_a = place("small_a", [41, P], M_AT)
        small_b = place("small_b", [2 * JU, P], M_AT + 512)
        small_c = place("small_c", [66, 2, P], M_AT + 1024)
        lam_t = place("lam_t", [P, 2, 2, 64], M_AT + 2048)
        lam_p = place("lam_p", [P, 2, 64], M_AT + 3072)
        x_t = place("x_t", [P, 4, DM], K_AT)
        x_s = place("x_s", [TS, DM], G_AT)
        diag = place("diag", [P, 5, P], DK_AT + up32(4 * T))
        hn_x = place("hn_x", [P, 4, T], Q_AT)
        ssum = {1: place("ssum1", [P, T], DK_AT), 2: place("ssum2", [P, T], H_AT)}
        rstd = [place("rstd0", [P, T], DK_AT)[:], tmp[:, 1, :]]
        f_tmp = place("f_tmp", [P, 2, T], M_AT)
        k_out = place("k_out", [P, 5, 512], M_AT + 8 * T)
        ui = place("ui", [36, 2, T], G_AT, F32R)
        bd_u = place("bd_u", [36, H, P], M_AT + 8 * T + 4 * 2560, F32R)
        bd_i = place("bd_i", [36, H, P], TMP_AT + up32(4 * T), F32R)
        rows_t = place("rows", [H, 8, T], G_AT)
        row = {nm: rows_t[:, i, :] for i, nm in enumerate(("lf", "ig", "cum", "m", "u", "g", "inter", "em"))}
        mkT = place("mkT", [P, 4, T], K_AT)
        mk_tok = place("mk_tok", [P, 5, H, P], K_AT + 16 * T)
        mv_tok = place("mv_tok", [P, 5, H, P + 1], K_AT + 16 * T + 4 * 2560)
        ml_junk = tmp[:, 0, :]
        mqT = place("mqT", [P, 4, T], Q_AT)
        dqT = place("dqT", [P, 4, T], DQ_AT)
        dkT = place("dkT", [P, 4, T], DK_AT)
        dv_tok = place("dv_tok", [P, 5, H, P], DV_AT)
        w_ml = place("w_ml", [P, H, P], WORK_AT)
        p_ml = place("p_ml", [P, H, P], WORK_AT + 2048)
        kw = place("kw", [P, H, P], WORK_AT + 4096)
        qi = place("qi", [P, H, P], WORK_AT + 6144)
        hn = qi
        C_p = place("C_p", [P, H, P + 1], WORK_AT + 8192)
        C_s = place("C_s", [P, H, P + 1], DQ_AT)
        ck = place("ck", [P, 8, 512], G_AT)
        cv = place("cv", [P, 8, 512], M_AT)
        ckT = place("ckT", [P, H, PAST], K_AT)
        prob = place("prob", [P, 2, 1056], K_AT + 16384)
        prob2 = place("prob2", [P, 2, 2, 512], K_AT + 16384)
        wdT = place("wdT", [P, 9, P], K_AT + 16384 + 8448)
        u_c = place("u_c", [P, 2, T + 2], K_AT)
        yc_l = place("yc_l", [P, 4, T], K_AT + up32(8 * (T + 2)), F32R)
        A_AT = K_AT + up32(8 * (T + 2)) + 16 * T
        on = place("on", [P, 2, P], A_AT)
        y_tmp = place("y_tmp", [P, 2, P], A_AT + 1024)
        junk = place("junk", [P, P], A_AT + 2048)
        assert A_AT + 2560 <= K_AT + 16384
        scb = place("scb", [P, 4, T], WORK_AT)
        ya_h, ya_l = place("ya_h", [P, 4, T], Q_AT, F32R), place("ya_l", [P, 4, T], G_AT, F32R)
        yb_h, yb_l = place("yb_h", [P, 4, T], WORK_AT, F32R), place("yb_l", [P, 4, T], G_AT + 16 * T, F32R)
        yc_h = place("yc_h", [P, 4, T], DQ_AT, F32R)
        merged = place("merged", [P, KD, T], M_AT)
        gate2 = place("gate2", [P, KD, T], G_AT)
        mg_h, mg_l = place("mg_h", [P, KD, T], M_AT, F32R), place("mg_l", [P, KD, T], G_AT, F32R)
        g_h = place("g_h", [P, JF, T], M_AT, F32R)
        g_l = place("g_l", [P, JF, T], M_AT + 4 * JF * T, F32R)
        FF_AT = M_AT + 8 * JF * T
        ups = place("ups", [P, 2, T + 2], FF_AT)
        acc = place("acc", [P, 2, 2, T], FF_AT + up32(8 * (T + 2)))
        ffn_last = place("ffn_last", [P, 2, 2, JU], FF_AT + up32(8 * (T + 2)) + 16 * T)
        assert FF_AT + up32(8 * (T + 2)) + 16 * T + 16 * JU <= END_AT
        Y_AT = H_AT + 2 * up32(4 * T)
        fst = place("fst", [P, 2, P], Y_AT)
        cst = place("cst", [16, P], Y_AT + 1024)
        yst = place("yst", [P, 4, DM], Y_AT + 1536)
        yst_s = place("yst_s", [TS, DM], Y_AT + 1536 + 16 * DM)
        norm_f_t = place("norm_f_t", [P, DM], Y_AT + 1536 + 20 * DM)
        assert Y_AT + 1536 + 24 * DM <= H_AT + 8 * KD * T

        sems = {}
        for nm in (
                "small_in late_in xs_in ck_in cv_in norm_f_in const_ready gates_zeroed "
                "dense_done act_drained dve_drained "
                "wh_ready wl_ready part_used "
                "sq_x rs_x sq_done sq_added norm_mm rs_sum rs_ready diag_ready rstd_mm rstd_ready "
                "hn_dve hh_act hl_dve hl_pool "
                "rows_act rows_dve ui_ready bd_ready "
                "ml_scores ml_w ml_qi ml_pt ml_kw ml_num ml_c ml_rd ml_ssq ml_rr ml_hn ml_ht ml_hm "
                "ck_tr ck_dve ck_act "
                "at_s at_mx at_exp at_wd at_tr at_wt at_o at_sq at_rr at_on at_ot at_yc "
                "lam_dve lam_act "
                "y_v y_h y_split yc_split yc_spare "
                "u_ready conv_kept "
                "merged_added merged_v merged_h merged_split "
                "hist_ready acc_ready conv_done th_ready silu_done g_ready gh_ready gl_ready "
                "y_tr y_copied y_dve y_act "
                "cst_ready out_k out_v out_m out_C state_out y_out "
                "dve_chain act_chain pool_chain").split():
            sems[nm] = sem(nm)
        x_in = [sem(f"x_in{c}") for c in range(4)]
        raw_in = [sem(f"raw_in{i}") for i in range(NRAW)]
        S = sems

        def wait_drained(eng, n):
            e, v = drained[n]
            eng.wait_ge(S[e + "_drained"], v)

        def wait_tmp_free(eng, key):
            if tmp_before[key]:
                name, v = tmp_before[key]
                eng.wait_ge(S[name], v)

        def tmp_of(key):
            return tmp[:, tmp_slot[key], :]

        def banks(n):
            i = buffer[n] % 2
            return (D if buffer[n] < 2 else X)[:, 2 * i:2 * i + 2, :]

        def dbuf(n):
            return banks(n)[:, :, 0:HALF]

        def two(ap):
            return ap.rearrange("p (a b) -> p a b", a=2)

        def src_tok(name, j):
            return {"mk": mkT[:, j, :], "mv": f_tmp[:, j % 2, :], "dk": dkT[:, j, :], "dv": f_tmp[:, j % 2, :]}[name]

        def raw_view(g):
            item, k0, m, c0 = GROUPS[g]
            slot = raw[:, ITEMS.index(item) % NRAW, :]
            if item[0] == "if":
                return slot[:, 0:KD * 2 * H].rearrange("p (k f) -> p k f", k=KD)
            width = {"pr": 512, "dn": P}.get(item[0], 256)
            kc = {"pr": 4, "dn": 11}.get(item[0], KD)
            return slot[:, 0:kc * width].rearrange("p (k f) -> p k f", k=kc)[:, k0:k0 + m, c0:c0 + P]

        def split_view(w, g):
            m, f = GROUPS[g][2], 36 if GROUPS[g][0][0] == "if" else P
            return w[:, g % NSPLIT, 0:m * f].rearrange("p (k f) -> p k f", k=m)

        def wait_raw(eng, g):
            i = ITEMS.index(GROUPS[g][0])
            eng.wait_ge(raw_in[i % NRAW], 16 * (i // NRAW + 1))

        def wait_split_slot(eng, g):
            if g >= NSPLIT:
                name, v = group_used[g - NSPLIT]
                eng.wait_ge(S[name], v)

        def splits(n):
            return range(first_group[n] + AHEAD, first_group.get(n + 1, len(GROUPS)) + AHEAD)

        block = ctx.enter_context(nc.Block())

        @block.sync
        def _(sp):
            for c in range(4):
                sp.dma_start(x_t[:, c, :], x_prompt[0, P * c:P * c + P, :]).then_inc(x_in[c], 16)
            def small(dst, src):
                sp.dma_start(dst, src).then_inc(S["small_in"], 16)

            blocks = lambda ap: ap.rearrange("(j f) -> j f", f=P)
            for i, item in enumerate(ITEMS):
                if i == 1:
                    small(small_a[0:8, :], blocks(norm1[0]))
                    small(small_a[8:16, :], blocks(norm2[0]))
                    small(small_a[16:28, :], w_sc_conv[0].rearrange("t (j f) -> (t j) f", f=P))
                    small(small_a[28:36, :], state_conv[0, 0].rearrange("t (j f) -> (t j) f", f=P))
                    small(small_a[36:40, :], ml_norm[0])
                    small(small_a[40:41, :], da_norm)
                    small(small_b[0:2 * JU, :], state_ffn[0, 0].rearrange("t (j f) -> (t j) f", f=P))
                    fc = w_fconv[0].rearrange("t (j f) -> (t j) f", f=P)
                    small(small_c[0:66, 0, :], fc[0:66, :])
                    small(small_c[0:66, 1, :], fc[66:132, :])
                if i >= NRAW:
                    v = last_group[ITEMS[i - NRAW]] + 1
                    sp.wait_ge(S["wh_ready"], v)
                    sp.wait_ge(S["wl_ready"], v)
                kind = item[0]
                rows, width = slice(0, DM), 256
                if kind == "if":
                    src, at, width = w_in[0], GATES_AT, 2 * H
                elif kind in W_IN_AT:
                    src, at = w_in[0], W_IN_AT[kind] + 256 * item[1]
                elif kind == "gt":
                    src, at = w_in[0], BRANCH_AT + DM * item[1] + 256 * item[2]
                elif kind == "pr":
                    src, at, width, rows = w_branch[0, item[1]], 512 * item[2], 512, slice(0, BW)
                elif kind == "wo":
                    src, at = w_out[0], 256 * item[1]
                elif kind == "up":
                    src, at = w_up[0], DFF * item[1] + 256 * item[2]
                else:
                    src, at, width, rows = w_down[0], P * item[1], P, slice(11 * P * item[2], 11 * P * (item[2] + 1))
                k = (rows.stop - rows.start) // P
                sp.dma_start(raw[:, i % NRAW, 0:k * width].rearrange("p (k f) -> p k f", k=k),
                             src[rows, at:at + width].rearrange("(k p) f -> p k f", p=P))\
                    .then_inc(raw_in[i % NRAW], 16)
            for i, c in enumerate((0, 2)):
                sp.wait_ge(S["y_dve"], i + 1)
                sp.dma_start(y_p[0, P * c:P * c + P, :], yst[:, c, :]).then_inc(S["y_out"], 16)
            sp.wait_ge(S["y_dve"], 3)
            sp.dma_start(y_s[0], yst_s[0:TS, :]).then_inc(S["y_out"], 16)
            sp.wait_ge(S["y_out"], 5 * 16)
            sp.wait_ge(S["out_k"], 32)
            sp.wait_ge(S["out_v"], 32)
            sp.wait_ge(S["out_m"], 32)
            sp.wait_ge(S["out_C"], 64)
            sp.wait_ge(S["state_out"], 64)

        @block.gpsimd
        def _(pool):
            g = nc.gpsimd
            chain = [0]

            def link(ins):
                chain[0] += 1
                ins.then_inc(S["pool_chain"], 1)
                pool.wait_ge(S["pool_chain"], chain[0])

            link(g.memset(ident, 0.0))
            g.affine_select(out=ident_r[:], in_=ident_r[:], compare_op=ALU.not_equal, fill=1.0, base=0,
                            pattern=[[-1, P]], channel_multiplier=1).then_inc(S["const_ready"], 1)
            g.memset(mean_w, 1.0 / DM).then_inc(S["const_ready"], 1)
            g.memset(xT[:, :, TP:S0], 0.0).then_inc(S["const_ready"], 1)
            link(g.memset(causal[:].bitcast(F32), 0.0))
            g.affine_select(out=causal[:], in_=causal[:], compare_op=ALU.is_ge, fill=NEG, base=0,
                            pattern=[[1, P]], channel_multiplier=-1).then_inc(S["const_ready"], 1)
            g.memset(m_half[:], -0.5).then_inc(S["const_ready"], 1)
            g.memset(ssx[:], 1.0).then_inc(S["const_ready"], 1)
            g.memset(C_p[:], 0.0).then_inc(S["const_ready"], 1)
            link(g.memset(sel[:], 0.0))
            g.affine_select(out=sel[0:H], in_=sel[0:H], compare_op=ALU.not_equal, fill=float(DM), base=0,
                            pattern=[[-1, H]], channel_multiplier=1).then_inc(S["const_ready"], 1)

            def block_diagonal(u):
                col, L = TILES[ML_ORDER[u]]
                if u >= 1:
                    pool.wait_ge(S["ml_scores"], u)
                for i, out in enumerate((bd_u, bd_i)):
                    last = g.tensor_tensor(out[:, :, 0:L],
                                           ui[:, i, col:col + L].bitcast(F32).unsqueeze(1).to_broadcast([36, H, L]),
                                           sel[:].unsqueeze(2).to_broadcast([36, H, L]), ALU.mult)
                last.then_inc(S["bd_ready"], 1)

            def rstd_small(x, scale, out, done):
                link(g.tensor_scalar(x, x, 1.0 / P, EPS, ALU.mult, ALU.add))
                link(g.tensor_tensor(x, x, m_half[0:x.shape[0], 0:1].to_broadcast(list(x.shape)), ALU.pow))
                g.tensor_tensor(out, x, scale, ALU.mult).then_inc(S[done], 1)

            def low_g(j):
                pool.wait_ge(S["gh_ready"], j + 1)
                g.tensor_tensor(g_l[:, j, :], acc[:, 0, j % 2, :], g_h[:, j, :].bitcast(F32), ALU.subtract)\
                    .then_inc(S["gl_ready"], 1)

            gates_h, gates_l = split_view(w_h, 0), split_view(w_l, 0)
            g.memset(gates_h[:, :, H:32].bitcast(F32), 0.0)
            g.memset(gates_l[:, :, H:32].bitcast(F32), 0.0).then_inc(S["gates_zeroed"], 1)

            for kind, a, n in ORDER:
                if kind == "xT":
                    c, L = a[0], TILES[a[0]][1]
                    pool.wait_ge(S["sq_x"], c + 1)
                    s = ssx[0:L, c:c + 1]
                    link(g.tensor_scalar(s, s, 1.0 / DM, EPS, ALU.mult, ALU.add))
                    g.tensor_tensor(s, s, m_half[0:L, 0:1], ALU.pow).then_inc(S["rs_x"], 1)
                elif kind == "rstd":
                    wait_raw(pool, 0)
                    pool.wait_ge(S["gates_zeroed"], 1)
                    pool.wait_ge(S["wh_ready"], 1)
                    for at, col in ((0, 0), (32, H)):
                        last = g.tensor_tensor(gates_l[:, :, at:at + H], raw_view(0)[:, :, col:col + H],
                                               gates_h[:, :, at:at + H].bitcast(F32), ALU.subtract)
                    last.then_inc(S["wl_ready"], 1)
                elif kind in ("wo", "dn") and a[0] < KD - 1:
                    r = {"wo": 1, "dn": 2}[kind]
                    done = (KD - 1) * (r - 1) + a[0]
                    pool.wait_ge(S["sq_done"], KD * (r - 1) + a[0] + 1)
                    if a[0] == 0:
                        g.tensor_copy(ssum[r][:], tmp_of(("sq", r, 0))).then_inc(S["sq_added"], 1)
                        if r == 1:
                            g.memset(ups[:, :, 0:2], 0.0).then_inc(S["conv_kept"], 1)
                    else:
                        pool.wait_ge(S["sq_added"], done)
                        g.tensor_tensor(ssum[r][:], ssum[r][:], tmp_of(("sq", r, a[0])), ALU.add)\
                            .then_inc(S["sq_added"], 1)
                elif kind == "ml" and a[0] == 0:
                    u, c = a[1], ML_ORDER[a[1]]
                    L = TILES[c][1]
                    pool.wait_ge(S["ml_w"], u + 1)
                    if u >= 1:
                        pool.wait_ge(S["ml_num"], u)
                    wait_drained(pool, block_of[("tok", ("mk", 3))])
                    g.tensor_tensor(kw[0:L], mk_tok[0:L, c], w_ml[0:L, :, L - 1:L].to_broadcast([L, H, P]),
                                    ALU.mult).then_inc(S["ml_kw"], 1)
                elif kind == "ml" and a[0] == 1:
                    u, c = a[1], ML_ORDER[a[1]]
                    L = TILES[c][1]
                    if u < 4:
                        block_diagonal(u + 1)
                    pool.wait_ge(S["ml_ssq"], u + 1)
                    rstd_small(ssq[0:L, :], rden[0:L, :], rr[0:L, :], "ml_rr")
                    if c >= 3:
                        pool.wait_ge(S["ml_c"], u + 1)
                        Cn, oC, on_ = (C_p, p_C, p_n) if c == 3 else (C_s, s_C, s_n)
                        pool.dma_start(oC[0, 0].rearrange("h d e -> d h e"), Cn[:, :, 0:P]).then_inc(S["out_C"], 16)
                        pool.dma_start(on_[0, 0].rearrange("h d -> d h").unsqueeze(2), Cn[:, :, P:P + 1],
                                       allow_slow_non_contiguous=True)\
                            .then_inc(S["out_C"], 16)
                elif kind == "tok" and a[0] in (("dk", 3), ("dv", 3)):
                    wait_drained(pool, n)
                    tok, op, os, so = (k_out, p_k, s_k, "out_k") if a[0][0] == "dk" else \
                        (dv_tok[:].rearrange("p c h d -> p c (h d)"), p_v, s_v, "out_v")
                    pool.dma_start(op[0, 0].rearrange("(c p) h d -> p c (h d)", p=P), tok[:, 0:4, :])\
                        .then_inc(S[so], 16)
                    pool.dma_start(os[0, 0].rearrange("t h d -> t (h d)"), tok[0:TS, 4, :]).then_inc(S[so], 16)
                elif kind == "gtr":
                    pool.wait_ge(S["ui_ready"], 1)
                    block_diagonal(0)
                    pool.wait_ge(S["rows_dve"], 6)
                    pool.dma_start(p_m[0, 0].unsqueeze(1), row["m"][:, TP - 1:TP],
                                   allow_slow_non_contiguous=True).then_inc(S["out_m"], 16)
                    pool.dma_start(s_m[0, 0].unsqueeze(1), row["m"][:, T - 1:T],
                                   allow_slow_non_contiguous=True).then_inc(S["out_m"], 16)
                elif kind == "sx":
                    j = a[0]
                    pool.wait_ge(S["u_ready"], j + 1)
                    g.tensor_copy(conv_last[:, 0, :, j], u_c[:, j % 2, TP:TP + 2])
                    g.tensor_copy(conv_last[:, 1, :, j], u_c[:, j % 2, T:T + 2]).then_inc(S["conv_kept"], 1)
                elif kind in ("mo", "sb"):
                    key, j = (kind, a[0]), a[0]
                    yh, yl = (ya_h, ya_l) if kind == "mo" else (yb_h, yb_l)
                    pool.wait_ge(S["y_h"], tmp_done[key][1])
                    g.tensor_tensor(yl[:, j, :], tmp_of(key), yh[:, j, :].bitcast(F32), ALU.subtract)\
                        .then_inc(S["y_split"], 1)
                elif kind == "pr" and a[0] == 2:
                    j = a[1]
                    pool.wait_ge(S["merged_h"], j + 1)
                    g.tensor_tensor(mg_l[:, j, :], tmp_of((kind, *a)), mg_h[:, j, :].bitcast(F32), ALU.subtract)\
                        .then_inc(S["merged_split"], 1)
                elif kind == "at" and a[0] == 2:
                    u = a[1]
                    pool.wait_ge(S["at_sq"], u + 1)
                    rstd_small(assq[:, u % 2:u % 2 + 1], rsum[:, u % 4, 0:1], arr[:, u % 2:u % 2 + 1], "at_rr")
                elif kind == "at" and a[0] == 3:
                    u = a[1]
                    h, i = (u - 1) // 4, (u - 1) % 4
                    pool.wait_ge(S["at_yc"], u + 1)
                    if u == 0:
                        src = y_tmp[:, 0, :].rearrange("p (h t) -> p h t", h=H)
                        yh, yl = yc_h[:, :, S0:T], yc_l[:, :, S0:T]
                    else:
                        src = y_tmp[:, u % 2, :]
                        yh, yl = (y[:, h, P * i:P * i + P] for y in (yc_h, yc_l))
                    link(g.tensor_copy(yh, src))
                    g.tensor_tensor(yl, src, yh.bitcast(F32), ALU.subtract).then_inc(S["yc_split"], 1)
                elif kind == "at" and a[0] == 0 and a[1] == 1:
                    for y in (yc_h, yc_l):
                        last = g.memset(y[:, :, TP:S0].bitcast(F32), 0.0)
                    last.then_inc(S["yc_spare"], 1)
                elif kind == "norm" and a[0] == 0:
                    for j in range(1, KD, 2):
                        pool.wait_ge(S["hh_act"], j + 1)
                        g.tensor_tensor(h_l[:, j, :], hn_x[:, j % 4, :], h_h[:, j, :].bitcast(F32), ALU.subtract)\
                            .then_inc(S["hl_pool"], 1)
                    g.memset(mv_tok[:, :, :, P:P + 1], 1.0).then_inc(S["const_ready"], 1)
                elif kind == "norm":
                    pool.wait_ge(S["rs_sum"], a[0])
                    g.tensor_tensor(ssx[:], ssx[:], m_half[:].to_broadcast([P, 5]), ALU.pow)\
                        .then_inc(S["rs_ready"], 1)
                elif kind == "up":
                    j, part = a
                    jj = j + JF * part
                    m = up_index[a]
                    buf = ups[:, m % 2, :]
                    wait_drained(pool, n)
                    g.tensor_copy(buf[:, S0:S0 + 2], hist[:, :, jj])
                    g.tensor_copy(ffn_last[:, 0, :, jj], buf[:, TP:TP + 2])
                    g.tensor_copy(ffn_last[:, 1, :, jj], buf[:, T:T + 2]).then_inc(S["hist_ready"], 1)
                    if m >= 1 and part_of[m - 1] == 1:
                        low_g(j_of[m - 1])
                elif kind == "last_g":
                    low_g(JF - 1)
                elif kind == "state":
                    pool.wait_ge(S["cst_ready"], 2)
                    pool.dma_start(p_ffn[0, 0].rearrange("r (j f) -> (r j) f", f=P), fst[0:2 * JU, 0, :])\
                        .then_inc(S["state_out"], 16)
                    pool.dma_start(s_ffn[0, 0].rearrange("r (j f) -> (r j) f", f=P), fst[0:2 * JU, 1, :])\
                        .then_inc(S["state_out"], 16)
                    pool.dma_start(p_conv[0, 0].rearrange("r (j f) -> (r j) f", f=P), cst[0:8, :])\
                        .then_inc(S["state_out"], 16)
                    pool.dma_start(s_conv[0, 0].rearrange("r (j f) -> (r j) f", f=P), cst[8:16, :])\
                        .then_inc(S["state_out"], 16)

        @block.scalar
        def _(act):
            sc = nc.scalar
            chain = [0]

            def link(ins):
                chain[0] += 1
                ins.then_inc(S["act_chain"], 1)
                act.wait_ge(S["act_chain"], chain[0])

            act.dma_start(x_s[0:TS, :], x_sample[0]).then_inc(S["xs_in"], 16)
            act.wait_ge(S["const_ready"], 8)
            for c, (_, L) in enumerate(TILES):
                act.wait_ge(x_in[c] if c < 4 else S["xs_in"], 16)
                if c >= 1:
                    act.wait_ge(S["sq_x"], c)
                sc.activation(tmp[0:L].rearrange("p a b -> p (a b)")[:, 0:DM],
                              x_t[:, c, :] if c < 4 else x_s[0:TS, :], ACT.Square, accum_out=ssx[0:L, c:c + 1]).then_inc(S["sq_x"], 1)

            def late(dst, src):
                act.dma_start(dst, src, allow_slow_non_contiguous=True).then_inc(S["late_in"], 16)

            late(b_i[:], b_if[0, 0].unsqueeze(1))
            late(b_f[:], b_if[0, 1].unsqueeze(1))
            late(m_s[:], state_m[0, 0].unsqueeze(1))
            late(lam_t[:], da_lambda[0].rearrange("(a b) f -> a b f", a=2).unsqueeze(0).to_broadcast([P, 2, 2, 64]))
            late(C_s[:, :, 0:P], state_C[0, 0].rearrange("h d e -> d h e"))
            late(C_s[:, :, P:P + 1], state_n[0, 0].rearrange("h d -> d h").unsqueeze(2))

            def split(g):
                wait_raw(act, g)
                wait_split_slot(act, g)
                src, dst = raw_view(g), split_view(w_h, g)
                if GROUPS[g][0][0] == "if":
                    sc.activation(dst[:, :, 0:H], src[:, :, 0:H], ACT.Copy)
                    sc.activation(dst[:, :, 32:36], src[:, :, H:2 * H], ACT.Copy).then_inc(S["wh_ready"], 1)
                else:
                    sc.activation(dst, src, ACT.Copy).then_inc(S["wh_ready"], 1)

            def high_g(j):
                act.wait_ge(S["g_ready"], j + 1)
                sc.activation(g_h[:, j, :], acc[:, 0, j % 2, :], ACT.Copy).then_inc(S["gh_ready"], 1)

            for g in range(AHEAD):
                split(g)

            def square_block(r, j, n):
                wait_drained(act, n)
                wait_tmp_free(act, ("sq", r, j))
                sc.activation(tmp_of(("sq", r, j)), xT[:, j, :], ACT.Square).then_inc(S["sq_done"], 1)

            for kind, a, n in ORDER:
                if n is not None:
                    for g in splits(n):
                        if g < len(GROUPS):
                            split(g)
                if kind == "rstd" or (kind == "norm" and a[0] == 1):
                    if kind == "rstd":
                        act.wait_ge(S["dense_done"], n + 1)
                        r, src, done = 0, banks(n), "act_drained"
                    else:
                        act.wait_ge(S["rstd_mm"], 1)
                        r, src, done = 1, X[:, 2:4, :], "rstd_ready"
                    sc.activation(rstd[r][:, 0:TP], src[:, 0, :], ACT.Copy, scale=float(DM))
                    sc.activation(rstd[r][:, S0:T], src[:, 1, 0:TS], ACT.Copy, scale=float(DM)).then_inc(S[done], 1)
                elif kind == "lam":
                    act.wait_ge(S["lam_dve"], 2)
                    sc.activation(lam_e[:], lam_e[:], ACT.Exp).then_inc(S["lam_act"], 1)
                elif kind == "wo":
                    j = a[0]
                    wait_drained(act, n)
                    sc.activation(h_h[:, j, :], xT[:, j, :], ACT.Copy, scale=vec[:, KD + j:KD + j + 1])\
                        .then_inc(S["hh_act"], 1)
                    square_block(1, j, n)
                elif kind == "dn":
                    square_block(2, a[0], n)
                elif kind == "norm" and a[0] == 0:
                    for j in range(KD):
                        act.wait_ge(S["hn_dve"], j + 1)
                        sc.activation(h_h[:, j, :], hn_x[:, j % 4, :], ACT.Copy).then_inc(S["hh_act"], 1)
                elif kind == "scale":
                    act.wait_ge(S["rs_ready"], 2)
                    act.wait_ge(S["y_copied"], KD)
                    for i, c in enumerate((1, 3)):
                        sc.activation(yst[:, c, :], yst[:, c, :], ACT.Copy, scale=ssx[:, c:c + 1])\
                            .then_inc(S["y_act"], 1)
                        act.wait_ge(S["y_act"], i + 1)
                        act.dma_start(y_p[0, P * c:P * c + P, :], yst[:, c, :]).then_inc(S["y_out"], 16)
                elif kind == "if":
                    act.wait_ge(S["dense_done"], n + 1)
                    act.wait_ge(S["late_in"], 6 * 16)
                    sc.activation(two(row["ig"]), dbuf(n)[0:H], ACT.Identity, bias=b_i[:])
                    sc.activation(two(row["lf"]), dbuf(n)[32:32 + H], ACT.Copy).then_inc(S["act_drained"], 1)
                elif kind == "rows" and a[0] == 0:
                    act.wait_ge(S["rows_dve"], 1)
                    link(sc.activation(row["g"], row["lf"], ACT.Abs))
                    link(sc.activation(row["g"], row["g"], ACT.Exp, scale=-1.0))
                    sc.activation(row["g"], row["g"], ACT.Ln, bias=1.0).then_inc(S["rows_act"], 1)
                elif kind == "rows" and a[0] == 2:
                    act.wait_ge(S["rows_dve"], 7)
                    sc.activation(row["em"], row["m"], ACT.Exp, scale=-1.0)
                    sc.activation(row["inter"][:, 0:P], row["u"][:, 0:P], ACT.Exp)
                    for col, L in TILES[1:4]:
                        sc.activation(row["inter"][:, col:col + L], row["u"][:, col:col + L], ACT.Exp,
                                      bias=row["m"][:, col - 1:col])
                    sc.activation(row["inter"][:, S0:T], row["u"][:, S0:T], ACT.Exp, bias=m_s[:])\
                        .then_inc(S["rows_act"], 1)
                elif kind in ("mk", "mq", "mv", "dk", "dv", "dq", "sc"):
                    j = a[0]
                    act.wait_ge(S["dense_done"], n + 1)
                    if kind in ("mv", "dv"):
                        if (kind, j) == ("mv", 0):
                            wait_drained(act, block_of[("small",)])
                            act.wait_ge(S["lam_dve"], 3)
                        elif j >= 2:
                            act.wait_ge(S["dense_done"], block_of[("tok", (kind, j - 2))] + 1)
                    if (kind, j) in (("dq", 0), ("sc", 0)):
                        act.wait_ge(S["out_C"], 32 if kind == "dq" else 64)
                    dst = {"mk": mkT, "mq": mqT, "dk": dkT, "dq": dqT, "sc": scb}.get(kind)
                    dst = f_tmp[:, j % 2, :] if dst is None else dst[:, j, :]
                    scale = {"mk": P ** -0.5, "dq": 64 ** -0.5}.get(kind, 1.0)
                    sc.activation(two(dst), dbuf(n), ACT.Copy, scale=scale).then_inc(S["act_drained"], 1)
                elif kind == "ml":
                    stage, u = a
                    c = ML_ORDER[u]
                    col, L = TILES[c]
                    if stage == 0:
                        act.wait_ge(S["ml_scores"], u + 1)
                        wait_drained(act, block_of[("gtr", 0)])
                        if u >= 1:
                            act.wait_ge(S["ml_pt"], u)
                            act.wait_ge(S["ml_kw"], u)
                        for h in range(H):
                            last = sc.activation(w_ml[0:L, h, 0:L], X[0:L, 0, P * h:P * h + L], ACT.Exp,
                                                 bias=gT[0:L, c, h:h + 1])
                        last.then_inc(S["ml_w"], 1)
                    elif stage == 1:
                        act.wait_ge(S["ml_rd"], u + 1)
                        for h in range(H):
                            last = sc.activation(ml_junk[0:L, P * h:P * h + P],
                                                 X[0:L, h // 2, 129 * (h % 2):129 * (h % 2) + P], ACT.Square,
                                                 scale=rden[0:L, h:h + 1], accum_out=ssq[0:L, h:h + 1])
                        last.then_inc(S["ml_ssq"], 1)
                    else:
                        act.wait_ge(S["ml_ht"], u + 1)
                        for h in range(H):
                            last = sc.activation(mqT[:, h, col:col + L], X[:, 3, P * h:P * h + L], ACT.Copy,
                                                 scale=vec[:, 36 + h:37 + h])
                        last.then_inc(S["ml_hm"], 1)
                        if u == 4:
                            act.wait_ge(S["ml_hm"], 5)
                            act.wait_ge(S["out_m"], 32)
                            act.dma_start(ck[:], cache_k[0, 0].rearrange("(b p) h d -> p b (h d)", p=P))\
                                .then_inc(S["ck_in"], 16)
                            act.wait_ge(S["out_k"], 32)
                            act.wait_ge(S["dense_done"], block_of[("tok", ("dv", 3))] + 1)
                            act.dma_start(cv[:], cache_v[0, 0].rearrange("(b p) h d -> p b (h d)", p=P))\
                                .then_inc(S["cv_in"], 16)
                elif kind == "ck":
                    act.wait_ge(S["ck_tr"], a[0] + 1)
                    sc.activation(ckT[:, 2 * a[0] + 1, :].rearrange("p (a b) -> p a b", a=2), X[:, 2:4, :],
                                  ACT.Copy).then_inc(S["ck_act"], 1)
                elif kind == "sample":
                    c = a[0]
                    act.wait_ge(S["at_mx"], c + 1)
                    sc.activation(prob[:, c, :], X[:].rearrange("p a b -> p (a b)")[:, 0:1056], ACT.Exp,
                                  bias=nmax[:, 0, c:c + 1], accum_out=psum_p[:, 0, c:c + 1]).then_inc(S["at_exp"], 1)
                elif kind == "at":
                    stage, u = a
                    h, i = (u - 1) // 4, (u - 1) % 4
                    nk = P * (i + 1)
                    if stage == 0:
                        act.wait_ge(S["at_mx"], u + 2)
                        if u >= 2:
                            act.wait_ge(S["at_tr"], u - 1)
                        for c in range(2):
                            last = sc.activation(prob2[:, u % 2, c, 0:nk], X[:, c, 0:nk], ACT.Exp,
                                                 bias=nmax[:, u % 2, c:c + 1], accum_out=psum_p[:, u % 2, c:c + 1])
                        last.then_inc(S["at_exp"], 1)
                    elif stage == 1:
                        act.wait_ge(S["at_tr"], u + 1)
                        if u == 0:
                            sc.activation(wdT[:, 0:8, :].rearrange("p a b -> p (a b)"),
                                          X[:].rearrange("p a b -> p (a b)")[:, 0:1024], ACT.Copy)
                            sc.activation(wdT[0:TS, 8, :], X[0:TS, 2, 0:P], ACT.Copy).then_inc(S["at_wt"], 1)
                        else:
                            act.wait_ge(S["at_o"], max(u - 1, 1))
                            sc.activation(wdT[:, 4 * (u % 2):4 * (u % 2) + i + 1, :].rearrange("p a b -> p (a b)"),
                                          X[:, 2, 0:nk], ACT.Copy).then_inc(S["at_wt"], 1)
                    elif stage == 2:
                        act.wait_ge(S["at_o"], u + 1)
                        sc.activation(junk[:], X[:, 3, 0:P], ACT.Square, scale=rsum[:, u % 4, 0:1],
                                      accum_out=assq[:, u % 2:u % 2 + 1]).then_inc(S["at_sq"], 1)
                    else:
                        act.wait_ge(S["at_ot"], u + 1)
                        if u >= 2:
                            act.wait_ge(S["yc_split"], u - 1)
                        sc.activation(y_tmp[:, u % 2, :], X[:, 2, 0:P], ACT.Copy, scale=vec[:, 40:41])\
                            .then_inc(S["at_yc"], 1)
                elif kind == "sb" or (kind == "pr" and a[0] == 2):
                    src = tmp_of((kind, *a))
                    if kind == "sb":
                        wait_drained(act, n)
                        sc.activation(yb_h[:, a[0], :], src, ACT.Copy).then_inc(S["y_h"], 1)
                    else:
                        act.wait_ge(S["merged_v"], a[1] + 1)
                        sc.activation(mg_h[:, a[1], :], src, ACT.Copy).then_inc(S["merged_h"], 1)
                elif kind in ("mo", "gt"):
                    act.wait_ge(S["dense_done"], n + 1)
                    if kind == "gt" and a[0] == 2:
                        if a[1] == 0:
                            act.wait_ge(S["dense_done"], block_of[("pr", 1, KD - 1)] + 1)
                        sc.activation(two(gate2[:, a[1], :]), dbuf(n), ACT.Tanh, scale=0.5)\
                            .then_inc(S["act_drained"], 1)
                    else:
                        tk = tmp_of((kind, *a))
                        wait_tmp_free(act, (kind, *a))
                        sc.activation(two(tk), dbuf(n), ACT.Tanh, scale=0.5)\
                            .then_inc(S["act_drained"], 1)
                        if kind == "mo":
                            act.wait_ge(S["y_v"], a[0] + 1)
                            if a[0] == 0:
                                act.wait_ge(S["ck_tr"], 2)
                            sc.activation(ya_h[:, a[0], :], tk, ACT.Copy).then_inc(S["y_h"], 1)
                elif kind == "up":
                    j, part = a
                    jj = j + JF * part
                    m = up_index[a]
                    act.wait_ge(S["hist_ready"], m + 1)
                    if j >= 2:
                        act.wait_ge(S["gl_ready"], j - 1)
                    sc.activation(acc[:, part, j % 2, :], ups[:, m % 2, 2:T + 2], ACT.Copy, scale=fcw[:, 2, jj:jj + 1])\
                        .then_inc(S["acc_ready"], 1)
                    if part == 1:
                        act.wait_ge(S["conv_done"], up_index[(j, 0)] + 1)
                        wait_tmp_free(act, ("up", j))
                        sc.activation(tmp_of(("up", j)), acc[:, 0, j % 2, :], ACT.Tanh, scale=0.5)\
                            .then_inc(S["th_ready"], 1)
                    if m >= 1 and part_of[m - 1] == 1:
                        high_g(j_of[m - 1])
                elif kind == "last_g":
                    high_g(JF - 1)
                    act.wait_ge(S["dense_done"], block_of[("up", JF - 1, 1)] + 1)
                    act.dma_start(norm_f_t[:], norm_f.unsqueeze(0).to_broadcast([P, DM])).then_inc(S["norm_f_in"], 16)

        @block.vector
        def _(dve):
            v = nc.vector
            chain = [0]

            def link(ins):
                chain[0] += 1
                ins.then_inc(S["dve_chain"], 1)
                dve.wait_ge(S["dve_chain"], chain[0])

            def split(g):
                wait_raw(dve, g)
                wait_split_slot(dve, g)
                src, hi, lo = raw_view(g), split_view(w_h, g), split_view(w_l, g)
                dve.wait_ge(S["wh_ready"], g + 1)
                if g == 1:
                    dve.wait_ge(S["wl_ready"], 1)
                v.tensor_tensor(lo, src, hi.bitcast(F32), ALU.subtract).then_inc(S["wl_ready"], 1)

            def combine(u, p0, p1):
                s = psum_p[:, u % 2, :]
                dve.wait_ge(S["at_exp"], u + 2)
                if u == 0:
                    dve.wait_ge(S["lam_dve"], 3)
                link(v.reciprocal(rsum[:, u % 4, :], s))
                link(v.scalar_tensor_tensor(out=kap[:], in0=s[:, 0:1], scalar=rsum[:, u % 4, 1:2], in1=neg_lam[:],
                                            op0=ALU.mult, op1=ALU.mult))
                v.scalar_tensor_tensor(out=p0, in0=p1, scalar=kap[:], in1=p0, op0=ALU.mult, op1=ALU.add)\
                    .then_inc(S["at_wd"], 1)

            for kind, a, n in ORDER:
                B = None if n is None else banks(n)
                if n is not None:
                    for g in splits(n):
                        if g < len(GROUPS):
                            split(g)
                if kind == "small":
                    v.memset(rstd[0][:, TP:S0], 0.0)
                    dve.wait_ge(S["dense_done"], n + 1)
                    link(v.tensor_copy(vec[:], B[:, 0, 0:41]))
                    link(v.tensor_scalar(vec[:, 36:40], vec[:, 36:40], 0.5, None, ALU.mult))
                    link(v.tensor_scalar(vec[:, 40:41], vec[:, 40:41], 1.0 - LAM_INIT, None, ALU.mult))
                    v.tensor_copy(hist[:].rearrange("p a b -> p (a b)"), B[:, 0, 41:41 + 2 * JU])
                    v.tensor_copy(fcw[:].rearrange("p a b -> p (a b)"), B[:, 1, 0:3 * JU])\
                        .then_inc(S["dve_drained"], 1)
                elif kind == "lam":
                    dve.wait_ge(S["late_in"], 6 * 16)
                    link(v.tensor_tensor(lam_p[:], lam_t[:, :, 0, :], lam_t[:, :, 1, :], ALU.mult))
                    v.reduce_sum(lam_e[:], lam_p[:], axis=AX.X).then_inc(S["lam_dve"], 2)
                    dve.wait_ge(S["lam_act"], 1)
                    link(v.tensor_scalar(neg_lam[:], lam_e[:, 1:2], -LAM_INIT, None, ALU.add))
                    v.tensor_tensor(neg_lam[:], neg_lam[:], lam_e[:, 0:1], ALU.subtract).then_inc(S["lam_dve"], 1)
                elif kind == "xT":
                    dve.wait_ge(S["dense_done"], n + 1)
                    c, (col, L) = a[0], TILES[a[0]]
                    v.tensor_copy(xT[:, :, col:col + L].rearrange("p (a j) t -> p a j t", a=2),
                                  B.rearrange("p a (j t) -> p a j t", j=4)[:, :, :, 0:L])\
                        .then_inc(S["dve_drained"], 1)
                    dve.wait_ge(S["rs_x"], c + 1)
                    v.tensor_scalar(diag[0:L, c, 0:L], ident[0:L, 0:L], ssx[0:L, c:c + 1], None, ALU.mult)\
                        .then_inc(S["diag_ready"], 1)
                elif kind == "norm" and a[0] == 0:
                    wait_drained(dve, block_of[("rstd",)])

                    def low(j):
                        dve.wait_ge(S["hh_act"], j + 1)
                        v.tensor_tensor(h_l[:, j, :], hn_x[:, j % 4, :], h_h[:, j, :].bitcast(F32), ALU.subtract)\
                            .then_inc(S["hl_dve"], 1)

                    for j in range(KD):
                        if j >= 4:
                            dve.wait_ge(S["hl_pool" if j % 2 else "hl_dve"], (j - 4) // 2 + 1)
                        v.scalar_tensor_tensor(out=hn_x[:, j % 4, :], in0=xT[:, j, :], scalar=vec[:, j:j + 1],
                                               in1=rstd[0], op0=ALU.mult, op1=ALU.mult).then_inc(S["hn_dve"], 1)
                        if j % 2 == 0 and j >= 2:
                            low(j - 2)
                    low(KD - 2)
                    for g in range(1, AHEAD):
                        split(g)
                elif kind == "norm":
                    r = a[0]
                    M = X[:, 0:2] if r == 1 else dbuf(block_of[("dn", KD - 2)])
                    dve.wait_ge(S["norm_mm"], 2 * r - 1)
                    v.tensor_scalar(ssx[:, 0:4], M[:, 0, 0:4], EPS, None, ALU.add)
                    link(v.tensor_scalar(ssx[0:TS, 4:5], M[0:TS, 0, 4:5], EPS, None, ALU.add))
                    dve.wait_ge(S["norm_mm"], 2 * r)
                    if r == 1:
                        v.memset(rstd[1][:, TP:S0], 0.0)
                    v.tensor_tensor(ssx[:, 0:4], ssx[:, 0:4], M[:, 1, 0:4], ALU.add)
                    v.tensor_tensor(ssx[0:TS, 4:5], ssx[0:TS, 4:5], M[0:TS, 1, 4:5], ALU.add)\
                        .then_inc(S["rs_sum"], 1)
                    if r == 1:
                        dve.wait_ge(S["rs_ready"], 1)
                        for c, (_, L) in enumerate(TILES):
                            v.tensor_scalar(diag[0:L, c, 0:L], ident[0:L, 0:L], ssx[0:L, c:c + 1], None, ALU.mult)\
                                .then_inc(S["diag_ready"], 1)
                elif kind == "scale":
                    dve.wait_ge(S["rs_ready"], 2)
                    dve.wait_ge(S["y_copied"], KD)
                    for c in (0, 2):
                        v.tensor_scalar(yst[:, c, :], yst[:, c, :], ssx[:, c:c + 1], None, ALU.mult)\
                            .then_inc(S["y_dve"], 1)
                    v.tensor_scalar(yst_s[0:TS], yst_s[0:TS], ssx[0:TS, 4:5], None, ALU.mult)\
                        .then_inc(S["y_dve"], 1)
                elif kind == "yT":
                    j, x = a[0], 2 * (a[0] % 2)
                    dve.wait_ge(S["y_tr"], j + 1)
                    if j == 0:
                        dve.wait_ge(S["norm_f_in"], 16)
                    w = norm_f_t[:, P * j:P * j + P]
                    v.tensor_tensor(yst[:, :, P * j:P * j + P], X[:, x, :].rearrange("p (c f) -> p c f", c=4),
                                    w.unsqueeze(1).to_broadcast([P, 4, P]), ALU.mult)
                    v.tensor_tensor(yst_s[0:TS, P * j:P * j + P], X[0:TS, x + 1, 0:P], w[0:TS], ALU.mult)\
                        .then_inc(S["y_copied"], 1)
                elif kind == "if":
                    wait_drained(dve, n)
                    v.tensor_scalar(row["lf"], row["lf"], b_f[:], None, ALU.add).then_inc(S["rows_dve"], 1)
                    v.memset(row["inter"][:, TP:S0], 0.0)
                    link(v.memset(row["em"], 1.0))
                    for col, _ in TILES:
                        last = v.memset(row["em"][:, col:col + 1], 0.0)
                    last.then_inc(S["rows_dve"], 1)
                elif kind == "rows" and a[0] == 1:
                    dve.wait_ge(S["rows_act"], 1)
                    dve.wait_ge(S["rows_dve"], 2)
                    v.scalar_tensor_tensor(out=row["lf"], in0=row["lf"], scalar=0.0, in1=row["g"], op0=ALU.min,
                                           op1=ALU.subtract).then_inc(S["rows_dve"], 1)
                    dve.wait_ge(S["rows_dve"], 3)
                    v.tensor_tensor_scan(row["cum"], row["em"], row["lf"], 0.0, ALU.mult, ALU.add)
                    v.memset(row["m"][:, TP:S0], 0.0)
                    v.tensor_tensor_scan(row["m"][:, 0:TP], row["lf"][:, 0:TP], row["ig"][:, 0:TP], 0.0,
                                         ALU.add, ALU.max).then_inc(S["rows_dve"], 2)
                    v.tensor_tensor_scan(row["m"][:, S0:T], row["lf"][:, S0:T], row["ig"][:, S0:T], m_s[:],
                                         ALU.add, ALU.max).then_inc(S["rows_dve"], 1)
                    dve.wait_ge(S["rows_dve"], 6)
                    v.tensor_tensor(row["g"], row["ig"], row["cum"], ALU.subtract)
                    v.tensor_tensor(row["u"], row["cum"], row["m"], ALU.subtract).then_inc(S["rows_dve"], 1)
                    dve.wait_ge(S["rows_dve"], 7)
                    v.memset(ui[:].bitcast(F32), 0.0)
                    link(v.tensor_copy(sel[32:36], sel[0:H]))
                elif kind == "rows" and a[0] == 2:
                    dve.wait_ge(S["rows_act"], 2)
                    v.tensor_copy(ui[0:H, 0, :], row["u"])
                    link(v.tensor_copy(ui[0:H, 1, :], row["inter"]))
                    for i, nm in enumerate(("u", "inter")):
                        last = v.tensor_tensor(ui[32:36, i, :], row[nm], ui[0:H, i, :].bitcast(F32), ALU.subtract)
                    last.then_inc(S["ui_ready"], 1)
                elif kind == "tok":
                    name, j = a[0]
                    dve.wait_ge(S["dense_done"], n + 1)
                    if name == "dv" or name == "mv":
                        dst = (mv_tok if name == "mv" else dv_tok)[:, :, j, 0:P]
                    elif name == "mk":
                        dst = mk_tok[:, :, j, :]
                    else:
                        dst = k_out[:, :, P * j:P * j + P]
                    v.tensor_copy(dst[:, 0:4, :], B[:, 0, :].rearrange("p (c f) -> p c f", c=4))
                    v.tensor_copy(dst[0:TS, 4, :], B[0:TS, 1, 0:P]).then_inc(S["dve_drained"], 1)
                elif kind == "gtr":
                    dve.wait_ge(S["dense_done"], n + 1)
                    for t, s in ((gT, 0), (emT, 1)):
                        v.tensor_copy(t[:, 0:4, :], B[:, s, 0:16].rearrange("p (c h) -> p c h", c=4))
                        last = v.tensor_copy(t[0:TS, 4, :], B[0:TS, s, 16:20])
                    last.then_inc(S["dve_drained"], 1)
                elif kind == "ml":
                    stage, u = a
                    c = ML_ORDER[u]
                    col, L = TILES[c]
                    C = C_p if c < 4 else C_s
                    if stage == 0:
                        dve.wait_ge(S["ml_scores"], u + 1)
                        if u >= 1:
                            dve.wait_ge(S["ml_ht"], u)
                        inter = X[:, 2, :].rearrange("p (h t) -> p h t", h=H)
                        v.tensor_tensor(qi[:, :, 0:L], mqT[:, :, col:col + L], inter[:, :, 0:L], ALU.mult)
                        v.tensor_copy(il[:], inter[:, :, L - 1]).then_inc(S["ml_qi"], 1)
                        dve.wait_ge(S["ml_w"], u + 1)
                        scores = X[:, 1, :].rearrange("p (h t) -> p h t", h=H)
                        v.tensor_tensor(p_ml[0:L, :, 0:L], w_ml[0:L, :, 0:L], scores[0:L, :, 0:L], ALU.mult)\
                            .then_inc(S["ml_pt"], 1)
                    elif stage == 1:
                        dve.wait_ge(S["ml_num"], u + 1)
                        num = X[0:L, 0:2, 0:2 * (P + 1)].rearrange("p a (b e) -> p a b e", b=2)
                        den2 = den[0:L, :].rearrange("p (a b) -> p a b", a=2)
                        em2 = emT[0:L, c, :].rearrange("p (a b) -> p a b", a=2)
                        link(v.scalar_tensor_tensor(out=den2, in0=num[:, :, :, P], scalar=-1.0, in1=em2,
                                                    op0=ALU.mult, op1=ALU.max))
                        link(v.scalar_tensor_tensor(out=den2, in0=num[:, :, :, P], scalar=1.0, in1=den2,
                                                    op0=ALU.mult, op1=ALU.max))
                        v.reciprocal(rden[0:L, :], den[0:L, :]).then_inc(S["ml_rd"], 1)
                        dve.wait_ge(S["ml_qi"], u + 1)
                        for h in range(H):
                            last = v.scalar_tensor_tensor(out=C[:, h, :], in0=C[:, h, :], scalar=il[:, h:h + 1],
                                                          in1=X[:, 2 + h // 2, 129 * (h % 2):129 * (h % 2) + 129],
                                                          op0=ALU.mult, op1=ALU.add)
                        last.then_inc(S["ml_c"], 1)
                        dve.wait_ge(S["ml_rr"], u + 1)
                        rr2 = rr[0:L, :].rearrange("p (a b) -> p a b", a=2).unsqueeze(3).to_broadcast([L, 2, 2, P])
                        v.tensor_tensor(hn[0:L].rearrange("p (a b) e -> p a b e", a=2), num[:, :, :, 0:P], rr2,
                                        ALU.mult).then_inc(S["ml_hn"], 1)
                elif kind == "ck":
                    dve.wait_ge(S["ck_tr"], a[0] + 1)
                    v.tensor_copy(ckT[:, 2 * a[0], :].rearrange("p (a b) -> p a b", a=2), X[:, 0:2, :])\
                        .then_inc(S["ck_dve"], 1)
                elif kind == "sample":
                    c = a[0]
                    dve.wait_ge(S["at_s"], c + 1)
                    v.tensor_reduce(nmax[:, 0, c:c + 1], X[:].rearrange("p a b -> p (a b)")[:, 0:1056], AX.X, ALU.max,
                                    negate=True).then_inc(S["at_mx"], 1)
                    if c == 1:
                        combine(0, prob[:, 0, :], prob[:, 1, :])
                elif kind == "at":
                    stage, u = a
                    if stage == 0:
                        nk = P * ((u - 1) % 4 + 1)
                        dve.wait_ge(S["at_s"], u + 2)
                        v.tensor_reduce(nmax[:, u % 2, :], X[:, 0:2, 0:nk], AX.X, ALU.max, negate=True)\
                            .then_inc(S["at_mx"], 1)
                        combine(u, prob2[:, u % 2, 0, 0:nk], prob2[:, u % 2, 1, 0:nk])
                    elif stage == 2:
                        dve.wait_ge(S["at_rr"], u + 1)
                        if u >= 2:
                            dve.wait_ge(S["at_ot"], u - 1)
                        v.tensor_scalar(on[:, u % 2, :], X[:, 3, 0:P], arr[:, u % 2:u % 2 + 1], None, ALU.mult)\
                            .then_inc(S["at_on"], 1)
                elif kind == "mo":
                    tk = tmp_of(("mo", a[0]))
                    wait_drained(dve, n)
                    dve.wait_ge(S["ml_hm"], 5)
                    v.scalar_tensor_tensor(out=tk, in0=tk, scalar=1.0, in1=mqT[:, a[0], :],
                                           op0=ALU.add, op1=ALU.mult).then_inc(S["y_v"], 1)
                elif kind == "sx":
                    j = a[0]
                    dve.wait_ge(S["dense_done"], n + 1)
                    wait_drained(dve, block_of[("sc", j)])
                    u = u_c[:, j % 2, :]
                    if j >= 2:
                        dve.wait_ge(S["conv_kept"], j - 1)
                    v.memset(u[:, 0:2], 0.0)
                    v.tensor_tensor(two(u[:, 2:T + 2]), dbuf(n), two(scb[:, j, :]), ALU.mult)\
                        .then_inc(S["dve_drained"], 1)
                    wait_drained(dve, n)
                    link(v.tensor_copy(u[:, S0:S0 + 2], vec[:, 28:36].rearrange("p (r j) -> p r j", r=2)[:, :, j]))
                    w = lambda t: vec[:, 16 + 4 * t + j:17 + 4 * t + j]
                    v.tensor_scalar(scb[:, j, :], u[:, 0:T], w(0), None, ALU.mult).then_inc(S["u_ready"], 1)
                    dve.wait_ge(S["u_ready"], j + 1)
                    link(v.scalar_tensor_tensor(out=scb[:, j, :], in0=u[:, 1:T + 1], scalar=w(1), in1=scb[:, j, :],
                                                op0=ALU.mult, op1=ALU.add))
                    link(v.scalar_tensor_tensor(out=scb[:, j, :], in0=u[:, 2:T + 2], scalar=w(2), in1=scb[:, j, :],
                                                op0=ALU.mult, op1=ALU.add))
                elif kind == "sb":
                    dve.wait_ge(S["dense_done"], n + 1)
                    wait_tmp_free(dve, ("sb", a[0]))
                    v.tensor_tensor(two(tmp_of(("sb", a[0]))), dbuf(n), two(scb[:, a[0], :]), ALU.mult)\
                        .then_inc(S["dve_drained"], 1)
                elif kind == "pr":
                    br, j = a
                    dve.wait_ge(S["dense_done"], n + 1)
                    if br == 2:
                        g = gate2[:, j, :]
                    else:
                        g = tmp_of(("gt", br, j))
                    wait_drained(dve, block_of[("gt", br, j)])
                    if br == 0 and j == 0:
                        dve.wait_ge(S["at_o"], 1)
                    out = merged[:, j, :] if br == 0 else g
                    v.scalar_tensor_tensor(out=two(out), in0=two(g), scalar=1.0, in1=dbuf(n), op0=ALU.add,
                                           op1=ALU.mult).then_inc(S["dve_drained"], 1)
                    if br == 1:
                        wait_drained(dve, n)
                        v.tensor_tensor(merged[:, j, :], merged[:, j, :], g, ALU.add).then_inc(S["merged_added"], 1)
                    elif br == 2:
                        wait_drained(dve, n)
                        wait_tmp_free(dve, ("pr", 2, j))
                        v.tensor_tensor(tmp_of(("pr", 2, j)), merged[:, j, :], g, ALU.add).then_inc(S["merged_v"], 1)
                elif kind in ("wo", "dn"):
                    dve.wait_ge(S["dense_done"], n + 1)
                    v.scalar_tensor_tensor(out=two(xT[:, a[0], :]), in0=dbuf(n), scalar=0.5, in1=two(xT[:, a[0], :]),
                                           op0=ALU.mult, op1=ALU.add).then_inc(S["dve_drained"], 1)
                    if kind == "wo":
                        for j in {0: [], KD - 1: [KD - 2, KD - 1]}.get(a[0], [a[0] - 1]):
                            dve.wait_ge(S["hh_act"], KD + j + 1)
                            v.scalar_tensor_tensor(out=h_l[:, j, :], in0=xT[:, j, :], scalar=vec[:, KD + j:KD + j + 1],
                                                   in1=h_h[:, j, :].bitcast(F32), op0=ALU.mult, op1=ALU.subtract)\
                                .then_inc(S["hl_dve"], 1)
                elif kind == "up":
                    j, part = a
                    jj = j + JF * part
                    m = up_index[a]
                    u, ac = ups[:, m % 2, :], acc[:, part, j % 2, :]
                    dve.wait_ge(S["dense_done"], n + 1)
                    if m == 0:
                        dve.wait_ge(S["rstd_ready"], 1)
                        dve.wait_ge(S["conv_kept"], 5)
                    else:
                        dve.wait_ge(S["hist_ready"], m)
                    v.tensor_tensor(two(u[:, 2:T + 2]), dbuf(n), two(rstd[1]), ALU.mult)\
                        .then_inc(S["dve_drained"], 1)
                    dve.wait_ge(S["acc_ready"], m + 1)
                    link(v.scalar_tensor_tensor(out=ac, in0=u[:, 1:T + 1], scalar=fcw[:, 1, jj:jj + 1], in1=ac,
                                                op0=ALU.mult, op1=ALU.add))
                    v.scalar_tensor_tensor(out=ac, in0=u[:, 0:T], scalar=fcw[:, 0, jj:jj + 1], in1=ac,
                                           op0=ALU.mult, op1=ALU.add).then_inc(S["conv_done"], 1)
                    if part == 1:
                        dve.wait_ge(S["th_ready"], j + 1)
                        v.scalar_tensor_tensor(out=acc[:, 0, j % 2, :], in0=tmp_of(("up", j)), scalar=1.0,
                                               in1=acc[:, 0, j % 2, :], op0=ALU.add, op1=ALU.mult)\
                            .then_inc(S["silu_done"], 1)
                        dve.wait_ge(S["silu_done"], j + 1)
                        dve.wait_ge(S["conv_done"], m + 1)
                        v.tensor_tensor(acc[:, 0, j % 2, :], acc[:, 0, j % 2, :], ac, ALU.mult)\
                            .then_inc(S["g_ready"], 1)
                elif kind == "state":
                    dve.wait_ge(S["dense_done"], n + 1)
                    v.tensor_copy(fst[0:2 * JU], B[0:2 * JU, 0, 0:2 * P].rearrange("p (g f) -> p g f", g=2))\
                        .then_inc(S["cst_ready"], 1)
                    v.tensor_copy(cst[:], B[0:16, 1, 0:P]).then_inc(S["cst_ready"], 1)
                    v.memset(kap[:], 0.0).then_inc(S["dve_drained"], 1)

        @block.tensor
        def _(pe):
            t = nc.tensor

            def product(n, x_h, x_l, wait_k=None):
                gs, kx = range(first_group[n], first_group.get(n + 1, len(GROUPS))), 0
                kall = sum(GROUPS[g][2] for g in gs)
                for g in gs:
                    pe.wait_ge(S["wh_ready"], g + 1)
                    pe.wait_ge(S["wl_ready"], g + 1)
                    wh, wl = split_view(w_h, g), split_view(w_l, g)
                    for k in range(GROUPS[g][2]):
                        if wait_k:
                            wait_k(kx)
                        for i, (w, x) in enumerate(((wh, x_h), (wh, x_l), (wl, x_h))):
                            for half in range(2):
                                last = t.matmul(banks(n)[0:w.shape[2], half, 0:HALF], w[:, k, :],
                                                x[:, kx, HALF * half:HALF * half + HALF],
                                                start=kx == 0 and i == 0, stop=kx == kall - 1 and i == 2)
                        kx += 1
                    last.then_inc(S["dense_done" if g == gs[-1] else "part_used"], 1)

            def wait_h(r):
                def wait(k):
                    if r == 0:
                        pe.wait_ge(S[("hl_dve", "hl_pool")[k % 2]], k // 2 + 1)
                    else:
                        if KD - 3 <= k < KD - 1:
                            mean_square(1, k - (KD - 3), X[:, k - (KD - 3), 0:5])
                        pe.wait_ge(S["hl_dve"], KD // 2 + k + 1)
                return wait

            def mean_square(r, part, out):
                pe.wait_ge(S[("sq_added", "sq_done")[part]], (KD - 1 + part) * r)
                src = tmp_of(("sq", r, KD - 1)) if part else ssum[r][:]
                for c, (col, L) in enumerate(TILES):
                    last = t.matmul(out[0:L, c:c + 1], src[:, col:col + L], mean_w[:, 0:1], start=True, stop=True)
                last.then_inc(S["norm_mm"], 1)

            def spread_rstd(out, before):
                for c, (_, L) in enumerate(TILES):
                    pe.wait_ge(S["diag_ready"], before + c + 1)
                    last = t.matmul(out[:, c // 4, P * (c % 4):P * (c % 4) + L], mean_w[0:L, :],
                                    diag[0:L, c, 0:L], start=True, stop=True)
                return last

            for kind, a, n in ORDER:
                if n is not None and used_before[n] is not None:
                    wait_drained(pe, used_before[n])
                B = None if n is None else banks(n)
                if kind == "small":
                    pe.wait_ge(S["small_in"], 9 * 16)
                    t.transpose(B[:, 0, 0:41], small_a[0:41, :], ident[0:41, 0:41])
                    t.transpose(B[:, 0, 41:41 + 2 * JU], small_b[0:2 * JU, :], ident[0:2 * JU, 0:2 * JU])
                    t.transpose(B[:, 1, 0:66], small_c[0:66, 0, :], ident[0:66, 0:66])
                    t.transpose(B[:, 1, 66:132], small_c[0:66, 1, :], ident[0:66, 0:66])\
                        .then_inc(S["dense_done"], 1)
                elif kind == "xT":
                    c, L = a[0], TILES[a[0]][1]
                    if c == 0:
                        pe.wait_ge(S["const_ready"], 8)
                    pe.wait_ge(x_in[c] if c < 4 else S["xs_in"], 16)
                    src = x_t[:, c, :] if c < 4 else x_s[0:TS, :]
                    for j in range(KD):
                        last = t.transpose(B[:, j // 4, P * (j % 4):P * (j % 4) + L], src[:, P * j:P * j + P],
                                           ident[0:L, 0:L])
                    last.then_inc(S["dense_done"], 1)
                elif kind == "rstd":
                    spread_rstd(B, 0).then_inc(S["dense_done"], 1)
                elif kind == "norm":
                    if a[0] == 2:
                        B = banks(block_of[("dn", KD - 2)])
                        wait_drained(pe, block_of[("dn", KD - 2)])
                        for part in range(2):
                            mean_square(2, part, B[:, part, 0:5])
                elif kind == "if":
                    product(n, h_h, h_l, wait_h(0))
                elif kind in W_IN_AT or kind == "gt":
                    product(n, h_h, h_l)
                elif kind == "pr":
                    br, j = a
                    if j == 0:
                        if br < 2:
                            pe.wait_ge(S["y_split"], 4 * (br + 1))
                        else:
                            pe.wait_ge(S["yc_split"], 17)
                            pe.wait_ge(S["yc_spare"], 1)
                    product(n, (ya_h, yb_h, yc_h)[br], (ya_l, yb_l, yc_l)[br])
                elif kind == "wo":
                    product(n, mg_h, mg_l, (lambda k: pe.wait_ge(S["merged_split"], k + 1)) if a[0] == 0 else None)
                elif kind == "up":
                    product(n, h_h, h_l, wait_h(1) if a == (0, 0) else None)
                    if a == (0, 0):
                        spread_rstd(X[:, 2:4, :], 5).then_inc(S["rstd_mm"], 1)
                elif kind == "dn":
                    product(n, g_h, g_l, (lambda k: pe.wait_ge(S["gl_ready"], k + 1)) if a[0] == 0 else None)
                elif kind == "tok":
                    name, j = a[0]
                    src = src_tok(name, j)
                    wait_drained(pe, block_of[(name, j)])
                    for c in range(4):
                        t.transpose(B[:, 0, P * c:P * c + P], src[:, P * c:P * c + P], ident[:])
                    t.transpose(B[0:TS, 1, 0:P], src[:, S0:T], ident[:]).then_inc(S["dense_done"], 1)
                elif kind == "gtr":
                    pe.wait_ge(S["rows_act"], 2)
                    for s, nm in enumerate(("g", "em")):
                        for c, (col, L) in enumerate(TILES):
                            last = t.transpose(B[0:L, s, H * c:H * c + H], row[nm][:, col:col + L], ident[0:H, 0:H])
                    last.then_inc(S["dense_done"], 1)
                elif kind == "ml":
                    stage, u = a
                    c = ML_ORDER[u]
                    col, L = TILES[c]
                    C = C_p if c < 4 else C_s
                    hs = range(H)
                    if stage == 0:
                        if u == 0:
                            wait_drained(pe, block_of[("mq", 3)])
                            wait_drained(pe, last_user[2])
                            wait_drained(pe, last_user[3])
                        else:
                            pe.wait_ge(S["ml_c"], u)
                        pe.wait_ge(S["bd_ready"], u + 1)
                        lw, inter = (X[:, i, :].rearrange("p (h t) -> p h t", h=H)[:, :, 0:L] for i in (0, 2))
                        t.matmul(lw[0:L], ident_r[0:L, 0:L], causal[0:L, 0:L].unsqueeze(1).to_broadcast([L, H, L]),
                                 start=True, stop=False, skip_group_check=True)
                        t.matmul(lw[0:L], mean_r[0:36, 0:L], bd_u[:, :, 0:L], start=False, stop=True,
                                 skip_group_check=True)
                        for h in hs:
                            t.matmul(X[0:L, 1, P * h:P * h + L], mkT[:, h, col:col + L], mqT[:, h, col:col + L],
                                     start=True, stop=True)
                        t.matmul(inter, mean_r[0:36, :], bd_i[:, :, 0:L], start=True, stop=True)\
                            .then_inc(S["ml_scores"], 1)
                    elif stage == 1:
                        if u >= 1:
                            pe.wait_ge(S["ml_hm"], u)
                        pe.wait_ge(S["ml_pt"], u + 1)
                        pe.wait_ge(S["ml_qi"], u + 1)
                        pe.wait_ge(S["ml_kw"], u + 1)
                        if u == 0:
                            wait_drained(pe, block_of[("tok", ("mv", 3))])
                            pe.wait_ge(S["const_ready"], 9)
                        for h in hs:
                            o = X[0:L, h // 2, 129 * (h % 2):129 * (h % 2) + 129]
                            t.matmul(o, qi[:, h, 0:L], C[:, h, :], start=True, stop=False)
                            t.matmul(o, p_ml[0:L, h, 0:L], mv_tok[0:L, c, h, :], start=False, stop=True)
                        for h in hs:
                            last = t.matmul(X[:, 2 + h // 2, 129 * (h % 2):129 * (h % 2) + 129], kw[0:L, h, :],
                                            mv_tok[0:L, c, h, :], start=True, stop=True)
                        last.then_inc(S["ml_num"], 1)
                    else:
                        pe.wait_ge(S["ml_c"], u + 1)
                        pe.wait_ge(S["ml_hn"], u + 1)
                        for h in hs:
                            last = t.transpose(X[:, 3, P * h:P * h + L], hn[0:L, h, :], ident[0:L, 0:L])
                        last.then_inc(S["ml_ht"], 1)
                elif kind == "ck":
                    if a[0] == 0:
                        pe.wait_ge(S["ck_in"], 16)
                        pe.wait_ge(S["ml_hm"], 5)
                        pe.wait_ge(S["ml_c"], 5)
                    else:
                        pe.wait_ge(S["ck_dve"], 1)
                        pe.wait_ge(S["ck_act"], 1)
                    for hh in range(2):
                        for kb in range(8):
                            h = 2 * a[0] + hh
                            last = t.transpose(X[:, 2 * hh + kb // 4, P * (kb % 4):P * (kb % 4) + P],
                                               ck[:, kb, P * h:P * h + P], ident[:])
                    last.then_inc(S["ck_tr"], 1)
                elif kind == "sample":
                    c = a[0]
                    if c == 0:
                        pe.wait_ge(S["ck_dve"], 2)
                        pe.wait_ge(S["ck_act"], 2)
                        wait_drained(pe, block_of[("dq", 3)])
                    else:
                        pe.wait_ge(S["at_exp"], 1)
                    d = slice(64 * c, 64 * c + 64)
                    for kb in range(3):
                        for h in range(H):
                            n_keys = 512 if kb < 2 else TS
                            keys = ckT[d, h, 512 * kb:512 * kb + 512] if kb < 2 else dkT[d, h, S0:T]
                            last = t.matmul(X[TS * h:TS * h + TS, kb, 0:n_keys], dqT[d, h, S0:T], keys,
                                            start=True, stop=True)
                    last.then_inc(S["at_s"], 1)
                elif kind == "at":
                    stage, u = a
                    h, i = (u - 1) // 4, (u - 1) % 4
                    nk = P * (i + 1)
                    if stage == 0:
                        pe.wait_ge(S["at_exp"], u + 1)
                        if u == 1:
                            pe.wait_ge(S["at_wt"], 1)
                        for c in range(2):
                            d = slice(64 * c, 64 * c + 64)
                            t.matmul(X[:, c, 0:nk], dqT[d, h, P * i:P * i + P], dkT[d, h, 0:nk],
                                     start=True, stop=False, skip_group_check=True)
                        for c in range(2):
                            last = t.matmul(X[:, c, nk - 64:nk], causal[64:65, :], mean_r[64:65, 0:64], start=False,
                                            stop=True, skip_group_check=True)
                        last.then_inc(S["at_s"], 1)
                    elif stage == 1:
                        pe.wait_ge(S["at_wd"], u + 1)
                        if u == 0:
                            for kb in range(8):
                                t.transpose(X[:, kb // 4, P * (kb % 4):P * (kb % 4) + P], prob[:, 0, P * kb:P * kb + P],
                                            ident[:])
                            last = t.transpose(X[0:TS, 2, 0:P], prob[:, 0, PAST:PAST + TS], ident[:])
                        else:
                            pe.wait_ge(S["at_wt"], u)
                            pe.wait_ge(S["at_yc"], max(u - 1, 1))
                            for kb in range(i + 1):
                                last = t.transpose(X[:, 2, P * kb:P * kb + P], prob2[:, u % 2, 0, P * kb:P * kb + P],
                                                   ident[:])
                        last.then_inc(S["at_tr"], 1)
                    elif stage == 2:
                        pe.wait_ge(S["at_wt"], u + 1)
                        if u == 0:
                            pe.wait_ge(S["cv_in"], 16)
                            wait_drained(pe, block_of[("tok", ("dv", 3))])
                            for kb in range(9):
                                for hh in range(H):
                                    o, r = X[TS * hh:TS * hh + TS, 3, 0:P], slice(0, P if kb < 8 else TS)
                                    values = cv[:, kb, P * hh:P * hh + P] if kb < 8 else dv_tok[0:TS, 4, hh, :]
                                    last = t.matmul(o, wdT[r, kb, TS * hh:TS * hh + TS], values,
                                                    start=kb == 0, stop=kb == 8)
                        else:
                            pe.wait_ge(S["at_on"], u)
                            for kb in range(i + 1):
                                last = t.matmul(X[:, 3, 0:P], wdT[:, 4 * (u % 2) + kb, :], dv_tok[:, kb, h, :],
                                                start=kb == 0, stop=kb == i)
                        last.then_inc(S["at_o"], 1)
                    else:
                        pe.wait_ge(S["at_on"], u + 1)
                        pe.wait_ge(S["at_wt"], min(u + 2, 17) if u else 1)
                        t.transpose(X[:, 2, 0:P], on[:, u % 2, :], ident[:]).then_inc(S["at_ot"], 1)
                elif kind == "state":
                    pe.wait_ge(S["hist_ready"], JU)
                    for s in range(2):
                        t.transpose(B[0:2 * JU, 0, P * s:P * s + P], ffn_last[:, s].rearrange("p r j -> p (r j)"),
                                    ident[:])
                    t.transpose(B[0:16, 1, 0:P], conv_last[:].rearrange("p s r j -> p (s r j)"), ident[:])\
                        .then_inc(S["dense_done"], 1)
                elif kind == "yT":
                    j, x = a[0], 2 * (a[0] % 2)
                    wait_drained(pe, block_of[("dn", j)])
                    if j >= 2:
                        pe.wait_ge(S["y_copied"], j - 1)
                    for c in range(4):
                        t.transpose(X[:, x, P * c:P * c + P], xT[:, j, P * c:P * c + P], ident[:])
                    t.transpose(X[0:TS, x + 1, 0:P], xT[:, j, S0:T], ident[:]).then_inc(S["y_tr"], 1)


_INS = ["x_prompt", "x_sample", "cache_k", "cache_v", "state_C", "state_n", "state_m", "state_conv", "state_ffn",
        "norm1", "w_in", "b_if", "ml_norm", "w_sc_conv", "da_lambda", "da_norm", "w_branch", "w_out", "norm2",
        "w_up", "w_fconv", "w_down", "norm_f"]
_OUTS = [(1, TP, DM), (1, TS, DM),
         (1, 1, TP, 4, 128), (1, 1, TP, 4, 128), (1, 1, 4, 128, 128), (1, 1, 4, 128), (1, 1, 4), (1, 1, 2, 512),
         (1, 1, 2, 2 * DFF),
         (1, 1, TS, 4, 128), (1, 1, TS, 4, 128), (1, 1, 4, 128, 128), (1, 1, 4, 128), (1, 1, 4), (1, 1, 2, 512),
         (1, 1, 2, 2 * DFF)]


def kernel(**inputs):
    import numpy as _np
    import concourse.bacc as _bacc
    from concourse.bass_utils import run_bass_kernel_spmd as _run

    nc = _bacc.Bacc("TRN2", target_bir_lowering=False, num_devices=1)
    arrays, args = {}, []
    for name in _INS:
        a = _np.ascontiguousarray(inputs[name])
        arrays[f"in_{name}"] = a
        args.append(nc.dram_tensor(f"in_{name}", a.shape, mybir.dt.from_np(a.dtype), kind="ExternalInput").ap())
    for i, shape in enumerate(_OUTS):
        args.append(nc.dram_tensor(f"out_{i}", shape, F32, kind="ExternalOutput").ap())
    streaming_encoder_step(nc, *args)
    r = _run(nc, [arrays], core_ids=[0])
    return tuple(r.results[0][f"out_{i}"] for i in range(len(_OUTS)))
```
